# Optimizing a Trainium2 kernel written in Bass

```python
import jax, jax.numpy as jnp
from jax import lax
import numpy as np

D_MODEL = 1024
BATCH = 1
SEQ = 1024
DEPTH = 1

PLE_DIM = 256
EPS = 1e-6
RG_WIDTH = 512
RG_BLOCKS = 8
RG_BLOCK_DIM = RG_WIDTH // RG_BLOCKS
RG_CONV = 4
RG_C = 8.0
FOX_HEADS = 8
FOX_HEAD_DIM = 64
FOX_WIDTH = FOX_HEADS * FOX_HEAD_DIM
FOX_QBLOCK = 128
FOX_F_BIAS = 3.0
ML_HEADS = 4
ML_HEAD_DIM = 128
ML_WIDTH = ML_HEADS * ML_HEAD_DIM
ML_CHUNK = 128
ML_F_BIAS = 3.0

MIX_WIDTH = RG_WIDTH + FOX_WIDTH + ML_WIDTH
IN_SIZES = (RG_WIDTH, RG_WIDTH,
            FOX_WIDTH, FOX_WIDTH, FOX_WIDTH, FOX_HEADS, FOX_WIDTH,
            ML_WIDTH, ML_WIDTH, ML_WIDTH, ML_HEADS, ML_HEADS, ML_WIDTH, ML_WIDTH)
IN_WIDTH = sum(IN_SIZES)

kernel_name = "hybrid_rglru_fox_mlstm_parallel_heads"

def rmsnorm(x, g):
    x32 = x.astype(jnp.float32)
    y = x32 * lax.rsqrt(jnp.mean(x32 * x32, axis=-1, keepdims=True) + EPS)
    return (y * g.astype(jnp.float32)).astype(x.dtype)

def rglru(xr, conv_w, conv_b, wa, ba, wx, bx, lam):
    B, S, _ = xr.shape
    xc = lax.conv_general_dilated(xr, conv_w[:, None, :], window_strides=(1,), padding=[(RG_CONV - 1, 0)],
                                  dimension_numbers=("NWC", "WIO", "NWC"), feature_group_count=RG_WIDTH) + conv_b
    xb = xc.reshape(B, S, RG_BLOCKS, RG_BLOCK_DIM)
    r = jax.nn.sigmoid(jnp.einsum('bsnc,ncd->bsnd', xb, wa).reshape(B, S, RG_WIDTH) + ba)
    i = jax.nn.sigmoid(jnp.einsum('bsnc,ncd->bsnd', xb, wx).reshape(B, S, RG_WIDTH) + bx)
    log_a = -RG_C * r.astype(jnp.float32) * jax.nn.softplus(-lam.astype(jnp.float32))
    a = jnp.exp(log_a)
    b = jnp.sqrt(-jnp.expm1(2.0 * log_a)) * (i * xc).astype(jnp.float32)

    def combine(left, right):
        a1, b1 = left
        a2, b2 = right
        return a1 * a2, a2 * b1 + b2

    _, h = lax.associative_scan(combine, (a, b), axis=1)
    return h.astype(xr.dtype)

def forgetting_attention(q, k, v, f_logit, b_f, q_g, k_g):
    B, S, _ = q.shape
    def heads(t):
        return t.reshape(B, S, FOX_HEADS, FOX_HEAD_DIM)
    qh = rmsnorm(heads(q), q_g).astype(jnp.float32).transpose(0, 2, 1, 3)
    kh = rmsnorm(heads(k), k_g).astype(jnp.float32).transpose(0, 2, 1, 3)
    vh = heads(v).astype(jnp.float32).transpose(0, 2, 1, 3)
    log_f = jax.nn.log_sigmoid(f_logit.astype(jnp.float32) + b_f.astype(jnp.float32))
    c = jnp.cumsum(log_f, axis=1).transpose(0, 2, 1)
    scale = FOX_HEAD_DIM ** -0.5
    kpos = jnp.arange(S)

    def block(j):
        start = j * FOX_QBLOCK
        qb = lax.dynamic_slice_in_dim(qh, start, FOX_QBLOCK, axis=2)
        cq = lax.dynamic_slice_in_dim(c, start, FOX_QBLOCK, axis=2)
        s = jnp.einsum('bhqd,bhkd->bhqk', qb, kh) * scale + cq[..., :, None] - c[..., None, :]
        qpos = start + jnp.arange(FOX_QBLOCK)
        mask = kpos[None, :] <= qpos[:, None]
        s = jnp.where(mask, s, -jnp.inf)
        w = jax.nn.softmax(s, axis=-1)
        return jnp.einsum('bhqk,bhkd->bhqd', w, vh)

    outs = lax.map(block, jnp.arange(S // FOX_QBLOCK))
    return outs.transpose(1, 0, 3, 2, 4).reshape(B, S, FOX_WIDTH).astype(q.dtype)

def mlstm(q, k, v, i_logit, f_logit, o_logit, b_i, b_f):
    B, S, _ = q.shape
    NC = S // ML_CHUNK
    def heads(t):
        return t.reshape(B, NC, ML_CHUNK, ML_HEADS, ML_HEAD_DIM).transpose(1, 0, 3, 2, 4).astype(jnp.float32)
    def gates(g, bias):
        g = g.astype(jnp.float32) + bias.astype(jnp.float32)
        return g.reshape(B, NC, ML_CHUNK, ML_HEADS).transpose(1, 0, 3, 2)
    qc = heads(q)
    kc = heads(k) * (ML_HEAD_DIM ** -0.5)
    vc = heads(v)
    ig = gates(i_logit, b_i)
    lf = jax.nn.log_sigmoid(gates(f_logit, b_f))
    causal = jnp.tril(jnp.ones((ML_CHUNK, ML_CHUNK), dtype=bool))

    def step(carry, inp):
        C, n, m = carry
        qt, kt, vt, it, ft = inp
        bcum = jnp.cumsum(ft, axis=-1)
        D = jnp.where(causal, bcum[..., :, None] - bcum[..., None, :] + it[..., None, :], -jnp.inf)
        inter = bcum + m[..., None]
        m_t = jnp.maximum(inter, jnp.max(D, axis=-1))
        sc = jnp.einsum('bhtd,bhsd->bhts', qt, kt) * jnp.exp(D - m_t[..., None])
        w_inter = jnp.exp(inter - m_t)
        num = w_inter[..., None] * jnp.einsum('bhtd,bhde->bhte', qt, C) + jnp.einsum('bhts,bhse->bhte', sc, vt)
        den = w_inter * jnp.einsum('bhtd,bhd->bht', qt, n) + jnp.sum(sc, axis=-1)
        h = num / jnp.maximum(jnp.abs(den), jnp.exp(-m_t))[..., None]
        b_last = bcum[..., -1]
        g = b_last[..., None] - bcum + it
        m_new = jnp.maximum(b_last + m, jnp.max(g, axis=-1))
        wk = jnp.exp(g - m_new[..., None])
        decay = jnp.exp(b_last + m - m_new)
        C_new = decay[..., None, None] * C + jnp.einsum('bhs,bhsd,bhse->bhde', wk, kt, vt)
        n_new = decay[..., None] * n + jnp.einsum('bhs,bhsd->bhd', wk, kt)
        return (C_new, n_new, m_new), h

    init = (jnp.zeros((B, ML_HEADS, ML_HEAD_DIM, ML_HEAD_DIM), jnp.float32),
            jnp.zeros((B, ML_HEADS, ML_HEAD_DIM), jnp.float32),
            jnp.zeros((B, ML_HEADS), jnp.float32))
    _, hs = lax.scan(step, init, (qc, kc, vc, ig, lf))
    h = hs.transpose(1, 0, 3, 2, 4).reshape(B, S, ML_WIDTH)
    return (jax.nn.sigmoid(o_logit.astype(jnp.float32)) * h).astype(q.dtype)

def setup_inputs(seed: int = 0) -> dict:
    key = jax.random.key(seed)
    ks = jax.random.split(key, 20)
    def nrm(k, shape, scale):
        return scale * jax.random.normal(k, shape, jnp.float32)
    u = jax.random.uniform(ks[10], (DEPTH, RG_WIDTH), jnp.float32, minval=0.9, maxval=0.999)
    a0 = u ** (1.0 / RG_C)
    rg_lambda = jnp.log(a0) - jnp.log1p(-a0)
    return {
        "x": nrm(ks[0], (BATCH, SEQ, D_MODEL), 1.0),
        "p": nrm(ks[1], (DEPTH, BATCH, SEQ, PLE_DIM), 1.0),
        "norm_g": 1.0 + nrm(ks[2], (DEPTH, D_MODEL), 0.02),
        "w_in": nrm(ks[3], (DEPTH, D_MODEL, IN_WIDTH), D_MODEL ** -0.5),
        "rg_conv_w": nrm(ks[4], (DEPTH, RG_CONV, RG_WIDTH), RG_CONV ** -0.5),
        "rg_conv_b": nrm(ks[5], (DEPTH, RG_WIDTH), 0.01),
        "rg_wa": nrm(ks[6], (DEPTH, RG_BLOCKS, RG_BLOCK_DIM, RG_BLOCK_DIM), RG_BLOCK_DIM ** -0.5),
        "rg_ba": nrm(ks[7], (DEPTH, RG_WIDTH), 0.01),
        "rg_wx": nrm(ks[8], (DEPTH, RG_BLOCKS, RG_BLOCK_DIM, RG_BLOCK_DIM), RG_BLOCK_DIM ** -0.5),
        "rg_bx": nrm(ks[9], (DEPTH, RG_WIDTH), 0.01),
        "rg_lambda": rg_lambda,
        "fox_b_f": FOX_F_BIAS + nrm(ks[11], (DEPTH, FOX_HEADS), 0.5),
        "fox_q_g": 1.0 + nrm(ks[12], (DEPTH, FOX_HEAD_DIM), 0.02),
        "fox_k_g": 1.0 + nrm(ks[13], (DEPTH, FOX_HEAD_DIM), 0.02),
        "ml_b_i": nrm(ks[14], (DEPTH, ML_HEADS), 0.5),
        "ml_b_f": ML_F_BIAS + nrm(ks[15], (DEPTH, ML_HEADS), 0.5),
        "w_out": nrm(ks[16], (DEPTH, MIX_WIDTH, D_MODEL), (MIX_WIDTH ** -0.5) * ((2 * DEPTH) ** -0.5)),
        "ple_norm_g": 1.0 + nrm(ks[17], (DEPTH, D_MODEL), 0.02),
        "w_ple_gate": nrm(ks[18], (DEPTH, D_MODEL, D_MODEL), D_MODEL ** -0.5),
        "w_ple": nrm(ks[19], (DEPTH, PLE_DIM, D_MODEL), 0.5 * PLE_DIM ** -0.5),
    }

def reference(x, p, norm_g, w_in, rg_conv_w, rg_conv_b, rg_wa, rg_ba, rg_wx, rg_bx, rg_lambda,
              fox_b_f, fox_q_g, fox_k_g, ml_b_i, ml_b_f, w_out, ple_norm_g, w_ple_gate, w_ple):
    splits = np.cumsum(IN_SIZES)[:-1].tolist()
    h = x
    for l in range(DEPTH):
        u = rmsnorm(h, norm_g[l])
        z = jnp.einsum('bsd,de->bse', u, w_in[l])
        (rg_x, rg_gate, fq, fk, fv, ff, f_gate,
         mq, mk, mv, mi, mf, mo, m_gate) = jnp.split(z, splits, axis=-1)
        y_rg = rglru(rg_x, rg_conv_w[l], rg_conv_b[l], rg_wa[l], rg_ba[l], rg_wx[l], rg_bx[l],
                     rg_lambda[l]) * jax.nn.silu(rg_gate)
        y_fox = forgetting_attention(fq, fk, fv, ff, fox_b_f[l], fox_q_g[l], fox_k_g[l]) * jax.nn.silu(f_gate)
        y_ml = mlstm(mq, mk, mv, mi, mf, mo, ml_b_i[l], ml_b_f[l]) * jax.nn.silu(m_gate)
        y = jnp.concatenate([y_rg, y_fox, y_ml], axis=-1)
        h = h + jnp.einsum('bse,ed->bsd', y, w_out[l])
        gate = jax.nn.sigmoid(jnp.einsum('bsd,de->bse', rmsnorm(h, ple_norm_g[l]), w_ple_gate[l]))
        h = h + gate * jnp.einsum('bsp,pd->bsd', p[l], w_ple[l])
    return h


_drawn_inputs = setup_inputs


def setup_inputs(seed=0):
    import zlib

    import numpy as np

    out = dict(_drawn_inputs(seed))
    spreads = {}
    factors = {'rg_conv_b': 4.632,
     'rg_ba': 64.0,
     'rg_bx': 64.0,
     'fox_b_f': 25.064,
     'fox_q_g': 8.0,
     'fox_k_g': 8.0,
     'ml_b_f': 21.477,
     'ple_norm_g': 64.0}
    for name, (base, spread) in spreads.items():
        noise = np.random.default_rng([zlib.crc32(name.encode()), seed]).standard_normal(out[name].shape)
        drawn = base * np.exp(spread * noise) if base else spread * noise
        out[name] = __import__('jax').numpy.asarray(drawn.astype(out[name].dtype))
    for name, factor in factors.items():
        out[name] = (out[name] * factor).astype(out[name].dtype)
    return out
```

```python
from contextlib import ExitStack

import concourse.bass as bass
from concourse import mybir

ALU = mybir.AluOpType
ACT = mybir.ActivationFunctionType
AX_X = mybir.AxisListType.X
F32 = mybir.dt.float32
FR = mybir.dt.float32r

P = 128
S = 1024
D = 1024
KD = D // P
HALF = 512
SB = S // P
PLE = 256
KP = PLE // P
EPS = 1e-6
KB = 1024

RG_W, FOX_W, ML_W = 512, 512, 512
FOX_H, FOX_D = 8, 64
ML_H = 4
CH = 128
NC = S // CH
CV = 130
RG_C = 8.0
NEG = -3.0e38

C_RX, C_RG = 0, 512
C_FQ, C_FK, C_FV, C_FF, C_FG = 1024, 1536, 2048, 2560, 2568
C_MQ, C_MK, C_MV, C_MI, C_MF, C_MO, C_MG = 3080, 3592, 4104, 4616, 4620, 4624, 5136

UNIT = {
    None: [],
    "F": [(C_FQ, 0), (C_FK, 1), (C_FV, 0), (C_FG, 1)],
    "M": [(C_MQ, 0), (C_MK, 1), (C_MV, 2), (C_MO, 0), (C_MG, 1)],
    "R": [(C_RX, 0), (C_RG, 1)],
}
TURNS = 4
FIRST = {None: 0, "F": 1, "M": 1 + 4 * 4, "R": 1 + 4 * 4 + 4 * 5}
BEFORE = {"F": 0, "M": 4, "R": 8}
YROW = {"R": 0, "F": 4, "M": 8}

EORD = [4, 5, 6, 7, 8, 9, 10, 11, 0, 1, 2, 3]


def spread(total, slots):
    return [total * (n + 1) // slots for n in range(slots)]


PARAMS = 14
FA, FD = 13, 8
MA, MD = 16, 21
RA, RD = 9, 11


def ngroups(t):
    return sum(i % SB // 4 + 1 for i in range(t))


def uses(kind, turn, b):
    slot = UNIT[kind][b][1]
    n = 0
    for k in "FMR":
        mine = sum(1 for _, s in UNIT[k] if s == slot)
        if k == kind:
            return n + mine * turn + sum(1 for _, s in UNIT[k][:b + 1] if s == slot)
        n += mine * TURNS


def hybrid(nc, x, p, norm_g, w_in, conv_w, conv_b, wa, ba, wx, bx, lam, fox_b_f, q_g, k_g, ml_b_i, ml_b_f,
           w_out, ple_g, w_gate, w_ple, out):
    ctx = ExitStack()
    with ctx:
        BASE = 16512
        top = nc.sbuf_usable_end
        arena = ctx.enter_context(nc.sbuf_tensor("arena", [P, (top - BASE - 96) // 4], F32))

        def at(name, shape, dt, off):
            size = 4
            for n in shape[1:]:
                size *= n
            assert BASE + off + size <= top, (name, off, size)
            return nc.alloc_sbuf_tensor_at(name, shape, dt, offset=BASE + off)

        def sem(name):
            return ctx.enter_context(nc.semaphore(name))

        uh = at("uh", [P, KD, S], FR, 0)
        ul = at("ul", [P, KD, S], FR, 32 * KB)
        W0 = 64 * KB
        wraw = [at(f"wraw{i}", [P, KD, P], F32, W0 + 4 * KB * i) for i in range(3)]
        wh = [at(f"wh{i}", [P, KD, P], FR, W0 + 4 * KB * (3 + i)) for i in range(3)]
        wl = [at(f"wl{i}", [P, KD, P], FR, W0 + 4 * KB * (6 + i)) for i in range(3)]
        Y = 100 * KB
        yt = at("yt", [P, 12, S], F32, Y)
        Y0, Y1, Y2 = Y, Y + 16 * KB, Y + 32 * KB
        C = Y + 48 * KB
        ident = at("ident", [P, P], F32, C)
        identr = at("identr", [P, P], FR, C + 512)
        maskf = at("maskf", [P, P], F32, C + 1024)
        maskr = at("maskr", [P, P], FR, C + 1536)
        headmean = at("headmean", [P, P], F32, C + 2048)
        prm = at("prm", [P, 96], F32, C + 2560)
        gcol = at("gcol", [96, 2], F32, C + 2560 + 384)
        cols = at("cols", [P, NC, 4, 4], F32, C + 3072)
        tri = at("tri", [P, P], F32, C + 3584)
        SC = C + 4096
        zst = [at(f"zst{i}", [P, S], F32, SC + 4 * KB * i) for i in range(5)]
        S1 = SC + 20 * KB

        xt = at("xt", [P, SB, D], F32, Y0)
        junk = at("junk", [P, SB, D], F32, 0)
        wgraw = at("wgraw", [P, KD, 16], F32, S1)
        wgh = at("wgh", [P, KD, 96], FR, S1 + 1 * KB)
        wgl = at("wgl", [P, KD, 96], FR, S1 + 4 * KB)
        xb = at("xb", [P, S], F32, Y1)
        ex = at("ex", [P, S], F32, Y1 + 4 * KB)
        lf = at("lf", [P, S], F32, Y1 + 8 * KB)
        nb = at("nb", [P, S], F32, Y1 + 12 * KB)
        ar = at("ar", [P, S], F32, Y2)
        gr = at("gr", [P, S], F32, Y2 + 4 * KB)
        rw = at("rw", [P, S], F32, Y2 + 8 * KB)
        dl = at("dl", [P, S], F32, Y2 + 12 * KB)
        rm = at("rm", [P, S], F32, S1 + 24 * KB)
        mc = at("mc", [P, NC], F32, S1 + 32 * KB)
        vhl = at("vhl", [P, SB, 2, P], FR, Y0)
        crow = at("crow", [64, S], FR, Y0 + 8 * KB)
        selall = at("selall", [64, FOX_H, P], FR, Y0 + 12 * KB)
        pr = [at(f"pr{i}", [P, S], F32, Y2 + 4 * KB * i) for i in range(2)]
        og = at("og", [P, S], F32, Y2 + 8 * KB)
        ot = at("ot", [P, S], F32, Y2 + 12 * KB)
        qs = [at(f"qs{i}", [P, S], FR, S1 + 4 * KB * i) for i in range(2)]
        ka = [at(f"ka{i}", [P, S], FR, S1 + 4 * KB * (2 + i)) for i in range(2)]
        kb = [at(f"kb{i}", [P, S], FR, S1 + 4 * KB * (4 + i)) for i in range(2)]
        pt = at("pt", [P, SB, 2 * P], FR, S1 + 24 * KB)
        rq = [at(f"rq{i}", [P, S], F32, S1 + (24 + 4 * i) * KB) for i in range(2)]
        SM = S1 + 32 * KB
        selu = at("selu", [64, 2, P], FR, SM + 64)
        oc = at("oc", [P, 2 * P], F32, SM + 64 + 1024)
        sm = at("sm", [P, 16], F32, SM + 64 + 2048)
        qth, qtl, kth, ktl = [at(n, [P, S], FR, S1 + 4 * KB * i) for i, n in enumerate(("qth", "qtl", "kth", "ktl"))]
        vh2 = at("vh2", [P, NC, CV], FR, S1 + 16 * KB)
        vl2 = at("vl2", [P, NC, CV], FR, S1 + 20 * KB + 128)
        eg = at("eg", [P, NC, CH], F32, S1 + 24 * KB + 256)
        hn = at("hn", [P, NC, CV], F32, S1 + 24 * KB + 256)
        kwh = at("kwh", [P, NC, P], FR, S1 + 28 * KB + 512)
        ucol = at("ucol", [P, NC, 4], F32, S1 + 35 * KB)
        dec = at("dec", [P, NC], F32, S1 + 35 * KB + 128)
        den = at("den", [P, NC], F32, S1 + 35 * KB + 192)
        kwl = at("kwl", [P, NC, P], FR, Y0)
        sch = at("sch", [P, S], FR, Y0 + 4 * KB)
        scl = at("scl", [P, S], FR, Y0 + 8 * KB)
        cf = at("cf", [P, CV], F32, Y0 + 12 * KB)
        chi = [at(f"chi{i}", [P, CV], FR, Y0 + 12 * KB + 544 * (1 + i)) for i in range(2)]
        clo = [at(f"clo{i}", [P, CV], FR, Y0 + 12 * KB + 544 * (3 + i)) for i in range(2)]
        ti2 = [at(f"ti{i}", [P, CV], F32, Y0 + 12 * KB + 544 * (5 + i)) for i in range(2)]
        xc, tr, ti, tt, l1, l2, tg = [at(n, [P, S], F32, S1 + 4 * KB * i) for i, n in
                                      enumerate(("xc", "tr", "ti", "tt", "l1", "l2", "tg"))]
        wad = at("wad", [P, 2, P], F32, S1 + 28 * KB)
        rcol = at("rcol", [P, 8], F32, S1 + 35 * KB + 256)
        wo = at("wo", [P, 12, 2, D], FR, 0)
        raw = zst[2:5]
        ysh = [at("ysh0", [P, HALF], FR, 96 * KB), at("ysh1", [P, HALF], FR, S1 + 29 * KB)]
        ysl = [at("ysl0", [P, HALF], FR, 98 * KB), at("ysl1", [P, HALF], FR, S1 + 31 * KB)]
        ht = [at(f"h{i}", [P, D], F32, S1 + 4 * KB * i) for i in range(7)] + [at("h7", [P, D], F32, SC)]
        hq = [at(f"hq{i}", [P, D], F32, Y + 4 * KB * i) for i in range(2)]
        hth = [at(f"hth{i}", [P, KD, P], FR, Y + (8 + 4 * i) * KB) for i in range(2)]
        htl = [at(f"htl{i}", [P, KD, P], FR, Y + (16 + 4 * i) * KB) for i in range(2)]
        th = [at(f"th{i}", [P, D], F32, Y + (24 + 4 * i) * KB) for i in range(2)]
        praw = at("praw", [P, SB, PLE], F32, Y + 32 * KB)
        pth = [at(f"pth{i}", [P, KP, P], FR, Y + (40 + i) * KB) for i in range(2)]
        ptl = [at(f"ptl{i}", [P, KP, P], FR, Y + (42 + i) * KB) for i in range(2)]
        tick = at("tick", [P, 4], F32, C + 2560 + 416)

        ps = [ctx.enter_context(nc.psum_tensor(f"ps{i}", [P, 2 * HALF], F32)) for i in range(4)]
        pz = [ps[0][:, 0:HALF], ps[0][:, HALF:]]
        p_s = [ps[1], ps[2]]
        p_t, p_o = ps[3][:, 0:HALF], ps[3][:, HALF:]

        g_dram = nc.dram_tensor("g_scratch", [ML_H, S], F32).ap()
        wl_dram = nc.dram_tensor("wl_scratch", [ML_H, NC], F32).ap()
        w_cols = w_in.rearrange("l (k p) n -> (l p) k n", p=P)

        s_par, s_gb0, s_gb = sem("params_loaded"), sem("gate_bias_cleared"), sem("gate_bias_loaded")
        s_x = [sem(f"x_loaded{i}") for i in range(2)]
        s_id0, s_id = sem("consts_cleared"), sem("consts_ready")
        s_cc = sem("const_casts_ready")
        s_ssq, s_ln, s_rstd, s_xn = sem("sumsq_ready"), sem("rstd_ln"), sem("rstd_ready"), sem("x_scaled")
        s_xT, s_uh, s_ul = sem("xT_ready"), sem("uh_ready"), sem("ul_ready")
        s_wd = [sem(f"w_loaded{i}") for i in range(3)]
        s_wgd, s_wgz, s_wgh, s_wg = (sem("wg_loaded"), sem("wg_cleared"), sem("wg_hi_ready"), sem("wg_ready"))
        s_wh, s_ws = sem("w_hi_ready"), sem("w_split")
        s_z, s_ze = sem("z_half_done"), sem("z_half_saved")
        s_ga, s_gd, s_gm = sem("gate_act"), sem("gate_dve"), sem("gate_memsets")
        s_hm, s_gv = sem("head_mean_ready"), sem("gate_rows_cleared")
        s_gt, s_gc = sem("gate_cols_transposed"), sem("gate_cols_ready")
        s_gw = sem("gate_rows_saved")
        s_pc, s_lam, s_lam0 = sem("param_steps"), sem("lambda_steps"), sem("lambda_abs")
        s_fa, s_fd = sem("fox_prep_act"), sem("fox_prep_dve")
        s_ms, s_vt = sem("fox_meansq"), sem("fox_v_transposed")
        s_su = sem("fox_selector_ready")
        s_vh, s_vl = sem("fox_v_hi"), sem("fox_v_lo")
        s_og = sem("fox_gate_ready")
        s_sc, s_nm, s_mx, s_ex = sem("scores_ready"), sem("negmax_ready"), sem("max_ready"), sem("probs_ready")
        s_rc, s_pn = sem("recip_ready"), sem("probs_scaled")
        s_pt, s_ph, s_pl = sem("probsT_ready"), sem("probsT_hi"), sem("probsT_lo")
        s_pv, s_oc, s_oa, s_ot = sem("pv_done"), sem("pv_copied"), sem("pv_added"), sem("o_ready")
        s_unit = sem("unit_finished")
        s_ma, s_md, s_mg = sem("ml_act"), sem("ml_dve"), sem("ml_rows_loaded")
        s_mone = sem("ml_ones_ready")
        s_mkt, s_mvt, s_mst = sem("ml_kT"), sem("ml_vT"), sem("ml_scoresT")
        s_mu, s_mx2, s_mi = sem("ml_update"), sem("ml_intra"), sem("ml_inter")
        s_mc, s_mch, s_mcl, s_mt, s_mh = (sem("ml_state"), sem("ml_state_hi"), sem("ml_state_lo"),
                                          sem("ml_inter_scaled"), sem("ml_h"))
        s_mht = sem("ml_hT")
        s_ra, s_rd, s_rg, s_rw = sem("rg_act"), sem("rg_dve"), sem("rg_gates"), sem("rg_weights_loaded")
        s_rz = sem("rg_weights_cleared")
        s_oh, s_ow = sem("wo_hi"), sem("wo_split")
        s_od = [sem(f"wo_loaded{i}") for i in range(3)]
        s_yh, s_yl, s_om = sem("y_hi"), sem("y_lo"), sem("out_row_block_multiplied")
        s_hx, s_h, s_pp = sem("h_x_loaded"), sem("h_ready"), sem("p_loaded")
        s_psc = sem("w_gate_scaled")
        s_q1, s_q2, s_q3, s_q4 = sem("h_sumsq"), sem("h_ln"), sem("h_rstd"), sem("h_scaled")
        s_qt, s_qh, s_ql = sem("hT_ready"), sem("hT_hi"), sem("hT_lo")
        s_gt2, s_th, s_t1, s_fin = sem("gate_ready"), sem("tanh_ready"), sem("gated"), sem("final_ready")
        s_out = sem("out_saved")

        block = ctx.enter_context(nc.Block())

        def blocks(kind, turn):
            n = len(UNIT[kind])
            return [(FIRST[kind] + n * turn + b, slot, c0 + P * turn) for b, (c0, slot) in enumerate(UNIT[kind])]

        @block.sync
        def _(sp):
            for i in range(SB):
                sp.dma_start(xt[:, i, :], x[0, i * P:(i + 1) * P, :]).then_inc(s_x[i // 4], 16)

            def load_blocks(kind, turn):
                for b, (B, slot, col) in enumerate(blocks(kind, turn)):
                    if not (isinstance(B, int) and B < 3):
                        sp.wait_ge(s_ws, B - 2)
                    sp.dma_start(wraw[slot][:, :, :], w_cols[:, :, bass.ds(col, P)]).then_inc(s_wd[slot], 16)

            for kind in "FMR":
                load_blocks(kind, 0)
                with sp.Fori(1, TURNS) as turn:
                    load_blocks(kind, turn)
            for n in range(22):
                if n == 0:
                    sp.wait_ge(s_unit, 9)
                if n >= 3:
                    sp.wait_ge(s_ow, n - 2)
                if n < 12:
                    src = w_out[0, EORD[n] * P:(EORD[n] + 1) * P, :]
                elif n < 20:
                    src = w_gate[0, (n - 12) * P:(n - 11) * P, :]
                else:
                    src = w_ple[0, (n - 20) * P:(n - 19) * P, :]
                sp.dma_start(raw[n % 3][:, :], src).then_inc(s_od[n % 3], 16)
                if n == 9:
                    sp.wait_ge(s_unit, 13)
                    for i in range(SB):
                        sp.dma_start(ht[i][:, :], x[0, i * P:(i + 1) * P, :]).then_inc(s_hx, 16)
            sp.wait_ge(s_yl, 24)
            sp.wait_ge(s_yh, 24)
            sp.dma_start(praw[:, :, :], p[0, 0].rearrange("(i q) c -> q i c", q=P)).then_inc(s_pp, 16)
            for i in range(SB):
                sp.wait_ge(s_fin, i + 1)
                sp.dma_start(out[0, i * P:(i + 1) * P, :], ht[i][:, :]).then_inc(s_out, 16)
            sp.wait_ge(s_out, 16 * SB)

        @block.gpsimd
        def _(g):
            g.memset(gcol[:, :], 0.0).then_inc(s_gb0, 1)
            g.memset(ident[:, :], 0.0).then_inc(s_id0, 1)
            g.memset(maskf[:, :], 0.0).then_inc(s_id0, 1)
            g.memset(tri[:, :], 1.0).then_inc(s_id0, 1)
            g.memset(prm[:, 52:53], EPS)
            g.memset(tick[:, :], 0.0)
            g.memset(prm[:, 53:54], 1.0)
            g.wait_ge(s_id0, 3)
            g.affine_select(out=ident[:, :], in_=ident[:, :], compare_op=ALU.not_equal, fill=1.0, base=0,
                            pattern=[[-1, P]], channel_multiplier=1).then_inc(s_id, 1)
            g.affine_select(out=maskf[:, :], in_=maskf[:, :], compare_op=ALU.is_ge, fill=NEG, base=0,
                            pattern=[[-1, P]], channel_multiplier=1).then_inc(s_id, 1)
            g.affine_select(out=tri[:, :], in_=tri[:, :], compare_op=ALU.is_ge, fill=0.0, base=0,
                            pattern=[[1, P]], channel_multiplier=-1).then_inc(s_id, 1)
            g.memset(wgh[:, :, :].bitcast(F32), 0.0).then_inc(s_wgz, 1)
            g.memset(wgl[:, :, :].bitcast(F32), 0.0).then_inc(s_wgz, 1)
            g.wait_ge(s_wgd, 32)
            g.wait_ge(s_wgz, 2)
            parts = [(0, 0, 8), (32, 8, 4), (64, 12, 4)]
            for to, frm, n in parts:
                last = g.tensor_copy(wgh[:, :, to:to + n], wgraw[:, :, frm:frm + n])
            last.then_inc(s_wgh, 1)
            g.wait_ge(s_wgh, 1)
            for to, frm, n in parts:
                last = g.tensor_tensor(wgl[:, :, to:to + n], wgraw[:, :, frm:frm + n], wgh[:, :, to:to + n],
                                       ALU.subtract)
            last.then_inc(s_wg, 1)
            g.wait_ge(s_xT, 16)
            g.memset(crow[:, :].bitcast(F32), 0.0).then_inc(s_gm, 1)
            g.memset(rw[:, :], 0.0).then_inc(s_gm, 1)
            g.memset(selall[:, :, :].bitcast(F32), 0.0).then_inc(s_gm, 1)
            for n, base in enumerate((0, 32)):
                g.wait_ge(s_gm, 3 + n)
                g.affine_select(out=selall[:, :, :], in_=selall[:, :, :], compare_op=ALU.not_equal, fill=1.0,
                                base=-base, pattern=[[-1, FOX_H], [0, P]], channel_multiplier=1).then_inc(s_gm, 1)

            def split(kind, turn):
                for b, (B, slot, _) in enumerate(blocks(kind, turn)):
                    g.wait_ge(s_wd[slot], 16 * uses(kind, turn, b))
                    if not (isinstance(B, int) and B < 3):
                        g.wait_ge(s_z, 2 * (B - 1))
                    g.tensor_tensor(tick[:, 2:3], tick[:, 0:1], tick[:, 1:2], ALU.add)
                    g.tensor_copy(wh[slot][:, :, :], wraw[slot][:, :, :]).then_inc(s_wh, 1)
                    g.wait_ge(s_wh, B)
                    g.tensor_tensor(wl[slot][:, :, :], wraw[slot][:, :, :], wh[slot][:, :, :],
                                    ALU.subtract).then_inc(s_ws, 1)

            for kind in "FMR":
                split(kind, 0)
                with g.Fori(1, TURNS) as turn:
                    split(kind, turn)
            for n in range(22):
                slot = n if n < 12 else n - 12
                g.wait_ge(s_od[n % 3], 16 * (n // 3 + 1))
                if n == 0:
                    g.wait_ge(s_z, 90)
                if n >= 12:
                    g.wait_ge(s_om, 12 + slot + 1)
                src = raw[n % 3]
                if 12 <= n < 20:
                    g.tensor_scalar(src[:, :], src[:, :], prm[:, 8 + slot:9 + slot], None, ALU.mult).then_inc(s_psc, 1)
                    g.wait_ge(s_psc, slot + 1)
                g.tensor_copy(wo[:, slot, 0, :], src[:, :]).then_inc(s_oh, 1)
                g.wait_ge(s_oh, n + 1)
                g.tensor_tensor(wo[:, slot, 1, :], src[:, :], wo[:, slot, 0, :], ALU.subtract).then_inc(s_ow, 1)

        @block.tensor
        def _(pe):
            mm = nc.tensor.matmul

            def z_steps(kind, turn):
                for b, (B, slot, _) in enumerate(blocks(kind, turn)):
                    for half in range(2):
                        if half == 0:
                            pe.wait_ge(s_ws, B)
                        pe.wait_ge(s_ze, 2 * B + half - 1)
                        for k in range(KD):
                            cs = slice(half * HALF, (half + 1) * HALF)
                            mm(pz[half], wh[slot][:, k, :], uh[:, k, cs], start=(k == 0), stop=False)
                            mm(pz[half], wh[slot][:, k, :], ul[:, k, cs], start=False, stop=False)
                            last = mm(pz[half], wl[slot][:, k, :], uh[:, k, cs], start=False, stop=(k == KD - 1))
                            if k == KD - 1:
                                last.then_inc(s_z, 1)
                            yield

            def run(steps, n):
                for _ in range(n):
                    if next(steps, 0) == 0:
                        break

            pe.wait_ge(s_id, 2)
            for half in range(2):
                for k in range(KD):
                    n = half * KD + k
                    pe.wait_ge(s_xn, 4 * half + 4)
                    if n >= 8:
                        pe.wait_ge(s_ul, n - 7)
                    bank = ps[n % 8 // 2][:, n % 2 * HALF:(n % 2 + 1) * HALF]
                    for i in range(4):
                        last = nc.tensor.transpose(bank[:, i * P:(i + 1) * P],
                                                   xt[:, 4 * half + i, k * P:(k + 1) * P], ident[:, :])
                    last.then_inc(s_xT, 1)
            pe.wait_ge(s_wg, 1)
            pe.wait_ge(s_ul, 16)
            for half in range(2):
                cs = slice(half * HALF, (half + 1) * HALF)
                for k in range(KD):
                    mm(pz[half][0:96], wgh[:, k, :], uh[:, k, cs], start=(k == 0), stop=False)
                    mm(pz[half][0:96], wgh[:, k, :], ul[:, k, cs], start=False, stop=False)
                    last = mm(pz[half][0:96], wgl[:, k, :], uh[:, k, cs], start=False, stop=(k == KD - 1))
                last.then_inc(s_z, 1)

            first = z_steps("F", 0)
            run(first, 32)
            pe.wait_ge(s_ga, 10)
            for half in range(2):
                bank = (p_t, p_o)[half]
                for c in range(4):
                    last = nc.tensor.transpose(bank[:, c * P:(c + 1) * P], rw[:, (4 * half + c) * CH:][:, 0:CH],
                                               ident[:, :])
                last.then_inc(s_gt, 1)
            run(first, 64)

            def fox(a, kind, turn):
                steps = z_steps(kind, turn)
                total = 16 * len(UNIT[kind])
                pe.wait_ge(s_hm, 3)
                for n in range(2):
                    if n == 0:
                        pe.wait_ge(s_unit, a + 1)
                    pe.wait_ge(s_fa, FA * a + 1 + n)
                    for half in range(2):
                        cs = slice(half * HALF, (half + 1) * HALF)
                        last = mm(p_s[n][:, cs], headmean[:, :], pr[n][:, cs], start=True, stop=True)
                    last.then_inc(s_ms, 1)
                    run(steps, 4)
                pe.wait_ge(s_gc, 2)
                pe.wait_ge(s_ze, 2 * (FIRST["F"] + 4 * a + 2) + 2)
                for half in range(2):
                    bank = (p_t, p_o)[half]
                    for i in range(4):
                        last = nc.tensor.transpose(bank[:, i * P:(i + 1) * P],
                                                   zst[2][:, (4 * half + i) * P:][:, 0:P], ident[:, :])
                    last.then_inc(s_vt, 1)
                run(steps, 24)

                def scores(t):
                    h, i = t // SB, t % SB
                    n = (i + 1) * P
                    if t == 0:
                        pe.wait_ge(s_fa, FA * a + 12)
                        pe.wait_ge(s_fd, FD * a + 8)
                        pe.wait_ge(s_su, 2 * a + 2)
                    if t >= 2:
                        pe.wait_ge(s_ex, 16 * a + t - 1)
                    bank = p_s[t % 2]
                    for c0 in range(0, n, HALF):
                        c1 = min(c0 + HALF, n)
                        o = bank[:, c0:c1]
                        diag = c1 == n
                        mm(o, qs[h][:, i * P:(i + 1) * P], ka[h][:, c0:c1], start=True, stop=False)
                        mm(o, qs[h][:, i * P:(i + 1) * P], kb[h][:, c0:c1], start=False, stop=False)
                        if diag:
                            mm(bank[:, n - P:n], identr[:, :], maskr[:, :], start=False, stop=False)
                        last = mm(o, selu[:, h, :], crow[:, c0:c1], start=False, stop=True)
                    last.then_inc(s_sc, 1)

                done = min(32, total)
                upto = spread(total - done, 16)
                scores(0)
                for t in range(16):
                    h, i = t // SB, t % SB
                    if t < 15:
                        scores(t + 1)
                    todo = upto[t] - (upto[t - 1] if t else 0)
                    groups = i // 4 + 1
                    run(steps, todo - groups)
                    pe.wait_ge(s_pn, 16 * a + t + 1)
                    for g in range(groups):
                        n_g = 24 * a + 12 * h + max(0, i - 4) * 2 + min(i, 4) + g
                        if t == 0 and g == 0:
                            pe.wait_ge(s_vl, 2 * a + 2)
                        else:
                            pe.wait_ge(s_pl, n_g)
                        for j in range(4 * g, min(4 * g + 4, i + 1)):
                            last = nc.tensor.transpose(p_t[:, (j % 4) * P:(j % 4 + 1) * P],
                                                       pr[t % 2][:, j * P:(j + 1) * P], ident[:, :])
                        last.then_inc(s_pt, 1)
                        run(steps, 1)
                    n_g += 1
                    pe.wait_ge(s_ph, n_g)
                    pe.wait_ge(s_pl, n_g)
                    if t:
                        pe.wait_ge(s_oa, 16 * a + t)
                    for j in range(i + 1):
                        last = mm(p_o[:, 0:2 * P], vhl[:, j, h, :], pt[:, j, :], start=(j == 0), stop=(j == i))
                    last.then_inc(s_pv, 1)
                run(steps, 100)

            def mlstm(m, kind, turn):
                steps = z_steps(kind, turn)
                total = 16 * len(UNIT[kind])
                done = min(24, total // 2)
                upto = spread(total - done, NC)
                pe.wait_ge(s_unit, 4 + m + 1)
                pe.wait_ge(s_md, MD * m + 1)
                for half in range(2):
                    for i in range(4 * half, 4 * half + 4):
                        last = nc.tensor.transpose(p_s[1][:, i * P:(i + 1) * P], zst[1][:, i * P:(i + 1) * P],
                                                   ident[:, :])
                last.then_inc(s_mkt, 1)
                run(steps, done // 3)
                for half in range(2):
                    bank = (p_t, p_o)[half]
                    for i in range(4):
                        last = nc.tensor.transpose(bank[:, i * P:(i + 1) * P],
                                                   zst[2][:, (4 * half + i) * P:][:, 0:P], ident[:, :])
                    last.then_inc(s_mvt, 1)
                run(steps, done // 3)
                pe.wait_ge(s_ma, MA * m + 2)
                pe.wait_ge(s_md, MD * m + 7)
                for c in range(NC):
                    o = p_s[0][:, c * CH:(c + 1) * CH]
                    cs = slice(c * CH, (c + 1) * CH)
                    mm(o, kth[:, cs], qth[:, cs], start=True, stop=False)
                    mm(o, kth[:, cs], qtl[:, cs], start=False, stop=False)
                    last = mm(o, ktl[:, cs], qth[:, cs], start=False, stop=True)
                    if c % 4 == 3:
                        last.then_inc(s_mst, 1)
                run(steps, done - 2 * (done // 3))
                for c in range(NC):
                    cs = slice(c * CH, (c + 1) * CH)
                    todo = upto[c] - (upto[c - 1] if c else 0)
                    if c == 0:
                        pe.wait_ge(s_md, MD * m + 11)
                        pe.wait_ge(s_ma, MA * m + 13)
                        pe.wait_ge(s_mone, 3)
                    elif c > 1:
                        pe.wait_ge(s_mc, (NC - 1) * m + c - 1)
                    if c < NC - 1:
                        o = p_s[1][:, (c % 2) * HALF:][:, 0:CV]
                        mm(o, kwh[:, c, :], vh2[:, c, :], start=True, stop=False)
                        mm(o, kwh[:, c, :], vl2[:, c, :], start=False, stop=False)
                        mm(o, kwl[:, c, :], vh2[:, c, :], start=False, stop=True).then_inc(s_mu, 1)
                    if c == 0:
                        pe.wait_ge(s_md, MD * m + 15)
                    elif c > 1:
                        pe.wait_ge(s_mh, NC * m + c - 1)
                    o = p_s[0][:, (c % 2) * HALF:][:, 0:CV]
                    mm(o, sch[:, cs], vh2[:, c, :], start=True, stop=False)
                    mm(o, sch[:, cs], vl2[:, c, :], start=False, stop=False)
                    mm(o, scl[:, cs], vh2[:, c, :], start=False, stop=True).then_inc(s_mx2, 1)
                    run(steps, todo // 2)
                    if c:
                        pe.wait_ge(s_mcl, (NC - 1) * m + c)
                        if c > 1:
                            pe.wait_ge(s_mt, NC * m + c - 1)
                    o = (p_t, p_o)[c % 2][:, 0:CV]
                    mm(o, qth[:, cs], chi[c % 2][:, :], start=True, stop=False)
                    mm(o, qth[:, cs], clo[c % 2][:, :], start=False, stop=False)
                    mm(o, qtl[:, cs], chi[c % 2][:, :], start=False, stop=True).then_inc(s_mi, 1)
                    run(steps, todo - todo // 2)
                pe.wait_ge(s_md, MD * m + 21)
                for i in range(NC):
                    last = nc.tensor.transpose(p_s[0][:, i * P:(i + 1) * P], hn[:, i, 0:P], ident[:, :])
                last.then_inc(s_mht, 1)
                run(steps, 100)

            def rglru(r, kind, turn):
                steps = z_steps(kind, turn)
                run(steps, 8)
                pe.wait_ge(s_unit, 8 + r + 1)
                pe.wait_ge(s_rw, 64 * (r + 1))
                pe.wait_ge(s_rd, RD * r + 4)
                for gate in range(2):
                    for half in range(2):
                        cs = slice(half * HALF, (half + 1) * HALF)
                        last = mm(p_s[gate][:, cs], wad[:, gate, :], xc[:, cs], start=True, stop=True)
                    last.then_inc(s_rg, 1)
                run(steps, 100)

            with pe.Fori(0, TURNS - 1) as a:
                fox(a, "F", a + 1)
            fox(TURNS - 1, "M", 0)
            with pe.Fori(0, TURNS - 1) as a:
                mlstm(a, "M", a + 1)
            mlstm(TURNS - 1, "R", 0)
            with pe.Fori(0, TURNS - 1) as a:
                rglru(a, "R", a + 1)
            rglru(TURNS - 1, None, 0)

            for grp in range(2):
                for n in range(12):
                    u = 12 * grp + n
                    if grp == 0:
                        pe.wait_ge(s_ow, n + 1)
                        if n == 0:
                            pe.wait_ge(s_unit, 13)
                    pe.wait_ge(s_yh, u + 1)
                    pe.wait_ge(s_yl, u + 1)
                    for i in range(4):
                        if grp and n == 0:
                            pe.wait_ge(s_h, i + 1)
                        sl = slice(i * P, (i + 1) * P)
                        for dh in range(2):
                            cs = slice(dh * HALF, (dh + 1) * HALF)
                            o = ps[i][:, cs]
                            mm(o, ysh[n % 2][:, sl], wo[:, n, 0, cs], start=(n == 0), stop=False)
                            mm(o, ysh[n % 2][:, sl], wo[:, n, 1, cs], start=False, stop=False)
                            last = mm(o, ysl[n % 2][:, sl], wo[:, n, 0, cs], start=False, stop=(n == 11))
                    last.then_inc(s_om, 1)

            def h_transposes(i):
                pe.wait_ge(s_q4, i + 1)
                if i == 0:
                    pe.wait_ge(s_h, 8)
                    pe.wait_ge(s_pp, 16)
                else:
                    pe.wait_ge(s_ql, i)
                for k in range(KD):
                    nc.tensor.transpose(ps[1][:, k * P:(k + 1) * P], hq[i % 2][:, k * P:(k + 1) * P], ident[:, :])
                for k in range(KP):
                    last = nc.tensor.transpose(ps[0][:, k * P:(k + 1) * P], praw[:, i, k * P:(k + 1) * P], ident[:, :])
                last.then_inc(s_qt, 1)

            h_transposes(0)
            for i in range(SB):
                if i < SB - 1:
                    h_transposes(i + 1)
                if i == 0:
                    pe.wait_ge(s_ow, 22)
                pe.wait_ge(s_ql, i + 1)
                for dst, hi, lo, k0, nk, free in ((ps[2], hth, htl, 0, KD, s_th), (ps[3], pth, ptl, KD, KP, s_t1)):
                    if i:
                        pe.wait_ge(free, i)
                    for half in range(2):
                        cs = slice(half * HALF, (half + 1) * HALF)
                        for k in range(nk):
                            mm(dst[:, cs], hi[i % 2][:, k, :], wo[:, k0 + k, 0, cs], start=(k == 0), stop=False)
                            mm(dst[:, cs], hi[i % 2][:, k, :], wo[:, k0 + k, 1, cs], start=False, stop=False)
                            last = mm(dst[:, cs], lo[i % 2][:, k, :], wo[:, k0 + k, 0, cs], start=False,
                                      stop=(k == nk - 1))
                    last.then_inc(s_gt2, 1)

        @block.scalar
        def _(act):
            af = nc.scalar.activation
            with nc.allow_non_contiguous_dma(reason="small parameter columns"):
                def col(c, n, src):
                    act.dma_start(prm[:, c:c + n], src.rearrange("l (k p) -> (l p) k", p=P)).then_inc(s_par, 16)
                col(0, 8, norm_g)
                col(8, 8, ple_g)
                for j in range(4):
                    col(16 + 4 * j, 4, conv_w[:, j, :])
                col(32, 4, conv_b)
                col(36, 4, ba)
                col(40, 4, bx)
                col(44, 4, lam)
                for h in range(2):
                    act.dma_start(prm[64 * h:64 * h + 64, 48:49], q_g.rearrange("l d -> d l")).then_inc(s_par, 16)
                    act.dma_start(prm[64 * h:64 * h + 64, 49:50], k_g.rearrange("l d -> d l")).then_inc(s_par, 16)
                act.wait_ge(s_gb0, 1)
                act.dma_start(gcol[0:8, 0:1], fox_b_f.rearrange("l d -> d l")).then_inc(s_gb, 16)
                act.dma_start(gcol[64:68, 0:1], ml_b_f.rearrange("l d -> d l")).then_inc(s_gb, 16)
                act.dma_start(gcol[64:68, 1:2], ml_b_i.rearrange("l d -> d l")).then_inc(s_gb, 16)
                act.dma_start(wgraw[:, :, 0:8], w_cols[:, :, C_FF:C_FF + 8]).then_inc(s_wgd, 16)
                act.dma_start(wgraw[:, :, 8:16], w_cols[:, :, C_MI:C_MI + 8]).then_inc(s_wgd, 16)

            for half in range(2):
                act.wait_ge(s_x[half], 64)
                for i in range(4 * half, 4 * half + 4):
                    last = af(junk[:, i, :], xt[:, i, :], ACT.Square, accum_out=prm[:, 80 + i:81 + i])
                last.then_inc(s_ssq, 1)
                act.wait_ge(s_ssq, half + 1)
                act.wait_ge(s_id, 1)
                r = prm[:, 80 + 4 * half:84 + 4 * half]
                af(r, r, ACT.Ln, bias=prm[:, 52:53], scale=1.0 / D).then_inc(s_ln, 1)
                act.wait_ge(s_ln, half + 1)
                af(r, r, ACT.Exp, scale=-0.5).then_inc(s_rstd, 1)
            act.wait_ge(s_par, PARAMS * 16)
            for n in range(16):
                half, k = n // KD, n % KD
                act.wait_ge(s_xT, n + 1)
                bank = ps[n % 8 // 2][:, n % 2 * HALF:(n % 2 + 1) * HALF]
                af(uh[:, k, half * HALF:(half + 1) * HALF], bank, ACT.Identity, scale=prm[:, k:k + 1])\
                    .then_inc(s_uh, 1)
            act.wait_ge(s_id, 2)
            af(identr[:, :], ident[:, :], ACT.Copy).then_inc(s_cc, 1)
            af(maskr[:, :], maskf[:, :], ACT.Copy).then_inc(s_cc, 1)

            af(prm[:, 76:80], prm[:, 44:48], ACT.Abs).then_inc(s_lam0, 1)
            act.wait_ge(s_lam0, 1)
            af(prm[:, 56:60], prm[:, 76:80], ACT.Exp, scale=-1.0).then_inc(s_lam, 1)
            act.wait_ge(s_pc, 3)
            af(prm[:, 64:68], prm[:, 60:64], ACT.Ln).then_inc(s_lam, 1)

            act.wait_ge(s_gb, 48)
            act.wait_ge(s_xT, 16)
            for half in range(2):
                cs = slice(half * HALF, (half + 1) * HALF)
                act.wait_ge(s_z, half + 1)
                af(xb[0:96, cs], pz[half][0:96], ACT.Identity, bias=gcol[:, 0:1]).then_inc(s_ga, 1)
                af(ar[64:68, cs], pz[half][32:36], ACT.Copy).then_inc(s_ze, 1)
            act.wait_ge(s_ga, 2)
            af(ex[0:96, :], xb[0:96, :], ACT.Abs).then_inc(s_ga, 1)
            act.wait_ge(s_ga, 3)
            af(ex[0:96, :], ex[0:96, :], ACT.Exp, scale=-1.0).then_inc(s_ga, 1)
            act.wait_ge(s_ga, 4)
            af(ex[0:96, :], ex[0:96, :], ACT.Ln, bias=prm[0:96, 53:54]).then_inc(s_ga, 1)

            def save(kind, turn, upto, state, frees=None):
                while state[0] < upto // 8:
                    n = state[0]
                    b, half = n // 2, n % 2
                    B = FIRST[kind] + len(UNIT[kind]) * turn + b
                    act.wait_ge(s_z, 2 * B + half + 1)
                    if half == 0 and frees:
                        act.wait_ge(*frees[b])
                    af(zst[b][:, half * HALF:(half + 1) * HALF], pz[half], ACT.Copy).then_inc(s_ze, 1)
                    state[0] += 1

            st = [0]
            save("F", 0, 32, st)
            act.wait_ge(s_gm, 2)
            act.wait_ge(s_gd, 3)
            af(rw[0:4, :], ar[64:68, :], ACT.Copy).then_inc(s_ga, 1)
            act.wait_ge(s_gd, 2)
            act.wait_ge(s_gm, 1)
            af(crow[0:8, :], nb[0:8, :], ACT.Copy).then_inc(s_ga, 1)
            act.wait_ge(s_gd, 7)
            af(rw[64:68, :], ex[64:68, :], ACT.Exp).then_inc(s_ga, 1)
            act.wait_ge(s_gd, 8)
            af(rw[96:100, :], xb[64:68, :], ACT.Exp).then_inc(s_ga, 1)
            act.wait_ge(s_gd, 9)
            af(rw[32:36, :], lf[64:68, :], ACT.Exp).then_inc(s_ga, 1)
            act.wait_ge(s_ga, 8)
            with nc.allow_non_contiguous_dma(reason="last token of each chunk"):
                act.dma_start(g_dram, gr[64:68, :]).then_inc(s_gw, 16)
                act.dma_start(wl_dram, rw[64:68, :].rearrange("p (c t) -> p c t", t=CH)[:, :, CH - 1])\
                    .then_inc(s_gw, 16)
            for half in range(2):
                act.wait_ge(s_gt, half + 1)
                af(cols[:, 4 * half:4 * half + 4, :, :],
                   (p_t, p_o)[half].rearrange("p (c q r) -> p c q r", c=4, q=4)[:, :, :, 0:4], ACT.Copy)\
                    .then_inc(s_gc, 1)
            save("F", 0, 64, st)

            def fox(a, kind, turn):
                state = [0]
                total = 16 * len(UNIT[kind])
                frees = [(s_fd, FD * a + 1), (s_fd, FD * a + 2), (s_vt, 2 * a + 2), (s_og, a + 1), (s_ga, 1)]
                act.wait_ge(s_unit, a + 1)
                act.wait_ge(s_gc, 2)
                act.wait_ge(s_gw, 32)
                for n in range(2):
                    act.wait_ge(s_ze, 2 * (FIRST["F"] + 4 * a + n) + 2)
                    af(pr[n][:, :], zst[n][:, :], ACT.Square).then_inc(s_fa, 1)
                for n in range(2):
                    act.wait_ge(s_ms, 2 * a + n + 1)
                    af(rq[n][:, :], p_s[n][:, :], ACT.Ln, bias=prm[:, 52:53]).then_inc(s_fa, 1)
                for n in range(2):
                    act.wait_ge(s_fa, FA * a + 3 + n)
                    af(rq[n][:, :], rq[n][:, :], ACT.Exp, scale=-0.5).then_inc(s_fa, 1)
                act.wait_ge(s_fd, FD * a + 1)
                af(qs[0][0:64, :], rq[0][0:64, :], ACT.Copy).then_inc(s_fa, 1)
                af(qs[1][64:128, :], rq[0][64:128, :], ACT.Copy).then_inc(s_fa, 1)
                act.wait_ge(s_fd, FD * a + 2)
                af(ka[0][0:64, :], rq[1][0:64, :], ACT.Copy).then_inc(s_fa, 1)
                af(ka[1][64:128, :], rq[1][64:128, :], ACT.Copy).then_inc(s_fa, 1)
                af(ka[0][64:128, :], rq[1][0:64, :], ACT.Copy).then_inc(s_fa, 1)
                af(ka[1][0:64, :], rq[1][64:128, :], ACT.Copy).then_inc(s_fa, 1)
                for half in range(2):
                    act.wait_ge(s_vt, 2 * a + half + 1)
                    src = (p_t, p_o)[half].rearrange("p (i h d) -> p i h d", i=4, h=2)
                    af(vhl[:, 4 * half:4 * half + 4, 0, 0:64], src[:, :, 0, :], ACT.Copy)
                    af(vhl[:, 4 * half:4 * half + 4, 1, 64:128], src[:, :, 1, :], ACT.Copy).then_inc(s_vh, 1)
                act.wait_ge(s_ze, 2 * (FIRST["F"] + 4 * a + 3) + 2)
                af(og[:, :], zst[3][:, :], ACT.Tanh, scale=0.5).then_inc(s_fa, 1)
                save(kind, turn, min(32, total), state, frees)
                done = min(32, total)
                upto = spread(total - done, 16)

                def probs(t):
                    h, i = t // SB, t % SB
                    n = (i + 1) * P
                    act.wait_ge(s_nm, 16 * a + t + 1)
                    if t >= 2:
                        act.wait_ge(s_pt, 24 * a + ngroups(t - 1))
                    af(pr[t % 2][:, 0:n], p_s[t % 2][:, 0:n], ACT.Exp, bias=sm[:, t % 2:t % 2 + 1],
                       accum_out=sm[:, 2 + t % 2:3 + t % 2]).then_inc(s_ex, 1)

                probs(0)
                for t in range(16):
                    h, i = t // SB, t % SB
                    for g in range(i // 4 + 1):
                        n_g = 24 * a + ngroups(t) + g
                        act.wait_ge(s_pt, n_g + 1)
                        if g == 0 and t:
                            act.wait_ge(s_pv, 16 * a + t)
                        j0, j1 = 4 * g, min(4 * g + 4, i + 1)
                        af(pt[:, j0:j1, 0:P], p_t[:, 0:(j1 - j0) * P].rearrange("p (j q) -> p j q", q=P), ACT.Copy)\
                            .then_inc(s_ph, 1)
                    if t < 15:
                        probs(t + 1)
                    act.wait_ge(s_pv, 16 * a + t + 1)
                    if t:
                        act.wait_ge(s_ot, 16 * a + t)
                    hi, lo = (slice(0, 64), slice(64, 128)) if h == 0 else (slice(64, 128), slice(0, 64))
                    af(oc[hi, :], p_o[lo, 0:2 * P], ACT.Copy).then_inc(s_oc, 1)
                    save(kind, turn, done + upto[t], state, frees)

            def mlstm(m, kind, turn):
                state = [0]
                total = 16 * len(UNIT[kind])
                done = min(24, total // 2)
                upto = spread(total - done, NC)
                frees = [(s_md, MD * m + 6), (s_md, MD * m + 11), (s_mvt, 2 * m + 2), (s_md, MD * m + 17),
                         (s_md, MD * m + 17)]
                B0 = FIRST["M"] + 5 * m
                act.wait_ge(s_unit, 4 + m + 1)
                act.dma_start(eg[:, :, :].rearrange("p c t -> p (c t)"),
                              g_dram[bass.ds(m, 1), :].broadcast_to([P, S])).then_inc(s_mg, 16)
                act.dma_start(dec[:, :], wl_dram[bass.ds(m, 1), :].broadcast_to([P, NC])).then_inc(s_mg, 16)
                act.wait_ge(s_ze, 2 * B0 + 2)
                af(qth[:, :], zst[0][:, :], ACT.Copy).then_inc(s_ma, 1)
                act.wait_ge(s_md, MD * m + 1)
                af(kth[:, :], zst[1][:, :], ACT.Copy).then_inc(s_ma, 1)
                for half in range(2):
                    act.wait_ge(s_mvt, 2 * m + half + 1)
                    af(vh2[:, 4 * half:4 * half + 4, 0:P], (p_t, p_o)[half].rearrange("p (c e) -> p c e", e=P),
                       ACT.Copy).then_inc(s_ma, 1)
                act.wait_ge(s_mg, 32 * (m + 1))
                act.wait_ge(s_md, MD * m + 2)
                for c in range(NC):
                    af(eg[:, c, :], eg[:, c, :], ACT.Exp, bias=ucol[:, c, 0:1], scale=-1.0).then_inc(s_ma, 1)
                act.wait_ge(s_md, MD * m + 10)
                af(kwh[:, :, :].rearrange("p c d -> p (c d)"), zst[1][:, :], ACT.Copy).then_inc(s_ma, 1)
                act.wait_ge(s_md, MD * m + 14)
                af(sch[:, :], eg[:, :, :].rearrange("p c t -> p (c t)"), ACT.Copy).then_inc(s_ma, 1)
                act.wait_ge(s_ze, 2 * (B0 + 4) + 2)
                af(zst[3][:, :], zst[3][:, :], ACT.Tanh, scale=0.5).then_inc(s_ma, 1)
                af(yt[:, bass.ds(8 + m, 1), :].rearrange("p o s -> p (o s)"), zst[4][:, :], ACT.Tanh, scale=0.5)\
                    .then_inc(s_ma, 1)
                save(kind, turn, done, state, frees)
                for c in range(NC):
                    if c < NC - 1:
                        act.wait_ge(s_mc, (NC - 1) * m + c + 1)
                        if c > 0:
                            act.wait_ge(s_mi, NC * m + c)
                        af(chi[(c + 1) % 2][:, :], cf[:, :], ACT.Copy).then_inc(s_mch, 1)
                    act.wait_ge(s_mi, NC * m + c + 1)
                    if c > 1:
                        act.wait_ge(s_mh, NC * m + c - 1)
                    af(ti2[c % 2][:, :], (p_t, p_o)[c % 2][:, 0:CV], ACT.Identity, scale=ucol[:, c, 2:3])\
                        .then_inc(s_mt, 1)
                    save(kind, turn, done + upto[c], state, frees)
                save(kind, turn, total, state, frees)

            def rglru(r, kind, turn):
                state = [0]
                total = 16 * len(UNIT[kind])
                B0 = FIRST["R"] + 2 * r
                frees = [(s_rd, RD * r + 4), (s_rd, RD * r + 11)]
                act.wait_ge(s_unit, 8 + r + 1)
                act.wait_ge(s_rz, 1)
                for gate, w in enumerate((wa, wx)):
                    for b in range(2):
                        act.dma_start(wad[64 * b:64 * b + 64, gate, 64 * b:64 * b + 64],
                                      w[0, bass.ds(2 * r + b, 1), :, :].rearrange("o c d -> (o c) d")).then_inc(s_rw, 16)
                act.wait_ge(s_ze, 2 * B0 + 4)
                act.wait_ge(s_rd, RD * r + 1)
                af(xc[:, :], zst[0][:, :], ACT.Identity, bias=rcol[:, 4:5], scale=rcol[:, 3:4]).then_inc(s_ra, 1)
                af(tg[:, :], zst[1][:, :], ACT.Tanh, scale=0.5).then_inc(s_ra, 1)
                save(kind, turn, min(8, total), state, frees)
                for gate, o in enumerate((tr, ti)):
                    act.wait_ge(s_rg, 2 * r + gate + 1)
                    af(o[:, :], p_s[gate][:, :], ACT.Tanh, bias=rcol[:, 5 + gate:6 + gate], scale=0.5)\
                        .then_inc(s_ra, 1)
                act.wait_ge(s_rd, RD * r + 5)
                af(tt[:, :], tr[:, :], ACT.Tanh).then_inc(s_ra, 1)
                act.wait_ge(s_ra, RA * r + 5)
                af(tr[:, :], tr[:, :], ACT.Exp, scale=-1.0).then_inc(s_ra, 1)
                act.wait_ge(s_rd, RD * r + 6)
                af(l1[:, :], tt[:, :], ACT.Ln, scale=2.0).then_inc(s_ra, 1)
                af(l2[:, :], tt[:, :], ACT.Ln, bias=prm[:, 53:54]).then_inc(s_ra, 1)
                act.wait_ge(s_rd, RD * r + 7)
                af(l1[:, :], l1[:, :], ACT.Exp, scale=0.5).then_inc(s_ra, 1)
                save(kind, turn, total, state, frees)

            with act.Fori(0, TURNS - 1) as a:
                fox(a, "F", a + 1)
            fox(TURNS - 1, "M", 0)
            with act.Fori(0, TURNS - 1) as a:
                mlstm(a, "M", a + 1)
            mlstm(TURNS - 1, "R", 0)
            with act.Fori(0, TURNS - 1) as a:
                rglru(a, "R", a + 1)
            rglru(TURNS - 1, None, 0)

            for u in range(24):
                n, grp = u % 12, u // 12
                act.wait_ge(s_unit, 13)
                if u >= 2:
                    act.wait_ge(s_om, u - 1)
                if u == 0:
                    act.wait_ge(s_z, 90)
                af(ysh[n % 2][:, :], yt[:, EORD[n], grp * HALF:(grp + 1) * HALF], ACT.Copy).then_inc(s_yh, 1)

            def h_stats(i):
                act.wait_ge(s_h, i + 1)
                if i == 0:
                    act.wait_ge(s_yl, 24)
                if i >= 2:
                    act.wait_ge(s_fin, i - 1)
                af(th[i % 2][:, :], ht[i][:, :], ACT.Square, accum_out=prm[:, 80 + i:81 + i]).then_inc(s_q1, 1)
                act.wait_ge(s_q1, i + 1)
                af(prm[:, 80 + i:81 + i], prm[:, 80 + i:81 + i], ACT.Ln, bias=prm[:, 52:53], scale=1.0 / D)\
                    .then_inc(s_q2, 1)
                act.wait_ge(s_q2, i + 1)
                af(prm[:, 80 + i:81 + i], prm[:, 80 + i:81 + i], ACT.Exp, scale=-0.5).then_inc(s_q3, 1)

            act.wait_ge(s_yh, 24)
            h_stats(0)
            h_stats(1)
            for i in range(SB):
                act.wait_ge(s_qt, i + 1)
                if i >= 2:
                    act.wait_ge(s_gt2, 2 * (i - 1))
                af(hth[i % 2][:, :, :].rearrange("p k s -> p (k s)"), ps[1][:, :], ACT.Copy)
                af(pth[i % 2][:, :, :].rearrange("p k s -> p (k s)"), ps[0][:, 0:KP * P], ACT.Copy).then_inc(s_qh, 1)
                act.wait_ge(s_gt2, 2 * i + 1)
                act.wait_ge(s_q4, min(i + 2, SB))
                af(th[i % 2][:, :], ps[2][:, :], ACT.Tanh, scale=0.5).then_inc(s_th, 1)
                if i + 2 < SB:
                    h_stats(i + 2)

        @block.vector
        def _(dve):
            v = nc.vector
            v.memset(headmean[:, :], 0.0).then_inc(s_hm, 1)
            dve.wait_ge(s_hm, 1)
            v.memset(headmean[0:64, 0:64], 1.0 / FOX_D).then_inc(s_hm, 1)
            v.memset(headmean[64:128, 64:128], 1.0 / FOX_D).then_inc(s_hm, 1)
            for half in range(2):
                dve.wait_ge(s_rstd, half + 1)
                for i in range(4 * half, 4 * half + 4):
                    v.tensor_scalar(xt[:, i, :], xt[:, i, :], prm[:, 80 + i:81 + i], None, ALU.mult).then_inc(s_xn, 1)
            dve.wait_ge(s_par, PARAMS * 16)
            v.tensor_scalar(prm[:, 54:55], prm[:, 48:49], FOX_D ** -0.5, None, ALU.mult).then_inc(s_pc, 1)
            for n in range(16):
                half, k = n // KD, n % KD
                cs = slice(half * HALF, (half + 1) * HALF)
                dve.wait_ge(s_uh, n + 1)
                bank = ps[n % 8 // 2][:, n % 2 * HALF:(n % 2 + 1) * HALF]
                v.scalar_tensor_tensor(ul[:, k, cs], bank, prm[:, k:k + 1], uh[:, k, cs], ALU.mult, ALU.subtract)\
                    .then_inc(s_ul, 1)
            dve.wait_ge(s_ssq, 2)
            v.memset(rm[0:96, :], 1.0).then_inc(s_gv, 1)
            v.memset(mc[64:96, :], 0.0).then_inc(s_gv, 1)
            v.memset(dl[64:96, :], 0.0).then_inc(s_gv, 1)
            dve.wait_ge(s_gv, 3)
            v.memset(rm[64:96, :].rearrange("p (c t) -> p c t", t=CH)[:, :, 0:1], 0.0).then_inc(s_gv, 1)
            pc = [0]

            def small(ins):
                pc[0] += 1
                ins.then_inc(s_pc, 1)
                dve.wait_ge(s_pc, 1 + pc[0])

            t = lambda n: prm[:, 56 + 4 * n:60 + 4 * n]
            small(v.tensor_scalar(prm[:, 36:44], prm[:, 36:44], 0.5, None, ALU.mult))
            dve.wait_ge(s_lam, 1)
            small(v.tensor_scalar(t(1), t(0), 1.0, None, ALU.add))
            dve.wait_ge(s_lam, 2)
            small(v.tensor_scalar(t(1), t(1), -1.0, None, ALU.add))
            small(v.tensor_scalar(t(3), t(1), 0.0, None, ALU.is_equal))
            small(v.tensor_tensor(t(1), t(1), t(3), ALU.add))
            small(v.tensor_tensor(t(2), t(2), t(3), ALU.add))
            small(v.reciprocal(t(4), t(1)))
            small(v.tensor_tensor(t(2), t(2), t(4), ALU.mult))
            small(v.tensor_tensor(t(2), t(2), t(0), ALU.mult))
            small(v.tensor_scalar(t(3), prm[:, 44:48], -1.0, 0.0, ALU.mult, ALU.max))
            small(v.tensor_tensor(t(2), t(2), t(3), ALU.add))
            small(v.tensor_scalar(prm[:, 44:48], t(2), RG_C / 2, None, ALU.mult))
            dve.wait_ge(s_ga, 5)
            v.scalar_tensor_tensor(lf[0:96, :], xb[0:96, :], 0.0, ex[0:96, :], ALU.min, ALU.subtract)\
                .then_inc(s_gd, 1)
            dve.wait_ge(s_gd, 1)
            dve.wait_ge(s_gv, 4)
            v.tensor_tensor_scan(nb[0:96, :], rm[0:96, :], lf[0:96, :], 0.0, ALU.mult, ALU.subtract)\
                .then_inc(s_gd, 1)
            dve.wait_ge(s_gd, 2)
            dve.wait_ge(s_ze, 2)
            v.scalar_tensor_tensor(ar[64:68, :], ar[64:68, :], gcol[64:68, 1:2], nb[64:68, :], ALU.add, ALU.add)\
                .then_inc(s_gd, 1)
            last_of = lambda t: t[64:68, :].rearrange("p (c t) -> p c t", t=CH)[:, :, CH - 1]
            dve.wait_ge(s_gd, 3)
            v.tensor_scalar(dl[64:68, :].rearrange("p (c t) -> p c t", t=CH)[:, 1:, 0], last_of(nb)[:, 0:NC - 1], -1.0,
                            None, ALU.mult).then_inc(s_gd, 1)
            dve.wait_ge(s_gd, 4)
            v.tensor_tensor_scan(gr[64:68, :], dl[64:68, :], ar[64:68, :], 0.0, ALU.add, ALU.max).then_inc(s_gd, 1)
            dve.wait_ge(s_gd, 5)
            v.tensor_tensor(mc[64:68, 1:NC], last_of(gr)[:, 0:NC - 1], last_of(nb)[:, 0:NC - 1], ALU.subtract)\
                .then_inc(s_gd, 1)
            dve.wait_ge(s_gd, 6)
            ch = lambda t: t[64:68, :].rearrange("p (c t) -> p c t", t=CH)
            v.tensor_tensor(ch(ex), bc(mc[64:68, :], CH), ch(gr), ALU.subtract).then_inc(s_gd, 1)
            v.tensor_tensor(ch(xb), ch(ar), bc(last_of(gr), CH), ALU.subtract).then_inc(s_gd, 1)
            v.tensor_tensor(lf[64:68, :], nb[64:68, :], gr[64:68, :], ALU.subtract).then_inc(s_gd, 1)
            dve.wait_ge(s_ga, 7)
            v.tensor_tensor(crow[32:40, :], nb[0:8, :], crow[0:8, :], ALU.subtract).then_inc(s_unit, 1)

            def fox(a):
                dve.wait_ge(s_unit, a + 1)
                dve.wait_ge(s_gm, 5)
                for base in (0, 32):
                    v.tensor_copy(selu[base:base + 32, :, :], selall[base:base + 32, bass.ds(2 * a, 2), :])\
                        .then_inc(s_su, 1)
                for n, g in ((0, 54), (1, 49)):
                    dve.wait_ge(s_fa, FA * a + 5 + n)
                    v.scalar_tensor_tensor(rq[n][:, :], zst[n][:, :], prm[:, g:g + 1], rq[n][:, :], ALU.mult, ALU.mult)\
                        .then_inc(s_fd, 1)
                dve.wait_ge(s_fd, FD * a + 2)
                for h, (hi, lo) in enumerate(((slice(0, 64), slice(64, 128)), (slice(64, 128), slice(0, 64)))):
                    dve.wait_ge(s_fa, FA * a + 7 + h)
                    v.tensor_tensor(qs[h][lo, :], rq[0][hi, :], qs[h][hi, :], ALU.subtract).then_inc(s_fd, 1)
                for h, (hi, lo) in enumerate(((slice(0, 64), slice(64, 128)), (slice(64, 128), slice(0, 64)))):
                    dve.wait_ge(s_fa, FA * a + 9 + h)
                    for to in (hi, lo):
                        v.tensor_tensor(kb[h][to, :], rq[1][hi, :], ka[h][hi, :], ALU.subtract)\
                            .then_inc(s_fd, 1)
                for half in range(2):
                    dve.wait_ge(s_vh, 2 * a + half + 1)
                    src = (p_t, p_o)[half].rearrange("p (i h d) -> p i h d", i=4, h=2)
                    dst = vhl[:, 4 * half:4 * half + 4, :, :]
                    v.tensor_tensor(dst[:, :, 0, 64:128], src[:, :, 0, :], dst[:, :, 0, 0:64], ALU.subtract)
                    v.tensor_tensor(dst[:, :, 1, 0:64], src[:, :, 1, :], dst[:, :, 1, 64:128], ALU.subtract)\
                        .then_inc(s_vl, 1)
                dve.wait_ge(s_fa, FA * a + 13)
                v.scalar_tensor_tensor(og[:, :], og[:, :], 1.0, zst[3][:, :], ALU.add, ALU.mult).then_inc(s_og, 1)

                def maxima(t):
                    n = (t % SB + 1) * P
                    dve.wait_ge(s_sc, 16 * a + t + 1)
                    v.tensor_reduce(sm[:, 4 + t % 2:5 + t % 2], p_s[t % 2][:, 0:n], AX_X, ALU.max).then_inc(s_mx, 1)
                    dve.wait_ge(s_mx, 16 * a + t + 1)
                    v.tensor_scalar(sm[:, t % 2:t % 2 + 1], sm[:, 4 + t % 2:5 + t % 2], -1.0, None, ALU.mult)\
                        .then_inc(s_nm, 1)

                def scale(t):
                    n = (t % SB + 1) * P
                    dve.wait_ge(s_ex, 16 * a + t + 1)
                    v.reciprocal(sm[:, 6 + t % 2:7 + t % 2], sm[:, 2 + t % 2:3 + t % 2]).then_inc(s_rc, 1)
                    dve.wait_ge(s_rc, 16 * a + t + 1)
                    v.tensor_scalar(pr[t % 2][:, 0:n], pr[t % 2][:, 0:n], sm[:, 6 + t % 2:7 + t % 2], None, ALU.mult)\
                        .then_inc(s_pn, 1)

                maxima(0)
                scale(0)
                for t in range(16):
                    h, i = t // SB, t % SB
                    if t < 15:
                        maxima(t + 1)
                    for g in range(i // 4 + 1):
                        n_g = 24 * a + ngroups(t) + g
                        dve.wait_ge(s_ph, n_g + 1)
                        j0, j1 = 4 * g, min(4 * g + 4, i + 1)
                        v.tensor_tensor(pt[:, j0:j1, P:], p_t[:, 0:(j1 - j0) * P].rearrange("p (j q) -> p j q", q=P),
                                        pt[:, j0:j1, 0:P], ALU.subtract).then_inc(s_pl, 1)
                    if t < 15:
                        scale(t + 1)
                    hi = slice(0, 64) if h == 0 else slice(64, 128)
                    dve.wait_ge(s_oc, 16 * a + t + 1)
                    v.tensor_tensor(oc[hi, :], p_o[hi, 0:2 * P], oc[hi, :], ALU.add).then_inc(s_oa, 1)
                    dve.wait_ge(s_oa, 16 * a + t + 1)
                    v.tensor_tensor(ot[hi, i * P:(i + 1) * P], oc[hi, 0:P], oc[hi, P:], ALU.add).then_inc(s_ot, 1)
                dve.wait_ge(s_ot, 16 * a + 16)
                dve.wait_ge(s_og, a + 1)
                v.scalar_tensor_tensor(yt[:, bass.ds(4 + a, 1), :].rearrange("p o s -> p (o s)"), ot[:, :], 0.5,
                                       og[:, :], ALU.mult, ALU.mult).then_inc(s_unit, 1)

            def mlstm(m):
                B0 = FIRST["M"] + 5 * m
                yrow = yt[:, bass.ds(8 + m, 1), :].rearrange("p o s -> p (o s)")
                e2 = eg[:, :, :].rearrange("p c t -> p (c t)")
                dve.wait_ge(s_unit, 4 + m + 1)
                dve.wait_ge(s_ze, 2 * (B0 + 1) + 2)
                v.tensor_scalar(zst[1][:, :], zst[1][:, :], CH ** -0.5, None, ALU.mult).then_inc(s_md, 1)
                v.tensor_copy(ucol[:, :, :], cols[:, :, :, bass.ds(m, 1)].rearrange("p c q o -> p c (q o)"))\
                    .then_inc(s_md, 1)
                v.memset(cf[:, :], 0.0).then_inc(s_md, 1)
                v.memset(chi[0][:, :].bitcast(F32), 0.0).then_inc(s_md, 1)
                v.memset(clo[0][:, :].bitcast(F32), 0.0).then_inc(s_md, 1)
                dve.wait_ge(s_ma, MA * m + 1)
                v.tensor_tensor(qtl[:, :], zst[0][:, :], qth[:, :], ALU.subtract).then_inc(s_md, 1)
                dve.wait_ge(s_ma, MA * m + 2)
                v.tensor_tensor(ktl[:, :], zst[1][:, :], kth[:, :], ALU.subtract).then_inc(s_md, 1)
                for half in range(2):
                    dve.wait_ge(s_ma, MA * m + 3 + half)
                    v.tensor_tensor(vl2[:, 4 * half:4 * half + 4, 0:P], (p_t, p_o)[half].rearrange(
                        "p (c e) -> p c e", e=P), vh2[:, 4 * half:4 * half + 4, 0:P], ALU.subtract).then_inc(s_md, 1)
                dve.wait_ge(s_mkt, m + 1)
                dve.wait_ge(s_md, MD * m + 7)
                v.tensor_tensor(zst[1][:, :].rearrange("p (c d) -> p c d", d=P), p_s[1][:, :].rearrange(
                    "p (c d) -> p c d", d=P), bc(ucol[:, :, 3], P), ALU.mult).then_inc(s_md, 1)
                dve.wait_ge(s_ma, MA * m + 13)
                v.tensor_tensor(kwl[:, :, :].rearrange("p c d -> p (c d)"), zst[1][:, :],
                                kwh[:, :, :].rearrange("p c d -> p (c d)"), ALU.subtract).then_inc(s_md, 1)
                v.scalar_tensor_tensor(eg[:, :, :], eg[:, :, :], 1.0, tri[:, :].unsqueeze(1).broadcast_to([P, NC, CH]),
                                       ALU.min, ALU.mult).then_inc(s_md, 1)
                dve.wait_ge(s_md, MD * m + 12)
                for half in range(2):
                    cs = slice(half * HALF, (half + 1) * HALF)
                    dve.wait_ge(s_mst, 2 * m + half + 1)
                    v.tensor_tensor(e2[:, cs], e2[:, cs], p_s[0][:, cs], ALU.mult).then_inc(s_md, 1)
                dve.wait_ge(s_ma, MA * m + 14)
                v.tensor_tensor(scl[:, :], e2, sch[:, :], ALU.subtract).then_inc(s_md, 1)
                dve.wait_ge(s_ma, MA * m + 16)
                v.scalar_tensor_tensor(zst[4][:, :], yrow, 1.0, zst[4][:, :], ALU.add, ALU.mult).then_inc(s_md, 1)
                dve.wait_ge(s_md, MD * m + 16)
                v.scalar_tensor_tensor(yrow, zst[3][:, :], 1.0, zst[4][:, :], ALU.add, ALU.mult).then_inc(s_md, 1)
                for c in range(NC):
                    if c < NC - 1:
                        dve.wait_ge(s_mu, (NC - 1) * m + c + 1)
                        if c:
                            dve.wait_ge(s_mcl, (NC - 1) * m + c)
                        v.scalar_tensor_tensor(cf[:, :], cf[:, :], dec[:, c:c + 1], p_s[1][:, (c % 2) * HALF:][:, 0:CV],
                                               ALU.mult, ALU.add).then_inc(s_mc, 1)
                        dve.wait_ge(s_mch, (NC - 1) * m + c + 1)
                        v.tensor_tensor(clo[(c + 1) % 2][:, :], cf[:, :], chi[(c + 1) % 2][:, :], ALU.subtract)\
                            .then_inc(s_mcl, 1)
                    dve.wait_ge(s_mx2, NC * m + c + 1)
                    dve.wait_ge(s_mt, NC * m + c + 1)
                    v.tensor_tensor(hn[:, c, :], ti2[c % 2][:, :], p_s[0][:, (c % 2) * HALF:][:, 0:CV], ALU.add)\
                        .then_inc(s_mh, 1)
                dve.wait_ge(s_mh, NC * (m + 1))
                v.scalar_tensor_tensor(den[:, :], hn[:, :, P], -1.0, hn[:, :, P], ALU.mult, ALU.max)\
                    .then_inc(s_md, 1)
                dve.wait_ge(s_md, MD * m + 18)
                v.tensor_tensor(den[:, :], den[:, :], ucol[:, :, 1], ALU.max).then_inc(s_md, 1)
                dve.wait_ge(s_md, MD * m + 19)
                v.reciprocal(den[:, :], den[:, :]).then_inc(s_md, 1)
                dve.wait_ge(s_md, MD * m + 20)
                v.tensor_tensor(hn[:, :, 0:P], hn[:, :, 0:P], bc(den[:, :], P), ALU.mult).then_inc(s_md, 1)
                dve.wait_ge(s_mht, m + 1)
                v.scalar_tensor_tensor(yrow, p_s[0][:, :], 0.25, yrow, ALU.mult, ALU.mult).then_inc(s_unit, 1)

            def rglru(r):
                stt = v.scalar_tensor_tensor
                dve.wait_ge(s_unit, 8 + r + 1)
                v.tensor_copy(rcol[:, :], prm[:, 16:48].rearrange("p (q k) -> p q k", k=4)[:, :, bass.ds(r, 1)]
                              .rearrange("p q o -> p (q o)")).then_inc(s_rd, 1)
                dve.wait_ge(s_ra, RA * r + 1)
                for j in range(1, 4):
                    if j > 1:
                        dve.wait_ge(s_rd, RD * r + j)
                    stt(xc[:, j:], zst[0][:, 0:S - j], rcol[:, 3 - j:4 - j], xc[:, j:], ALU.mult, ALU.add)\
                        .then_inc(s_rd, 1)
                dve.wait_ge(s_ra, RA * r + 3)
                v.tensor_scalar(tr[:, :], tr[:, :], 1.0, rcol[:, 7:8], ALU.add, ALU.mult).then_inc(s_rd, 1)
                dve.wait_ge(s_ra, RA * r + 6)
                v.tensor_scalar(tt[:, :], tt[:, :], 1e-18, None, ALU.max).then_inc(s_rd, 1)
                dve.wait_ge(s_ra, RA * r + 8)
                v.tensor_tensor(l1[:, :], l1[:, :], l2[:, :], ALU.subtract).then_inc(s_rd, 1)
                stt(xc[:, :], ti[:, :], 1.0, xc[:, :], ALU.add, ALU.mult).then_inc(s_rd, 1)
                dve.wait_ge(s_rd, RD * r + 8)
                dve.wait_ge(s_ra, RA * r + 9)
                stt(xc[:, :], xc[:, :], 0.5, l1[:, :], ALU.mult, ALU.mult).then_inc(s_rd, 1)
                dve.wait_ge(s_rd, RD * r + 9)
                v.tensor_tensor_scan(ti[:, :], tr[:, :], xc[:, :], 0.0, ALU.mult, ALU.add).then_inc(s_rd, 1)
                stt(tg[:, :], tg[:, :], 1.0, zst[1][:, :], ALU.add, ALU.mult).then_inc(s_rd, 1)
                dve.wait_ge(s_rd, RD * r + 11)
                stt(yt[:, bass.ds(r, 1), :].rearrange("p o s -> p (o s)"), ti[:, :], 0.5, tg[:, :], ALU.mult,
                    ALU.mult).then_inc(s_unit, 1)

            with dve.Fori(0, TURNS - 1) as a:
                fox(a)
            fox(TURNS - 1)
            dve.wait_ge(s_unit, 5)
            v.memset(vh2[:, :, P:P + 1].bitcast(F32), 1.0).then_inc(s_mone, 1)
            v.memset(vh2[:, :, P + 1:CV].bitcast(F32), 0.0).then_inc(s_mone, 1)
            v.memset(vl2[:, :, P:CV].bitcast(F32), 0.0).then_inc(s_mone, 1)
            with dve.Fori(0, TURNS - 1) as a:
                mlstm(a)
            mlstm(TURNS - 1)
            dve.wait_ge(s_unit, 9)
            v.memset(wad[:, :, :], 0.0).then_inc(s_rz, 1)
            with dve.Fori(0, TURNS - 1) as a:
                rglru(a)
            rglru(TURNS - 1)

            def save_h(i):
                dve.wait_ge(s_hx, 16 * SB)
                dve.wait_ge(s_om, 12 * (i // 4 + 1))
                v.tensor_tensor(ht[i][:, :], ht[i][:, :], ps[i % 4][:, :], ALU.add).then_inc(s_h, 1)

            for u in range(24):
                n, grp = u % 12, u // 12
                if u == 12:
                    for i in range(4):
                        save_h(i)
                dve.wait_ge(s_yh, u + 1)
                v.tensor_tensor(ysl[n % 2][:, :], yt[:, EORD[n], grp * HALF:(grp + 1) * HALF], ysh[n % 2][:, :],
                                ALU.subtract).then_inc(s_yl, 1)
            for i in range(4, 8):
                save_h(i)

            def h_scale(i):
                dve.wait_ge(s_q3, i + 1)
                if i >= 2:
                    dve.wait_ge(s_qt, i - 1)
                v.tensor_scalar(hq[i % 2][:, :], ht[i][:, :], prm[:, 80 + i:81 + i], None, ALU.mult).then_inc(s_q4, 1)

            dve.wait_ge(s_yl, 24)
            h_scale(0)
            h_scale(1)
            for i in range(SB):
                dve.wait_ge(s_qh, i + 1)
                if i >= 2:
                    dve.wait_ge(s_gt2, 2 * (i - 1))
                v.tensor_tensor(htl[i % 2][:, :, :].rearrange("p k s -> p (k s)"), ps[1][:, :],
                                hth[i % 2][:, :, :].rearrange("p k s -> p (k s)"), ALU.subtract)
                v.tensor_tensor(ptl[i % 2][:, :, :].rearrange("p k s -> p (k s)"), ps[0][:, 0:KP * P],
                                pth[i % 2][:, :, :].rearrange("p k s -> p (k s)"), ALU.subtract).then_inc(s_ql, 1)
                dve.wait_ge(s_th, i + 1)
                dve.wait_ge(s_gt2, 2 * i + 2)
                v.scalar_tensor_tensor(th[i % 2][:, :], th[i % 2][:, :], 1.0, ps[3][:, :], ALU.add, ALU.mult)\
                    .then_inc(s_t1, 1)
                dve.wait_ge(s_t1, i + 1)
                v.scalar_tensor_tensor(ht[i][:, :], th[i % 2][:, :], 0.5, ht[i][:, :], ALU.mult, ALU.add)\
                    .then_inc(s_fin, 1)
                if i + 2 < SB:
                    h_scale(i + 2)


def bc(ap, n):
    return ap.unsqueeze(2).broadcast_to([ap.shape[0], ap.shape[1], n])


_INS = ["x", "p", "norm_g", "w_in", "rg_conv_w", "rg_conv_b", "rg_wa", "rg_ba", "rg_wx", "rg_bx", "rg_lambda",
        "fox_b_f", "fox_q_g", "fox_k_g", "ml_b_i", "ml_b_f", "w_out", "ple_norm_g", "w_ple_gate", "w_ple"]


def kernel(**inputs):
    import numpy as _np
    import concourse.bacc as _bacc
    from concourse.bass_utils import run_bass_kernel_spmd as _run

    nc = _bacc.Bacc("TRN2", target_bir_lowering=False, num_devices=1)
    arrays, args = {}, []
    for name in _INS:
        a = _np.ascontiguousarray(inputs[name])
        arrays[f"in_{name}"] = a
        args.append(nc.dram_tensor(f"in_{name}", a.shape, mybir.dt.from_np(a.dtype), kind="ExternalInput").ap())
    args.append(nc.dram_tensor("out_0", (1, S, D), F32, kind="ExternalOutput").ap())
    hybrid(nc, *args)
    r = _run(nc, [arrays], core_ids=[0])
    return r.results[0]["out_0"]
```

```python
from contextlib import ExitStack

import concourse.bass as bass
from concourse import mybir

ALU = mybir.AluOpType
ACT = mybir.ActivationFunctionType
AX_X = mybir.AxisListType.X
F32 = mybir.dt.float32
FR = mybir.dt.float32r

P = 128
S = 1024
D = 1024
KD = D // P
HALF = 512
SB = S // P
PLE = 256
KP = PLE // P
EPS = 1e-6
KB = 1024

RG_W, FOX_W, ML_W = 512, 512, 512
FOX_H, FOX_D = 8, 64
ML_H = 4
CH = 128
NC = S // CH
CV = 130
RG_C = 8.0
NEG = -3.0e38

C_RX, C_RG = 0, 512
C_FQ, C_FK, C_FV, C_FF, C_FG = 1024, 1536, 2048, 2560, 2568
C_MQ, C_MK, C_MV, C_MI, C_MF, C_MO, C_MG = 3080, 3592, 4104, 4616, 4620, 4624, 5136

UNIT = {
    None: [],
    "F": [(C_FQ, 0), (C_FK, 1), (C_FV, 0), (C_FG, 1)],
    "M": [(C_MQ, 0), (C_MK, 1), (C_MV, 2), (C_MO, 0), (C_MG, 1)],
    "R": [(C_RX, 0), (C_RG, 1)],
}
TURNS = 4
FIRST = {None: 0, "F": 1, "M": 1 + 4 * 4, "R": 1 + 4 * 4 + 4 * 5}
BEFORE = {"F": 0, "M": 4, "R": 8}
FOX_ROW = RG_W // P


def spread(total, weights):
    return [total * sum(weights[:n + 1]) // sum(weights) for n in range(len(weights))]


FOX_WEIGHTS = [1, 1, 1, 1, 3, 3, 3, 3] * 2
FOX_EARLY = [1, 1, 2, 2]
FOX_LEAD = 32
PARAMS = 13
FA, FD = 13, 8
MA, MD = 16, 21
RA, RD = 9, 11


def ngroups(t):
    return sum(i % SB // 4 + 1 for i in range(t))


def uses(kind, turn, b):
    slot = UNIT[kind][b][1]
    n = 0
    for k in "FMR":
        mine = sum(1 for _, s in UNIT[k] if s == slot)
        if k == kind:
            return n + mine * turn + sum(1 for _, s in UNIT[k][:b + 1] if s == slot)
        n += mine * TURNS


def hybrid(nc, x, p, norm_g, w_in, conv_w, conv_b, wa, ba, wx, bx, lam, fox_b_f, q_g, k_g, ml_b_i, ml_b_f,
           w_out, ple_g, w_gate, w_ple, out):
    ctx = ExitStack()
    with ctx:
        BASE = 16512
        top = nc.sbuf_usable_end
        arena = ctx.enter_context(nc.sbuf_tensor("arena", [P, (top - BASE - 96) // 4], F32))

        def at(name, shape, dt, off):
            size = 4
            for n in shape[1:]:
                size *= n
            assert BASE + off + size <= top, (name, off, size)
            return nc.alloc_sbuf_tensor_at(name, shape, dt, offset=BASE + off)

        def sem(name):
            return ctx.enter_context(nc.semaphore(name))

        uh = at("uh", [P, KD, S], FR, 0)
        ul = at("ul", [P, KD, S], FR, 32 * KB)
        W0 = 64 * KB
        wraw = [at(f"wraw{i}", [P, KD, P], F32, W0 + 4 * KB * i) for i in range(3)]
        wh = [at(f"wh{i}", [P, KD, P], FR, W0 + 4 * KB * (3 + i)) for i in range(3)]
        wl = [at(f"wl{i}", [P, KD, P], FR, W0 + 4 * KB * (6 + i)) for i in range(3)]
        Y = 100 * KB
        yt = at("yt", [P, 12, S], F32, Y)
        Y1, Y2, Y0 = Y, Y + 16 * KB, Y + 32 * KB
        C = Y + 48 * KB
        ident = at("ident", [P, P], F32, C)
        identr = at("identr", [P, P], FR, C + 512)
        maskf = at("maskf", [P, P], F32, C + 1024)
        maskr = at("maskr", [P, P], FR, C + 1536)
        headmean = at("headmean", [P, P], F32, C + 2048)
        prm = at("prm", [P, 96], F32, C + 2560)
        gcol = at("gcol", [96, 2], F32, C + 2560 + 384)
        cols = at("cols", [P, NC, 4, 4], F32, C + 3072)
        tri = at("tri", [P, P], F32, C + 3584)
        SC = C + 4096
        zst = [at(f"zst{i}", [P, S], F32, SC + 4 * KB * i) for i in range(5)]
        S1 = SC + 20 * KB

        xt = at("xt", [P, SB, D], F32, Y)
        junk = at("junk", [P, 2, D], F32, S1 + 8 * KB)
        wgraw = at("wgraw", [P, KD, 16], F32, S1)
        wgh = at("wgh", [P, KD, 96], FR, S1 + 1 * KB)
        wgl = at("wgl", [P, KD, 96], FR, S1 + 4 * KB)
        xb = at("xb", [P, S], F32, Y1)
        ex = at("ex", [P, S], F32, Y1 + 4 * KB)
        lf = at("lf", [P, S], F32, Y1 + 8 * KB)
        nb = at("nb", [P, S], F32, Y1 + 12 * KB)
        ar = at("ar", [P, S], F32, Y2)
        gr = at("gr", [P, S], F32, Y2 + 4 * KB)
        rw = at("rw", [P, S], F32, Y2 + 8 * KB)
        dl = at("dl", [P, S], F32, Y2 + 12 * KB)
        rm = at("rm", [P, S], F32, S1 + 24 * KB)
        crow = at("crow", [64, S], FR, S1 + 8 * KB)
        mc = at("mc", [P, NC], F32, S1 + 32 * KB)
        vhl = at("vhl", [P, SB, 2, P], FR, Y0)
        qb = [at(f"qb{i}", [P, S], FR, Y0 + (8 + 4 * i) * KB) for i in range(2)]
        pr = [at(f"pr{i}", [P, S], F32, Y2 + 4 * KB * i) for i in range(2)]
        og = at("og", [P, S], F32, Y2 + 8 * KB)
        ot = at("ot", [P, S], F32, Y2 + 12 * KB)
        qs = [at(f"qs{i}", [P, S], FR, S1 + 4 * KB * i) for i in range(2)]
        ka = [at(f"ka{i}", [P, S], FR, S1 + 4 * KB * (2 + i)) for i in range(2)]
        kb = [at(f"kb{i}", [P, S], FR, S1 + 4 * KB * (4 + i)) for i in range(2)]
        pt = at("pt", [P, SB, 2 * P], FR, S1 + 24 * KB)
        rq = [at(f"rq{i}", [P, S], F32, S1 + (24 + 4 * i) * KB) for i in range(2)]
        SM = S1 + 32 * KB
        oc = at("oc", [P, 2 * P], F32, SM + 64 + 1024)
        sm = at("sm", [P, 16], F32, SM + 64 + 2048)
        qth, qtl, kth, ktl = [at(n, [P, S], FR, S1 + 4 * KB * i) for i, n in enumerate(("qth", "qtl", "kth", "ktl"))]
        vh2 = at("vh2", [P, NC, CV], FR, S1 + 16 * KB)
        vl2 = at("vl2", [P, NC, CV], FR, S1 + 20 * KB + 128)
        eg = at("eg", [P, NC, CH], F32, S1 + 24 * KB + 256)
        hn = at("hn", [P, NC, CV], F32, S1 + 24 * KB + 256)
        kwh = at("kwh", [P, NC, P], FR, S1 + 28 * KB + 512)
        ucol = at("ucol", [P, NC, 4], F32, S1 + 35 * KB)
        dec = at("dec", [P, NC], F32, S1 + 35 * KB + 128)
        den = at("den", [P, NC], F32, S1 + 35 * KB + 192)
        kwl = at("kwl", [P, NC, P], FR, Y0)
        sch = at("sch", [P, S], FR, Y0 + 4 * KB)
        scl = at("scl", [P, S], FR, Y0 + 8 * KB)
        cf = at("cf", [P, CV], F32, Y0 + 12 * KB)
        chi = [at(f"chi{i}", [P, CV], FR, Y0 + 12 * KB + 544 * (1 + i)) for i in range(2)]
        clo = [at(f"clo{i}", [P, CV], FR, Y0 + 12 * KB + 544 * (3 + i)) for i in range(2)]
        ti2 = [at(f"ti{i}", [P, CV], F32, Y0 + 12 * KB + 544 * (5 + i)) for i in range(2)]
        xc, tr, ti, tt, l1, l2, tg = [at(n, [P, S], F32, S1 + 4 * KB * i) for i, n in
                                      enumerate(("xc", "tr", "ti", "tt", "l1", "l2", "tg"))]
        wad = at("wad", [P, 2, P], F32, S1 + 28 * KB)
        rcol = at("rcol", [P, 8], F32, S1 + 35 * KB + 256)
        wo = at("wo", [P, 12, 2, D], FR, 0)
        raw = zst[2:4]
        ysh = [at("ysh0", [P, HALF], FR, 96 * KB), at("ysh1", [P, HALF], FR, SC)]
        ysl = [at("ysl0", [P, HALF], FR, 98 * KB), at("ysl1", [P, HALF], FR, SC + 2 * KB)]
        ht = at("ht", [P, SB, D], F32, S1)
        junk2 = at("junk2", [P, D], F32, Y)
        hth = [at(f"hth{i}", [P, KD, P], FR, Y + (8 + 4 * i) * KB) for i in range(2)]
        htl = [at(f"htl{i}", [P, KD, P], FR, Y + (16 + 4 * i) * KB) for i in range(2)]
        th = [at(f"th{i}", [P, D], F32, Y + (24 + 4 * i) * KB) for i in range(2)]
        praw = at("praw", [P, SB, PLE], F32, Y + 32 * KB)
        pth = [at(f"pth{i}", [P, KP, P], FR, Y + (40 + i) * KB) for i in range(2)]
        ptl = [at(f"ptl{i}", [P, KP, P], FR, Y + (42 + i) * KB) for i in range(2)]
        pcol = at("pcol", [P, 2], F32, C + 2560 + 448)
        hr = at("hr", [P, 4], F32, C + 2560 + 480)
        tick = at("tick", [P, 4], F32, C + 2560 + 416)

        ps = [ctx.enter_context(nc.psum_tensor(f"ps{i}", [P, 2 * HALF], F32)) for i in range(4)]
        pz = [ps[0][:, 0:HALF], ps[0][:, HALF:]]
        p_s = [ps[1], ps[2]]
        p_t, p_o = ps[3][:, 0:HALF], ps[3][:, HALF:]

        c_dram = nc.dram_tensor("c_scratch", [FOX_H, 2, S], F32).ap()
        g_dram = nc.dram_tensor("g_scratch", [ML_H, S], F32).ap()
        wl_dram = nc.dram_tensor("wl_scratch", [ML_H, NC], F32).ap()
        w_cols = w_in.rearrange("l (k p) n -> (l p) k n", p=P)

        s_par, s_gb0, s_gb = sem("params_loaded"), sem("gate_bias_cleared"), sem("gate_bias_loaded")
        s_x = [sem(f"x_loaded{i}") for i in range(SB)]
        s_ng = sem("norm_weights_loaded")
        s_id0, s_id = sem("consts_cleared"), sem("consts_ready")
        s_cc = sem("const_casts_ready")
        s_ssq, s_ln, s_rstd, s_xn = sem("sumsq_ready"), sem("rstd_ln"), sem("rstd_ready"), sem("x_scaled")
        s_xT, s_uh, s_ul = sem("xT_ready"), sem("uh_ready"), sem("ul_ready")
        s_wd = [sem(f"w_loaded{i}") for i in range(3)]
        s_wgd, s_wgz, s_wgh, s_wg = (sem("wg_loaded"), sem("wg_cleared"), sem("wg_hi_ready"), sem("wg_ready"))
        s_wh, s_ws = sem("w_hi_ready"), sem("w_split")
        s_z, s_ze = sem("z_half_done"), sem("z_half_saved")
        s_ga, s_gd, s_gm = sem("gate_act"), sem("gate_dve"), sem("gate_memsets")
        s_hm, s_gv = sem("head_mean_ready"), sem("gate_rows_cleared")
        s_gt, s_gc = sem("gate_cols_transposed"), sem("gate_cols_ready")
        s_gw = sem("gate_rows_saved")
        s_pc, s_lam, s_lam0 = sem("param_steps"), sem("lambda_steps"), sem("lambda_abs")
        s_fa, s_fd = sem("fox_prep_act"), sem("fox_prep_dve")
        s_ms, s_vt = sem("fox_meansq"), sem("fox_v_transposed")
        s_on, s_ck = sem("fox_ones_ready"), sem("fox_c_loaded")
        s_vh, s_vl = sem("fox_v_hi"), sem("fox_v_lo")
        s_og = sem("fox_gate_ready")
        s_sc, s_nm, s_mx, s_ex = sem("scores_ready"), sem("negmax_ready"), sem("max_ready"), sem("probs_ready")
        s_rc, s_pn = sem("recip_ready"), sem("probs_scaled")
        s_pt, s_ph, s_pl = sem("probsT_ready"), sem("probsT_hi"), sem("probsT_lo")
        s_pv, s_oc, s_oa, s_ot = sem("pv_done"), sem("pv_copied"), sem("pv_added"), sem("o_ready")
        s_unit = sem("unit_finished")
        s_ma, s_md, s_mg = sem("ml_act"), sem("ml_dve"), sem("ml_rows_loaded")
        s_mone = sem("ml_ones_ready")
        s_mkt, s_mvt, s_mst = sem("ml_kT"), sem("ml_vT"), sem("ml_scoresT")
        s_mu, s_mx2, s_mi = sem("ml_update"), sem("ml_intra"), sem("ml_inter")
        s_mc, s_mch, s_mcl, s_mt, s_mh = (sem("ml_state"), sem("ml_state_hi"), sem("ml_state_lo"),
                                          sem("ml_inter_scaled"), sem("ml_h"))
        s_mht = sem("ml_hT")
        s_ra, s_rd, s_rg, s_rw = sem("rg_act"), sem("rg_dve"), sem("rg_gates"), sem("rg_weights_loaded")
        s_rz = sem("rg_weights_cleared")
        s_oh, s_ow = sem("wo_hi"), sem("wo_split")
        s_od = [sem(f"wo_loaded{i}") for i in range(3)]
        s_yh, s_yl, s_om = sem("y_hi"), sem("y_lo"), sem("out_row_block_multiplied")
        s_hx, s_h, s_pp = sem("h_x_loaded"), sem("h_ready"), sem("p_loaded")
        s_pg, s_ob, s_hr = sem("ple_norm_column"), sem("out_block_done"), sem("h_eps_ready")
        s_q1, s_q2, s_q3 = sem("h_sumsq"), sem("h_ln"), sem("h_rstd")
        s_qt, s_qh, s_ql = sem("hT_ready"), sem("hT_hi"), sem("hT_lo")
        s_gt2, s_th, s_t1, s_fin = sem("gate_ready"), sem("tanh_ready"), sem("gated"), sem("final_ready")
        s_out = sem("out_saved")

        block = ctx.enter_context(nc.Block())

        def blocks(kind, turn):
            n = len(UNIT[kind])
            return [(FIRST[kind] + n * turn + b, slot, c0 + P * turn) for b, (c0, slot) in enumerate(UNIT[kind])]

        @block.sync
        def _(sp):
            for i in range(SB):
                sp.dma_start(xt[:, i, :], x[0, i * P:(i + 1) * P, :]).then_inc(s_x[i], 16)
                if i == 3:
                    with nc.allow_non_contiguous_dma(reason="small parameter columns"):
                        sp.dma_start(prm[:, 0:8], norm_g.rearrange("l (k p) -> (l p) k", p=P)).then_inc(s_ng, 16)
            with nc.allow_non_contiguous_dma(reason="small parameter columns"):
                def col(c, n, src):
                    sp.dma_start(prm[:, c:c + n], src.rearrange("l (k p) -> (l p) k", p=P)).then_inc(s_par, 16)
                sp.dma_start(wgraw[:, :, 0:8], w_cols[:, :, C_FF:C_FF + 8]).then_inc(s_wgd, 16)
                sp.dma_start(wgraw[:, :, 8:16], w_cols[:, :, C_MI:C_MI + 8]).then_inc(s_wgd, 16)
                sp.wait_ge(s_gb0, 1)
                sp.dma_start(gcol[0:8, 0:1], fox_b_f.rearrange("l d -> d l")).then_inc(s_gb, 16)
                sp.dma_start(gcol[64:68, 0:1], ml_b_f.rearrange("l d -> d l")).then_inc(s_gb, 16)
                sp.dma_start(gcol[64:68, 1:2], ml_b_i.rearrange("l d -> d l")).then_inc(s_gb, 16)
                for j in range(4):
                    col(16 + 4 * j, 4, conv_w[:, j, :])
                col(32, 4, conv_b)
                col(36, 4, ba)
                col(40, 4, bx)
                col(44, 4, lam)
                col(8, 8, ple_g)
                for h in range(2):
                    sp.dma_start(prm[64 * h:64 * h + 64, 48:49], q_g.rearrange("l d -> d l")).then_inc(s_par, 16)
                    sp.dma_start(prm[64 * h:64 * h + 64, 49:50], k_g.rearrange("l d -> d l")).then_inc(s_par, 16)

            def load_blocks(kind, turn):
                for b, (B, slot, col) in enumerate(blocks(kind, turn)):
                    if not (isinstance(B, int) and B < 3):
                        sp.wait_ge(s_ws, B - 2)
                    sp.dma_start(wraw[slot][:, :, :], w_cols[:, :, bass.ds(col, P)]).then_inc(s_wd[slot], 16)

            for kind in "FMR":
                load_blocks(kind, 0)
                with sp.Fori(1, TURNS) as turn:
                    load_blocks(kind, turn)
            def load_rows(src, n):
                for b in range(2):
                    if not isinstance(n, int) or n:
                        sp.wait_ge(s_ow, 2 * n + b - 1)
                    sp.dma_start(raw[b][:, :], src(b)).then_inc(s_od[b], 16)

            sp.wait_ge(s_unit, 9)
            load_rows(lambda b: w_out[0, (FOX_ROW + b) * P:(FOX_ROW + b + 1) * P, :], 0)
            with sp.Fori(1, 4) as n:
                load_rows(lambda b: w_out[0, bass.ds((2 * n + (FOX_ROW + b)) * P, P), :], n)
            with sp.Fori(4, 6) as n:
                load_rows(lambda b: w_out[0, bass.ds((2 * n - (8 - b)) * P, P), :], n)
            sp.wait_ge(s_unit, 13)
            for i in range(SB):
                sp.dma_start(ht[:, i, :], x[0, i * P:(i + 1) * P, :]).then_inc(s_hx, 16)
            with sp.Fori(6, 10) as n:
                load_rows(lambda b: w_gate[0, bass.ds((2 * n - (12 - b)) * P, P), :], n)
            load_rows(lambda b: w_ple[0, b * P:(b + 1) * P, :], 10)
            sp.wait_ge(s_yl, 24)
            sp.wait_ge(s_yh, 24)
            sp.dma_start(praw[:, :, :], p[0, 0].rearrange("(i q) c -> q i c", q=P)).then_inc(s_pp, 16)
            with sp.Fori(0, SB) as i:
                sp.wait_ge(s_fin, i + 1)
                sp.dma_start(out[0, bass.ds(i * P, P), :], ht[:, bass.ds(i, 1), :].rearrange("p o d -> p (o d)"))\
                    .then_inc(s_out, 16)
            sp.wait_ge(s_out, 16 * SB)

        @block.gpsimd
        def _(g):
            g.memset(gcol[:, :], 0.0).then_inc(s_gb0, 1)
            g.memset(ident[:, :], 0.0).then_inc(s_id0, 1)
            g.memset(maskf[:, :], 0.0).then_inc(s_id0, 1)
            g.memset(tri[:, :], 1.0).then_inc(s_id0, 1)
            g.memset(prm[:, 52:53], EPS)
            g.memset(tick[:, :], 0.0)
            g.memset(prm[:, 53:54], 1.0)
            g.wait_ge(s_id0, 3)
            g.affine_select(out=ident[:, :], in_=ident[:, :], compare_op=ALU.not_equal, fill=1.0, base=0,
                            pattern=[[-1, P]], channel_multiplier=1).then_inc(s_id, 1)
            g.affine_select(out=maskf[:, :], in_=maskf[:, :], compare_op=ALU.is_ge, fill=NEG, base=0,
                            pattern=[[-1, P]], channel_multiplier=1).then_inc(s_id, 1)
            g.affine_select(out=tri[:, :], in_=tri[:, :], compare_op=ALU.is_ge, fill=0.0, base=0,
                            pattern=[[1, P]], channel_multiplier=-1).then_inc(s_id, 1)
            g.memset(wgh[:, :, :].bitcast(F32), 0.0).then_inc(s_wgz, 1)
            g.memset(wgl[:, :, :].bitcast(F32), 0.0).then_inc(s_wgz, 1)
            g.wait_ge(s_wgd, 32)
            g.wait_ge(s_wgz, 2)
            parts = [(0, 0, 8), (32, 8, 4), (64, 12, 4)]
            for to, frm, n in parts:
                last = g.tensor_copy(wgh[:, :, to:to + n], wgraw[:, :, frm:frm + n])
            last.then_inc(s_wgh, 1)
            g.wait_ge(s_wgh, 1)
            for to, frm, n in parts:
                last = g.tensor_tensor(wgl[:, :, to:to + n], wgraw[:, :, frm:frm + n], wgh[:, :, to:to + n],
                                       ALU.subtract)
            last.then_inc(s_wg, 1)
            def clear_rows():
                g.wait_ge(s_xT, 16)
                g.memset(rw[:, :], 0.0).then_inc(s_gm, 1)
                for h in range(2):
                    g.memset(qb[h][:, :].bitcast(F32), 0.0).then_inc(s_gm, 1)
                    g.memset(kb[h][:, :].bitcast(F32), 0.0).then_inc(s_gm, 1)

            def split(kind, turn):
                for b, (B, slot, _) in enumerate(blocks(kind, turn)):
                    g.wait_ge(s_wd[slot], 16 * uses(kind, turn, b))
                    if not (isinstance(B, int) and B < 3):
                        g.wait_ge(s_z, 2 * (B - 1))
                    g.tensor_tensor(tick[:, 2:3], tick[:, 0:1], tick[:, 1:2], ALU.add)
                    g.tensor_copy(wh[slot][:, :, :], wraw[slot][:, :, :]).then_inc(s_wh, 1)
                    g.wait_ge(s_wh, B)
                    g.tensor_tensor(wl[slot][:, :, :], wraw[slot][:, :, :], wh[slot][:, :, :],
                                    ALU.subtract).then_inc(s_ws, 1)
                    if isinstance(B, int) and B == 2:
                        clear_rows()

            for kind in "FMR":
                split(kind, 0)
                with g.Fori(1, TURNS) as turn:
                    split(kind, turn)

        @block.tensor
        def _(pe):
            mm = nc.tensor.matmul

            def z_steps(kind, turn):
                for b, (B, slot, _) in enumerate(blocks(kind, turn)):
                    for half in range(2):
                        if half == 0:
                            pe.wait_ge(s_ws, B)
                        pe.wait_ge(s_ze, 2 * B + half - 1)
                        for k in range(KD):
                            cs = slice(half * HALF, (half + 1) * HALF)
                            mm(pz[half], wh[slot][:, k, :], uh[:, k, cs], start=(k == 0), stop=False)
                            mm(pz[half], wh[slot][:, k, :], ul[:, k, cs], start=False, stop=False)
                            last = mm(pz[half], wl[slot][:, k, :], uh[:, k, cs], start=False, stop=(k == KD - 1))
                            if k == KD - 1:
                                last.then_inc(s_z, 1)
                            yield

            def run(steps, n):
                for _ in range(n):
                    if next(steps, 0) == 0:
                        break

            pe.wait_ge(s_id, 2)
            for half in range(2):
                pe.wait_ge(s_xn, 4 * half + 4)
                for k in range(KD):
                    n = half * KD + k
                    if n >= 6:
                        pe.wait_ge(s_ul, n - 5)
                    bank = ps[1 + n % 6 // 2][:, n % 2 * HALF:(n % 2 + 1) * HALF]
                    for i in range(4):
                        last = nc.tensor.transpose(bank[:, i * P:(i + 1) * P],
                                                   xt[:, 4 * half + i, k * P:(k + 1) * P], ident[:, :])
                    last.then_inc(s_xT, 1)
                cs = slice(half * HALF, (half + 1) * HALF)
                pe.wait_ge(s_wg, 1)
                for k in range(KD):
                    pe.wait_ge(s_ul, half * KD + k + 1)
                    mm(pz[half][0:96], wgh[:, k, :], uh[:, k, cs], start=(k == 0), stop=False)
                    mm(pz[half][0:96], wgh[:, k, :], ul[:, k, cs], start=False, stop=False)
                    last = mm(pz[half][0:96], wgl[:, k, :], uh[:, k, cs], start=False, stop=(k == KD - 1))
                last.then_inc(s_z, 1)

            first = z_steps("F", 0)
            run(first, 48)
            pe.wait_ge(s_ga, 10)
            for half in range(2):
                bank = (p_t, p_o)[half]
                for c in range(4):
                    last = nc.tensor.transpose(bank[:, c * P:(c + 1) * P], rw[:, (4 * half + c) * CH:][:, 0:CH],
                                               ident[:, :])
                last.then_inc(s_gt, 1)
            run(first, 64)

            def fox(a, kind, turn):
                steps = z_steps(kind, turn)
                total = 16 * len(UNIT[kind])
                run(steps, 6)
                pe.wait_ge(s_unit, a + 1)
                pe.wait_ge(s_gc, 2)
                pe.wait_ge(s_ze, 2 * (FIRST["F"] + 4 * a + 2) + 2)
                for half in range(2):
                    bank = (p_t, p_o)[half]
                    for i in range(4):
                        last = nc.tensor.transpose(bank[:, i * P:(i + 1) * P],
                                                   zst[2][:, (4 * half + i) * P:][:, 0:P], ident[:, :])
                    last.then_inc(s_vt, 1)
                pe.wait_ge(s_hm, 3)
                for n in range(2):
                    pe.wait_ge(s_fa, FA * a + 1 + n)
                    for half in range(2):
                        cs = slice(half * HALF, (half + 1) * HALF)
                        last = mm(p_s[n][:, cs], headmean[:, :], pr[n][:, cs], start=True, stop=True)
                    last.then_inc(s_ms, 1)
                    run(steps, 3)
                run(steps, min(FOX_LEAD, total) - 12)

                def scores(t):
                    h, i = t // SB, t % SB
                    n = (i + 1) * P
                    if t == 0:
                        pe.wait_ge(s_on, 2)
                        pe.wait_ge(s_fa, FA * a + 13)
                        pe.wait_ge(s_fd, FD * a + 8)
                        pe.wait_ge(s_ck, 32 * (a + 1))
                    if t >= 2:
                        pe.wait_ge(s_ex, 16 * a + t - 1)
                    bank = p_s[t % 2]
                    for c0 in range(0, n, HALF):
                        c1 = min(c0 + HALF, n)
                        o = bank[:, c0:c1]
                        diag = c1 == n
                        mm(o, qs[h][:, i * P:(i + 1) * P], ka[h][:, c0:c1], start=True, stop=False)
                        if diag:
                            mm(bank[:, n - P:n], identr[:, :], maskr[:, :], start=False, stop=False)
                        last = mm(o, qb[h][:, i * P:(i + 1) * P], kb[h][:, c0:c1], start=False, stop=True)
                    last.then_inc(s_sc, 1)

                upto = spread(total - min(FOX_LEAD, total), FOX_WEIGHTS)
                scores(0)
                scores(1)
                for t in range(16):
                    h, i = t // SB, t % SB
                    groups = i // 4 + 1
                    todo, early = upto[t] - (upto[t - 1] if t else 0), 0
                    pe.wait_ge(s_pn, 16 * a + t + 1)
                    for g in range(groups):
                        n_g = 24 * a + 12 * h + max(0, i - 4) * 2 + min(i, 4) + g
                        if t == 0 and g == 0:
                            pe.wait_ge(s_vl, 2 * a + 2)
                        else:
                            pe.wait_ge(s_pl, n_g)
                        for j in range(4 * g, min(4 * g + 4, i + 1)):
                            last = nc.tensor.transpose(p_t[:, (j % 4) * P:(j % 4 + 1) * P],
                                                       pr[t % 2][:, j * P:(j + 1) * P], ident[:, :])
                        last.then_inc(s_pt, 1)
                        if g == 0 and t + 2 < 16:
                            scores(t + 2)
                        if g == 0 and groups == 2:
                            early = min(todo, FOX_EARLY[i - 4])
                            run(steps, early)
                    run(steps, todo - early)
                    n_g += 1
                    pe.wait_ge(s_ph, n_g)
                    pe.wait_ge(s_pl, n_g)
                    if t:
                        pe.wait_ge(s_oa, 16 * a + t)
                    for j in range(i + 1):
                        last = mm(p_o[:, 0:2 * P], vhl[:, j, h, :], pt[:, j, :], start=(j == 0), stop=(j == i))
                    last.then_inc(s_pv, 1)
                run(steps, 100)

            def mlstm(m, kind, turn):
                steps = z_steps(kind, turn)
                total = 16 * len(UNIT[kind])
                done = min(24, total // 2)
                upto = spread(total - done, [1] * NC)
                run(steps, 4)
                pe.wait_ge(s_unit, 4 + m + 1)
                pe.wait_ge(s_md, MD * m + 1)
                for half in range(2):
                    for i in range(4 * half, 4 * half + 4):
                        last = nc.tensor.transpose(p_s[1][:, i * P:(i + 1) * P], zst[1][:, i * P:(i + 1) * P],
                                                   ident[:, :])
                last.then_inc(s_mkt, 1)
                run(steps, done // 3 - 4)
                for half in range(2):
                    bank = (p_t, p_o)[half]
                    for i in range(4):
                        last = nc.tensor.transpose(bank[:, i * P:(i + 1) * P],
                                                   zst[2][:, (4 * half + i) * P:][:, 0:P], ident[:, :])
                    last.then_inc(s_mvt, 1)
                run(steps, done // 3)
                pe.wait_ge(s_ma, MA * m + 2)
                pe.wait_ge(s_md, MD * m + 7)
                for c in range(NC):
                    o = p_s[0][:, c * CH:(c + 1) * CH]
                    cs = slice(c * CH, (c + 1) * CH)
                    mm(o, kth[:, cs], qth[:, cs], start=True, stop=False)
                    mm(o, kth[:, cs], qtl[:, cs], start=False, stop=False)
                    last = mm(o, ktl[:, cs], qth[:, cs], start=False, stop=True)
                    if c % 4 == 3:
                        last.then_inc(s_mst, 1)
                run(steps, done - 2 * (done // 3))
                for c in range(NC):
                    cs = slice(c * CH, (c + 1) * CH)
                    todo = upto[c] - (upto[c - 1] if c else 0)
                    if c == 0:
                        pe.wait_ge(s_md, MD * m + 11)
                        pe.wait_ge(s_ma, MA * m + 13)
                        pe.wait_ge(s_mone, 3)
                    elif c > 1:
                        pe.wait_ge(s_mc, (NC - 1) * m + c - 1)
                    if c < NC - 1:
                        o = p_s[1][:, (c % 2) * HALF:][:, 0:CV]
                        mm(o, kwh[:, c, :], vh2[:, c, :], start=True, stop=False)
                        mm(o, kwh[:, c, :], vl2[:, c, :], start=False, stop=False)
                        mm(o, kwl[:, c, :], vh2[:, c, :], start=False, stop=True).then_inc(s_mu, 1)
                    if c == 0:
                        pe.wait_ge(s_md, MD * m + 15)
                    elif c > 1:
                        pe.wait_ge(s_mh, NC * m + c - 1)
                    o = p_s[0][:, (c % 2) * HALF:][:, 0:CV]
                    mm(o, sch[:, cs], vh2[:, c, :], start=True, stop=False)
                    mm(o, sch[:, cs], vl2[:, c, :], start=False, stop=False)
                    mm(o, scl[:, cs], vh2[:, c, :], start=False, stop=True).then_inc(s_mx2, 1)
                    run(steps, todo // 2)
                    if c:
                        pe.wait_ge(s_mcl, (NC - 1) * m + c)
                        if c > 1:
                            pe.wait_ge(s_mt, NC * m + c - 1)
                    o = (p_t, p_o)[c % 2][:, 0:CV]
                    mm(o, qth[:, cs], chi[c % 2][:, :], start=True, stop=False)
                    mm(o, qth[:, cs], clo[c % 2][:, :], start=False, stop=False)
                    mm(o, qtl[:, cs], chi[c % 2][:, :], start=False, stop=True).then_inc(s_mi, 1)
                    run(steps, todo - todo // 2)
                pe.wait_ge(s_md, MD * m + 21)
                for i in range(NC):
                    last = nc.tensor.transpose(p_s[0][:, i * P:(i + 1) * P], hn[:, i, 0:P], ident[:, :])
                last.then_inc(s_mht, 1)
                run(steps, 100)

            def rglru(r, kind, turn):
                steps = z_steps(kind, turn)
                run(steps, 12)
                pe.wait_ge(s_unit, 8 + r + 1)
                pe.wait_ge(s_rw, 64 * (r + 1))
                pe.wait_ge(s_rd, RD * r + 4)
                for gate in range(2):
                    for half in range(2):
                        cs = slice(half * HALF, (half + 1) * HALF)
                        last = mm(p_s[gate][:, cs], wad[:, gate, :], xc[:, cs], start=True, stop=True)
                    last.then_inc(s_rg, 1)
                run(steps, 100)

            with pe.Fori(0, TURNS - 1) as a:
                fox(a, "F", a + 1)
            fox(TURNS - 1, "M", 0)
            with pe.Fori(0, TURNS - 1) as a:
                mlstm(a, "M", a + 1)
            mlstm(TURNS - 1, "R", 0)
            with pe.Fori(0, TURNS - 1) as a:
                rglru(a, "R", a + 1)
            rglru(TURNS - 1, None, 0)

            def row_block(grp, n, b):
                first, final = isinstance(n, int) and n == 0, isinstance(n, int) and n == 11
                if grp == 0:
                    pe.wait_ge(s_ow, n + 1)
                pe.wait_ge(s_yl, n + (12 * grp + 1))
                for i in range(4):
                    if first and grp == 0:
                        if i == 0:
                            pe.wait_ge(s_ze, 90)
                        if i == 1:
                            pe.wait_ge(s_ra, RA * (TURNS - 1) + 4)
                    if first and grp == 1:
                        pe.wait_ge(s_h, i + 1)
                    sl = slice(i * P, (i + 1) * P)
                    for dh in range(2):
                        cs = slice(dh * HALF, (dh + 1) * HALF)
                        o = ps[i][:, cs]
                        w_hi, w_lo = [wo[:, bass.ds(n, 1), j, cs].rearrange("p o d -> p (o d)") for j in range(2)]
                        mm(o, ysh[b][:, sl], w_hi, start=first, stop=False)
                        mm(o, ysh[b][:, sl], w_lo, start=False, stop=False)
                        last = mm(o, ysl[b][:, sl], w_hi, start=False, stop=final)
                    if final and i < 3:
                        last.then_inc(s_ob, 1)
                last.then_inc(s_om, 1)

            for grp in range(2):
                row_block(grp, 0, 0)
                row_block(grp, 1, 1)
                with pe.Fori(1, 5) as n:
                    row_block(grp, 2 * n, 0)
                    row_block(grp, 2 * n + 1, 1)
                row_block(grp, 10, 0)
                row_block(grp, 11, 1)

            def h_transposes(i):
                if i == 0:
                    pe.wait_ge(s_h, 6)
                    pe.wait_ge(s_pp, 16)
                else:
                    pe.wait_ge(s_ql, i)
                for k in range(KD):
                    nc.tensor.transpose(ps[1][:, k * P:(k + 1) * P], ht[:, i, k * P:(k + 1) * P], ident[:, :])
                for k in range(KP):
                    last = nc.tensor.transpose(ps[0][:, k * P:(k + 1) * P], praw[:, i, k * P:(k + 1) * P], ident[:, :])
                last.then_inc(s_qt, 1)

            def gated(i, b):
                if i == 0:
                    pe.wait_ge(s_ow, 22)
                    pe.wait_ge(s_h, 8)
                pe.wait_ge(s_ql, i + 1)
                for dst, hi, lo, k0, nk, free in ((ps[2], hth, htl, 0, KD, s_th), (ps[3], pth, ptl, KD, KP, s_t1)):
                    if i:
                        pe.wait_ge(free, i)
                    for half in range(2):
                        cs = slice(half * HALF, (half + 1) * HALF)
                        for k in range(nk):
                            mm(dst[:, cs], hi[b][:, k, :], wo[:, k0 + k, 0, cs], start=(k == 0), stop=False)
                            mm(dst[:, cs], hi[b][:, k, :], wo[:, k0 + k, 1, cs], start=False, stop=False)
                            last = mm(dst[:, cs], lo[b][:, k, :], wo[:, k0 + k, 0, cs], start=False,
                                      stop=(k == nk - 1))
                    last.then_inc(s_gt2, 1)

            h_transposes(0)
            for i in range(SB):
                if i < SB - 1:
                    h_transposes(i + 1)
                gated(i, i % 2)

        @block.scalar
        def _(act):
            af = nc.scalar.activation
            nc.scalar.preload_act_table_set("natural_log_exp_and_others")
            act.wait_ge(s_id, 1)
            hi_after = {4: (0, 2), 5: (2, 4), 6: (4, 6), 7: (6, 16)}
            for i in range(SB):
                r = prm[:, 80 + i:81 + i]
                act.wait_ge(s_x[i], 16)
                if i >= 2:
                    act.wait_ge(s_ssq, i - 1)
                af(junk[:, i % 2, :], xt[:, i, :], ACT.Square, accum_out=r).then_inc(s_ssq, 1)
                act.wait_ge(s_ssq, i + 1)
                af(r, r, ACT.Ln, bias=prm[:, 52:53], scale=1.0 / D).then_inc(s_ln, 1)
                act.wait_ge(s_ln, i + 1)
                af(r, r, ACT.Exp, scale=-0.5).then_inc(s_rstd, 1)
                if i == 4:
                    act.wait_ge(s_ng, 16)
                for n in range(*hi_after.get(i, (0, 0))):
                    half, k = n // KD, n % KD
                    act.wait_ge(s_xT, n + 1)
                    bank = ps[1 + n % 6 // 2][:, n % 2 * HALF:(n % 2 + 1) * HALF]
                    af(uh[:, k, half * HALF:(half + 1) * HALF], bank, ACT.Identity, scale=prm[:, k:k + 1])\
                        .then_inc(s_uh, 1)
            act.wait_ge(s_par, PARAMS * 16)
            act.wait_ge(s_id, 2)
            af(identr[:, :], ident[:, :], ACT.Copy).then_inc(s_cc, 1)
            af(maskr[:, :], maskf[:, :], ACT.Copy).then_inc(s_cc, 1)

            af(prm[:, 76:80], prm[:, 44:48], ACT.Abs).then_inc(s_lam0, 1)
            act.wait_ge(s_lam0, 1)
            af(prm[:, 56:60], prm[:, 76:80], ACT.Exp, scale=-1.0).then_inc(s_lam, 1)
            act.wait_ge(s_pc, 3)
            af(prm[:, 64:68], prm[:, 60:64], ACT.Ln).then_inc(s_lam, 1)

            act.wait_ge(s_gb, 48)
            act.wait_ge(s_xT, 16)
            for half in range(2):
                cs = slice(half * HALF, (half + 1) * HALF)
                act.wait_ge(s_z, half + 1)
                af(xb[0:96, cs], pz[half][0:96], ACT.Identity, bias=gcol[:, 0:1]).then_inc(s_ga, 1)
                af(ar[64:68, cs], pz[half][32:36], ACT.Copy).then_inc(s_ze, 1)
            act.wait_ge(s_ga, 2)
            af(ex[0:96, :], xb[0:96, :], ACT.Abs).then_inc(s_ga, 1)
            act.wait_ge(s_ga, 3)
            af(ex[0:96, :], ex[0:96, :], ACT.Exp, scale=-1.0).then_inc(s_ga, 1)
            act.wait_ge(s_ga, 4)
            af(ex[0:96, :], ex[0:96, :], ACT.Ln, bias=prm[0:96, 53:54]).then_inc(s_ga, 1)

            def save(kind, turn, upto, state, frees=None):
                while state[0] < upto // 8:
                    n = state[0]
                    b, half = n // 2, n % 2
                    B = FIRST[kind] + len(UNIT[kind]) * turn + b
                    act.wait_ge(s_z, 2 * B + half + 1)
                    if half == 0 and frees:
                        act.wait_ge(*frees[b])
                    af(zst[b][:, half * HALF:(half + 1) * HALF], pz[half], ACT.Copy).then_inc(s_ze, 1)
                    state[0] += 1

            st = [0]
            save("F", 0, 32, st)
            act.wait_ge(s_gm, 1)
            act.wait_ge(s_gd, 3)
            af(rw[0:4, :], ar[64:68, :], ACT.Copy).then_inc(s_ga, 1)
            act.wait_ge(s_gd, 2)
            af(crow[0:8, :], nb[0:8, :], ACT.Copy).then_inc(s_ga, 1)
            act.wait_ge(s_gd, 7)
            af(rw[64:68, :], ex[64:68, :], ACT.Exp).then_inc(s_ga, 1)
            act.wait_ge(s_gd, 8)
            af(rw[96:100, :], xb[64:68, :], ACT.Exp).then_inc(s_ga, 1)
            act.wait_ge(s_gd, 9)
            af(rw[32:36, :], lf[64:68, :], ACT.Exp).then_inc(s_ga, 1)
            act.wait_ge(s_ga, 8)
            with nc.allow_non_contiguous_dma(reason="last token of each chunk"):
                act.dma_start(g_dram, gr[64:68, :]).then_inc(s_gw, 16)
                act.dma_start(wl_dram, rw[64:68, :].rearrange("p (c t) -> p c t", t=CH)[:, :, CH - 1])\
                    .then_inc(s_gw, 16)
            for half in range(2):
                act.wait_ge(s_gt, half + 1)
                af(cols[:, 4 * half:4 * half + 4, :, :],
                   (p_t, p_o)[half].rearrange("p (c q r) -> p c q r", c=4, q=4)[:, :, :, 0:4], ACT.Copy)\
                    .then_inc(s_gc, 1)
            act.wait_ge(s_unit, 1)
            act.dma_start(c_dram[:, 0, :], crow[0:8, :].bitcast(F32)).then_inc(s_gw, 16)
            act.dma_start(c_dram[:, 1, :], crow[32:40, :].bitcast(F32)).then_inc(s_gw, 16)
            save("F", 0, 64, st)

            def fox(a, kind, turn):
                state = [0]
                total = 16 * len(UNIT[kind])
                frees = [(s_fd, FD * a + 1), (s_fd, FD * a + 2), (s_vt, 2 * a + 2), (s_og, a + 1), (s_ga, 1)]
                act.wait_ge(s_unit, a + 1)
                act.wait_ge(s_gc, 2)
                act.wait_ge(s_gw, 64)
                act.wait_ge(s_gm, 5)
                for h, row in enumerate((64, 0)):
                    act.dma_start(kb[h][row:row + 2, :].bitcast(F32), c_dram[bass.ds(2 * a + h, 1), :, :]
                                  .rearrange("o r s -> (o r) s")).then_inc(s_ck, 16)
                for n in range(2):
                    act.wait_ge(s_ze, 2 * (FIRST["F"] + 4 * a + n) + 2)
                    af(pr[n][:, :], zst[n][:, :], ACT.Square).then_inc(s_fa, 1)
                act.wait_ge(s_ze, 2 * (FIRST["F"] + 4 * a + 3) + 2)
                af(og[:, :], zst[3][:, :], ACT.Tanh, scale=0.5).then_inc(s_fa, 1)
                for half in range(2):
                    act.wait_ge(s_vt, 2 * a + half + 1)
                    src = (p_t, p_o)[half].rearrange("p (i h d) -> p i h d", i=4, h=2)
                    af(vhl[:, 4 * half:4 * half + 4, 0, 0:64], src[:, :, 0, :], ACT.Copy)
                    af(vhl[:, 4 * half:4 * half + 4, 1, 64:128], src[:, :, 1, :], ACT.Copy).then_inc(s_vh, 1)
                nc.scalar.preload_act_table_set("natural_log_exp_and_others")
                for n in range(2):
                    act.wait_ge(s_ms, 2 * a + n + 1)
                    af(rq[n][:, :], p_s[n][:, :], ACT.Ln, bias=prm[:, 52:53]).then_inc(s_fa, 1)
                for n in range(2):
                    act.wait_ge(s_fa, FA * a + 4 + n)
                    af(rq[n][:, :], rq[n][:, :], ACT.Exp, scale=-0.5).then_inc(s_fa, 1)
                act.wait_ge(s_fd, FD * a + 1)
                save(kind, turn, min(8, total), state, frees)
                af(qs[0][0:64, :], rq[0][0:64, :], ACT.Copy).then_inc(s_fa, 1)
                af(qs[1][64:128, :], rq[0][64:128, :], ACT.Copy).then_inc(s_fa, 1)
                act.wait_ge(s_fd, FD * a + 2)
                af(ka[0][0:64, :], rq[1][0:64, :], ACT.Copy).then_inc(s_fa, 1)
                save(kind, turn, min(16, total), state, frees)
                af(ka[1][64:128, :], rq[1][64:128, :], ACT.Copy).then_inc(s_fa, 1)
                af(ka[0][64:128, :], rq[1][0:64, :], ACT.Copy).then_inc(s_fa, 1)
                af(ka[1][0:64, :], rq[1][64:128, :], ACT.Copy).then_inc(s_fa, 1)
                save(kind, turn, min(FOX_LEAD, total), state, frees)
                done = min(FOX_LEAD, total)
                upto = spread(total - done, FOX_WEIGHTS)

                def probs(t):
                    h, i = t // SB, t % SB
                    n = (i + 1) * P
                    act.wait_ge(s_nm, 16 * a + t + 1)
                    if t >= 2:
                        act.wait_ge(s_pt, 24 * a + ngroups(t - 1))
                    af(pr[t % 2][:, 0:n], p_s[t % 2][:, 0:n], ACT.Exp, bias=sm[:, t % 2:t % 2 + 1],
                       accum_out=sm[:, 2 + t % 2:3 + t % 2]).then_inc(s_ex, 1)

                probs(0)
                for t in range(16):
                    h, i = t // SB, t % SB
                    for g in range(i // 4 + 1):
                        n_g = 24 * a + ngroups(t) + g
                        act.wait_ge(s_pt, n_g + 1)
                        if g == 0 and t:
                            act.wait_ge(s_pv, 16 * a + t)
                        j0, j1 = 4 * g, min(4 * g + 4, i + 1)
                        af(pt[:, j0:j1, 0:P], p_t[:, 0:(j1 - j0) * P].rearrange("p (j q) -> p j q", q=P), ACT.Copy)\
                            .then_inc(s_ph, 1)
                        if g == 0 and t < 15:
                            probs(t + 1)
                    act.wait_ge(s_pv, 16 * a + t + 1)
                    if t:
                        act.wait_ge(s_ot, 16 * a + t)
                    hi, lo = (slice(0, 64), slice(64, 128)) if h == 0 else (slice(64, 128), slice(0, 64))
                    af(oc[hi, :], p_o[lo, 0:2 * P], ACT.Copy).then_inc(s_oc, 1)
                    save(kind, turn, done + upto[t], state, frees)

            def mlstm(m, kind, turn):
                state = [0]
                total = 16 * len(UNIT[kind])
                done = min(24, total // 2)
                upto = spread(total - done, [1] * NC)
                frees = [(s_md, MD * m + 6), (s_md, MD * m + 11), (s_mvt, 2 * m + 2), (s_md, MD * m + 17),
                         (s_md, MD * m + 17)]
                B0 = FIRST["M"] + 5 * m
                act.wait_ge(s_unit, 4 + m + 1)
                act.dma_start(eg[:, :, :].rearrange("p c t -> p (c t)"),
                              g_dram[bass.ds(m, 1), :].broadcast_to([P, S])).then_inc(s_mg, 16)
                act.dma_start(dec[:, :], wl_dram[bass.ds(m, 1), :].broadcast_to([P, NC])).then_inc(s_mg, 16)
                act.wait_ge(s_ze, 2 * B0 + 2)
                af(qth[:, :], zst[0][:, :], ACT.Copy).then_inc(s_ma, 1)
                act.wait_ge(s_md, MD * m + 1)
                af(kth[:, :], zst[1][:, :], ACT.Copy).then_inc(s_ma, 1)
                for half in range(2):
                    act.wait_ge(s_mvt, 2 * m + half + 1)
                    af(vh2[:, 4 * half:4 * half + 4, 0:P], (p_t, p_o)[half].rearrange("p (c e) -> p c e", e=P),
                       ACT.Copy).then_inc(s_ma, 1)
                save(kind, turn, min(8, total), state, frees)
                act.wait_ge(s_mg, 32 * (m + 1))
                act.wait_ge(s_md, MD * m + 2)
                for c in range(NC):
                    af(eg[:, c, :], eg[:, c, :], ACT.Exp, bias=ucol[:, c, 0:1], scale=-1.0).then_inc(s_ma, 1)
                save(kind, turn, min(16, total), state, frees)
                act.wait_ge(s_md, MD * m + 10)
                af(kwh[:, :, :].rearrange("p c d -> p (c d)"), zst[1][:, :], ACT.Copy).then_inc(s_ma, 1)
                act.wait_ge(s_md, MD * m + 14)
                af(sch[:, :], eg[:, :, :].rearrange("p c t -> p (c t)"), ACT.Copy).then_inc(s_ma, 1)
                act.wait_ge(s_ze, 2 * (B0 + 4) + 2)
                af(zst[3][:, :], zst[3][:, :], ACT.Tanh, scale=0.5).then_inc(s_ma, 1)
                af(yt[:, bass.ds(4 + m, 1), :].rearrange("p o s -> p (o s)"), zst[4][:, :], ACT.Tanh, scale=0.5)\
                    .then_inc(s_ma, 1)
                save(kind, turn, done, state, frees)
                for c in range(NC):
                    if c < NC - 1:
                        act.wait_ge(s_mc, (NC - 1) * m + c + 1)
                        if c > 0:
                            act.wait_ge(s_mi, NC * m + c)
                        af(chi[(c + 1) % 2][:, :], cf[:, :], ACT.Copy).then_inc(s_mch, 1)
                    act.wait_ge(s_mi, NC * m + c + 1)
                    if c > 1:
                        act.wait_ge(s_mh, NC * m + c - 1)
                    af(ti2[c % 2][:, :], (p_t, p_o)[c % 2][:, 0:CV], ACT.Identity, scale=ucol[:, c, 2:3])\
                        .then_inc(s_mt, 1)
                    save(kind, turn, done + upto[c], state, frees)
                save(kind, turn, total, state, frees)

            def loads(n, b):
                return 8 * (n - b) + 16

            def rows(grp, n, b, weights=None):
                first = isinstance(n, int) and n == 0
                if grp == 0:
                    if first:
                        act.wait_ge(s_z, 90)
                        act.wait_ge(s_rd, RD * (TURNS - 1) + 4)
                    act.wait_ge(s_od[b], loads(n, b))
                    af(wo[:, bass.ds(n, 1), 0, :].rearrange("p o d -> p (o d)"), raw[b][:, :], ACT.Copy)\
                        .then_inc(s_oh, 1)
                if isinstance(n, int) and n == 11:
                    act.wait_ge(s_unit, 13)
                if not (isinstance(n, int) and n < 2) or grp:
                    act.wait_ge(s_om, n + (12 * grp - 1))
                af(ysh[b][:, :], yt[:, bass.ds(n, 1), grp * HALF:(grp + 1) * HALF].rearrange("p o s -> p (o s)"),
                   ACT.Copy).then_inc(s_yh, 1)
                if weights:
                    act.wait_ge(s_od[b], loads(n + 10, b))
                    to = wo[:, bass.ds(n - 2, 1), 0, :].rearrange("p o d -> p (o d)")
                    if weights == "gate":
                        act.wait_ge(s_pg, n - 1)
                        af(to, raw[b][:, :], ACT.Identity, scale=pcol[:, b:b + 1]).then_inc(s_oh, 1)
                    else:
                        af(to, raw[b][:, :], ACT.Copy).then_inc(s_oh, 1)

            def rglru(r, kind, turn):
                state = [0]
                total = 16 * len(UNIT[kind])
                B0 = FIRST["R"] + 2 * r
                frees = [(s_rd, RD * r + 4), (s_rd, RD * r + 5)]
                act.wait_ge(s_unit, 8 + r + 1)
                act.wait_ge(s_rz, 1)
                for gate, w in enumerate((wa, wx)):
                    for b in range(2):
                        act.dma_start(wad[64 * b:64 * b + 64, gate, 64 * b:64 * b + 64],
                                      w[0, bass.ds(2 * r + b, 1), :, :].rearrange("o c d -> (o c) d")).then_inc(s_rw, 16)
                act.wait_ge(s_ze, 2 * B0 + 4)
                act.wait_ge(s_rd, RD * r + 1)
                af(xc[:, :], zst[0][:, :], ACT.Identity, bias=rcol[:, 4:5], scale=rcol[:, 3:4]).then_inc(s_ra, 1)
                af(tg[:, :], zst[1][:, :], ACT.Tanh, scale=0.5).then_inc(s_ra, 1)
                if kind is None:
                    rows(0, 0, 0)
                save(kind, turn, min(8, total), state, frees)
                for gate, o in enumerate((tr, ti)):
                    act.wait_ge(s_rg, 2 * r + gate + 1)
                    af(o[:, :], p_s[gate][:, :], ACT.Tanh, bias=rcol[:, 5 + gate:6 + gate], scale=0.5)\
                        .then_inc(s_ra, 1)
                if kind is None:
                    rows(0, 1, 1)
                act.wait_ge(s_rd, RD * r + 6)
                af(tt[:, :], tr[:, :], ACT.Tanh).then_inc(s_ra, 1)
                act.wait_ge(s_ra, RA * r + 5)
                af(tr[:, :], tr[:, :], ACT.Exp, scale=-1.0).then_inc(s_ra, 1)
                save(kind, turn, min(16, total), state, frees)
                nc.scalar.preload_act_table_set("natural_log_exp_and_others")
                act.wait_ge(s_rd, RD * r + 7)
                af(l1[:, :], tt[:, :], ACT.Ln, scale=2.0).then_inc(s_ra, 1)
                af(l2[:, :], tt[:, :], ACT.Ln, bias=prm[:, 53:54]).then_inc(s_ra, 1)
                if kind is None:
                    rows(0, 2, 0)
                save(kind, turn, min(24, total), state, frees)
                act.wait_ge(s_rd, RD * r + 8)
                af(l1[:, :], l1[:, :], ACT.Exp, scale=0.5).then_inc(s_ra, 1)
                save(kind, turn, total, state, frees)

            with act.Fori(0, TURNS - 1) as a:
                fox(a, "F", a + 1)
            fox(TURNS - 1, "M", 0)
            with act.Fori(0, TURNS - 1) as a:
                mlstm(a, "M", a + 1)
            mlstm(TURNS - 1, "R", 0)
            with act.Fori(0, TURNS - 1) as a:
                rglru(a, "R", a + 1)
            rglru(TURNS - 1, None, 0)

            rows(0, 3, 1)
            with act.Fori(2, 5) as n:
                rows(0, 2 * n, 0)
                rows(0, 2 * n + 1, 1)
            rows(0, 10, 0)
            rows(0, 11, 1)
            rows(1, 0, 0)
            rows(1, 1, 1)
            with act.Fori(1, 5) as n:
                rows(1, 2 * n, 0, "gate")
                rows(1, 2 * n + 1, 1, "gate")
            rows(1, 10, 0, "ple")
            rows(1, 11, 1, "ple")

            def halves(i, b):
                act.wait_ge(s_qt, i + 1)
                if isinstance(i, int) and i == 0:
                    act.wait_ge(s_yl, 24)
                    act.wait_ge(s_yh, 24)
                if not (isinstance(i, int) and i < 2):
                    act.wait_ge(s_gt2, 2 * (i - 1))
                af(hth[b][:, :, :].rearrange("p k s -> p (k s)"), ps[1][:, :], ACT.Copy)
                af(pth[b][:, :, :].rearrange("p k s -> p (k s)"), ps[0][:, 0:KP * P], ACT.Copy).then_inc(s_qh, 1)

            def stats(i, b):
                c = hr[:, b:b + 1]
                if not (isinstance(i, int) and i < 2):
                    act.wait_ge(s_th, i - 1)
                if not (isinstance(i, int) and i == 0):
                    act.wait_ge(s_q1, i)
                af(junk2[:, :], ht[:, bass.ds(i, 1), :].rearrange("p o d -> p (o d)"), ACT.Square, accum_out=c)\
                    .then_inc(s_q1, 1)
                act.wait_ge(s_q1, i + 1)
                af(c, c, ACT.Ln, bias=hr[:, 2:3], scale=4.0 / D).then_inc(s_q2, 1)
                act.wait_ge(s_q2, i + 1)
                af(c, c, ACT.Exp, scale=-0.5).then_inc(s_q3, 1)

            def gate(i, b):
                act.wait_ge(s_gt2, 2 * i + 1)
                act.wait_ge(s_q3, i + 1)
                if not (isinstance(i, int) and i < 2):
                    act.wait_ge(s_fin, i - 1)
                af(th[b][:, :], ps[2][:, :], ACT.Tanh, scale=hr[:, b:b + 1]).then_inc(s_th, 1)

            halves(0, 0)
            act.wait_ge(s_hr, 1)
            stats(0, 0)
            halves(1, 1)
            stats(1, 1)
            gate(0, 0)
            with act.Fori(1, 4) as n:
                for b in range(2):
                    halves(2 * n + b, b)
                    stats(2 * n + b, b)
                    gate(2 * n + (b - 1), 1 - b)
            gate(7, 1)

        @block.vector
        def _(dve):
            v = nc.vector
            v.memset(headmean[:, :], 0.0).then_inc(s_hm, 1)
            dve.wait_ge(s_hm, 1)
            v.memset(headmean[0:64, 0:64], 1.0 / FOX_D).then_inc(s_hm, 1)
            v.memset(headmean[64:128, 64:128], 1.0 / FOX_D).then_inc(s_hm, 1)
            lo_after = {4: (0, 2), 5: (2, 4), 6: (4, 6), 7: (6, 16)}
            for i in range(SB):
                dve.wait_ge(s_rstd, i + 1)
                v.tensor_scalar(xt[:, i, :], xt[:, i, :], prm[:, 80 + i:81 + i], None, ALU.mult).then_inc(s_xn, 1)
                if i == 4:
                    dve.wait_ge(s_ng, 16)
                for n in range(*lo_after.get(i, (0, 0))):
                    half, k = n // KD, n % KD
                    cs = slice(half * HALF, (half + 1) * HALF)
                    dve.wait_ge(s_uh, n + 1)
                    bank = ps[1 + n % 6 // 2][:, n % 2 * HALF:(n % 2 + 1) * HALF]
                    v.scalar_tensor_tensor(ul[:, k, cs], bank, prm[:, k:k + 1], uh[:, k, cs], ALU.mult, ALU.subtract)\
                        .then_inc(s_ul, 1)
            dve.wait_ge(s_par, PARAMS * 16)
            v.tensor_scalar(prm[:, 54:55], prm[:, 48:49], FOX_D ** -0.5, None, ALU.mult).then_inc(s_pc, 1)
            dve.wait_ge(s_ssq, 2)
            v.memset(rm[0:96, :], 1.0).then_inc(s_gv, 1)
            v.memset(mc[64:96, :], 0.0).then_inc(s_gv, 1)
            v.memset(dl[64:96, :], 0.0).then_inc(s_gv, 1)
            dve.wait_ge(s_gv, 3)
            v.memset(rm[64:96, :].rearrange("p (c t) -> p c t", t=CH)[:, :, 0:1], 0.0).then_inc(s_gv, 1)
            pc = [0]

            def small(ins):
                pc[0] += 1
                ins.then_inc(s_pc, 1)
                dve.wait_ge(s_pc, 1 + pc[0])

            t = lambda n: prm[:, 56 + 4 * n:60 + 4 * n]
            small(v.tensor_scalar(prm[:, 36:44], prm[:, 36:44], 0.5, None, ALU.mult))
            dve.wait_ge(s_lam, 1)
            small(v.tensor_scalar(t(1), t(0), 1.0, None, ALU.add))
            dve.wait_ge(s_lam, 2)
            small(v.tensor_scalar(t(1), t(1), -1.0, None, ALU.add))
            small(v.tensor_scalar(t(3), t(1), 0.0, None, ALU.is_equal))
            small(v.tensor_tensor(t(1), t(1), t(3), ALU.add))
            small(v.tensor_tensor(t(2), t(2), t(3), ALU.add))
            small(v.reciprocal(t(4), t(1)))
            small(v.tensor_tensor(t(2), t(2), t(4), ALU.mult))
            small(v.tensor_tensor(t(2), t(2), t(0), ALU.mult))
            small(v.tensor_scalar(t(3), prm[:, 44:48], -1.0, 0.0, ALU.mult, ALU.max))
            small(v.tensor_tensor(t(2), t(2), t(3), ALU.add))
            small(v.tensor_scalar(prm[:, 44:48], t(2), RG_C / 2, None, ALU.mult))
            dve.wait_ge(s_ga, 5)
            v.scalar_tensor_tensor(lf[0:96, :], xb[0:96, :], 0.0, ex[0:96, :], ALU.min, ALU.subtract)\
                .then_inc(s_gd, 1)
            dve.wait_ge(s_gd, 1)
            dve.wait_ge(s_gv, 4)
            v.tensor_tensor_scan(nb[0:96, :], rm[0:96, :], lf[0:96, :], 0.0, ALU.mult, ALU.subtract)\
                .then_inc(s_gd, 1)
            dve.wait_ge(s_gd, 2)
            dve.wait_ge(s_ze, 2)
            v.scalar_tensor_tensor(ar[64:68, :], ar[64:68, :], gcol[64:68, 1:2], nb[64:68, :], ALU.add, ALU.add)\
                .then_inc(s_gd, 1)
            last_of = lambda t: t[64:68, :].rearrange("p (c t) -> p c t", t=CH)[:, :, CH - 1]
            dve.wait_ge(s_gd, 3)
            v.tensor_scalar(dl[64:68, :].rearrange("p (c t) -> p c t", t=CH)[:, 1:, 0], last_of(nb)[:, 0:NC - 1], -1.0,
                            None, ALU.mult).then_inc(s_gd, 1)
            dve.wait_ge(s_gd, 4)
            v.tensor_tensor_scan(gr[64:68, :], dl[64:68, :], ar[64:68, :], 0.0, ALU.add, ALU.max).then_inc(s_gd, 1)
            dve.wait_ge(s_gd, 5)
            v.tensor_tensor(mc[64:68, 1:NC], last_of(gr)[:, 0:NC - 1], last_of(nb)[:, 0:NC - 1], ALU.subtract)\
                .then_inc(s_gd, 1)
            dve.wait_ge(s_gd, 6)
            ch = lambda t: t[64:68, :].rearrange("p (c t) -> p c t", t=CH)
            v.tensor_tensor(ch(ex), bc(mc[64:68, :], CH), ch(gr), ALU.subtract).then_inc(s_gd, 1)
            v.tensor_tensor(ch(xb), ch(ar), bc(last_of(gr), CH), ALU.subtract).then_inc(s_gd, 1)
            v.tensor_tensor(lf[64:68, :], nb[64:68, :], gr[64:68, :], ALU.subtract).then_inc(s_gd, 1)
            dve.wait_ge(s_ga, 7)
            v.tensor_tensor(crow[32:40, :], nb[0:8, :], crow[0:8, :], ALU.subtract).then_inc(s_unit, 1)

            def fox(a):
                dve.wait_ge(s_unit, a + 1)
                for half in range(2):
                    dve.wait_ge(s_vh, 2 * a + half + 1)
                    src = (p_t, p_o)[half].rearrange("p (i h d) -> p i h d", i=4, h=2)
                    dst = vhl[:, 4 * half:4 * half + 4, :, :]
                    v.tensor_tensor(dst[:, :, 0, 64:128], src[:, :, 0, :], dst[:, :, 0, 0:64], ALU.subtract)
                    v.tensor_tensor(dst[:, :, 1, 0:64], src[:, :, 1, :], dst[:, :, 1, 64:128], ALU.subtract)\
                        .then_inc(s_vl, 1)
                dve.wait_ge(s_fa, FA * a + 3)
                v.scalar_tensor_tensor(og[:, :], og[:, :], 1.0, zst[3][:, :], ALU.add, ALU.mult).then_inc(s_og, 1)
                for n, g in ((0, 54), (1, 49)):
                    dve.wait_ge(s_fa, FA * a + 6 + n)
                    v.scalar_tensor_tensor(rq[n][:, :], zst[n][:, :], prm[:, g:g + 1], rq[n][:, :], ALU.mult, ALU.mult)\
                        .then_inc(s_fd, 1)
                dve.wait_ge(s_fd, FD * a + 2)
                head = (slice(0, 64), slice(64, 128))
                for h in range(2):
                    v.tensor_copy(qb[h][head[h], :], rq[0][head[h], :]).then_inc(s_fd, 1)
                for h in range(2):
                    dve.wait_ge(s_fa, FA * a + 8 + h)
                    v.tensor_tensor(qs[h][head[1 - h], :], rq[0][head[h], :], qs[h][head[h], :], ALU.subtract)\
                        .then_inc(s_fd, 1)
                for h in range(2):
                    dve.wait_ge(s_fa, FA * a + 10 + h)
                    v.tensor_tensor(kb[h][head[h], :], rq[1][head[h], :], ka[h][head[h], :], ALU.subtract)\
                        .then_inc(s_fd, 1)

                def maxima(t):
                    n = (t % SB + 1) * P
                    dve.wait_ge(s_sc, 16 * a + t + 1)
                    v.tensor_reduce(sm[:, 4 + t % 2:5 + t % 2], p_s[t % 2][:, 0:n], AX_X, ALU.max).then_inc(s_mx, 1)
                    dve.wait_ge(s_mx, 16 * a + t + 1)
                    v.tensor_scalar(sm[:, t % 2:t % 2 + 1], sm[:, 4 + t % 2:5 + t % 2], -1.0, None, ALU.mult)\
                        .then_inc(s_nm, 1)

                def scale(t):
                    n = (t % SB + 1) * P
                    dve.wait_ge(s_ex, 16 * a + t + 1)
                    v.reciprocal(sm[:, 6 + t % 2:7 + t % 2], sm[:, 2 + t % 2:3 + t % 2]).then_inc(s_rc, 1)
                    dve.wait_ge(s_rc, 16 * a + t + 1)
                    v.tensor_scalar(pr[t % 2][:, 0:n], pr[t % 2][:, 0:n], sm[:, 6 + t % 2:7 + t % 2], None, ALU.mult)\
                        .then_inc(s_pn, 1)

                maxima(0)
                scale(0)
                maxima(1)
                for t in range(16):
                    h, i = t // SB, t % SB
                    for g in range(i // 4 + 1):
                        n_g = 24 * a + ngroups(t) + g
                        dve.wait_ge(s_ph, n_g + 1)
                        j0, j1 = 4 * g, min(4 * g + 4, i + 1)
                        v.tensor_tensor(pt[:, j0:j1, P:], p_t[:, 0:(j1 - j0) * P].rearrange("p (j q) -> p j q", q=P),
                                        pt[:, j0:j1, 0:P], ALU.subtract).then_inc(s_pl, 1)
                        if g == 0 and i >= 4 and t + 2 < 16:
                            maxima(t + 2)
                    if t < 15:
                        scale(t + 1)
                    if i < 4:
                        maxima(t + 2)
                    hi = slice(0, 64) if h == 0 else slice(64, 128)
                    dve.wait_ge(s_oc, 16 * a + t + 1)
                    v.tensor_tensor(oc[hi, :], p_o[hi, 0:2 * P], oc[hi, :], ALU.add).then_inc(s_oa, 1)
                    dve.wait_ge(s_oa, 16 * a + t + 1)
                    v.tensor_tensor(ot[hi, i * P:(i + 1) * P], oc[hi, 0:P], oc[hi, P:], ALU.add).then_inc(s_ot, 1)
                dve.wait_ge(s_ot, 16 * a + 16)
                dve.wait_ge(s_og, a + 1)
                v.scalar_tensor_tensor(yt[:, bass.ds(a, 1), :].rearrange("p o s -> p (o s)"), ot[:, :], 0.5,
                                       og[:, :], ALU.mult, ALU.mult).then_inc(s_unit, 1)

            def mlstm(m):
                B0 = FIRST["M"] + 5 * m
                yrow = yt[:, bass.ds(4 + m, 1), :].rearrange("p o s -> p (o s)")
                e2 = eg[:, :, :].rearrange("p c t -> p (c t)")
                dve.wait_ge(s_unit, 4 + m + 1)
                dve.wait_ge(s_ze, 2 * (B0 + 1) + 2)
                v.tensor_scalar(zst[1][:, :], zst[1][:, :], CH ** -0.5, None, ALU.mult).then_inc(s_md, 1)
                v.tensor_copy(ucol[:, :, :], cols[:, :, :, bass.ds(m, 1)].rearrange("p c q o -> p c (q o)"))\
                    .then_inc(s_md, 1)
                v.memset(cf[:, :], 0.0).then_inc(s_md, 1)
                v.memset(chi[0][:, :].bitcast(F32), 0.0).then_inc(s_md, 1)
                v.memset(clo[0][:, :].bitcast(F32), 0.0).then_inc(s_md, 1)
                dve.wait_ge(s_ma, MA * m + 1)
                v.tensor_tensor(qtl[:, :], zst[0][:, :], qth[:, :], ALU.subtract).then_inc(s_md, 1)
                dve.wait_ge(s_ma, MA * m + 2)
                v.tensor_tensor(ktl[:, :], zst[1][:, :], kth[:, :], ALU.subtract).then_inc(s_md, 1)
                for half in range(2):
                    dve.wait_ge(s_ma, MA * m + 3 + half)
                    v.tensor_tensor(vl2[:, 4 * half:4 * half + 4, 0:P], (p_t, p_o)[half].rearrange(
                        "p (c e) -> p c e", e=P), vh2[:, 4 * half:4 * half + 4, 0:P], ALU.subtract).then_inc(s_md, 1)
                dve.wait_ge(s_mkt, m + 1)
                dve.wait_ge(s_md, MD * m + 7)
                v.tensor_tensor(zst[1][:, :].rearrange("p (c d) -> p c d", d=P), p_s[1][:, :].rearrange(
                    "p (c d) -> p c d", d=P), bc(ucol[:, :, 3], P), ALU.mult).then_inc(s_md, 1)
                dve.wait_ge(s_ma, MA * m + 13)
                v.tensor_tensor(kwl[:, :, :].rearrange("p c d -> p (c d)"), zst[1][:, :],
                                kwh[:, :, :].rearrange("p c d -> p (c d)"), ALU.subtract).then_inc(s_md, 1)
                v.scalar_tensor_tensor(eg[:, :, :], eg[:, :, :], 1.0, tri[:, :].unsqueeze(1).broadcast_to([P, NC, CH]),
                                       ALU.min, ALU.mult).then_inc(s_md, 1)
                dve.wait_ge(s_md, MD * m + 12)
                for half in range(2):
                    cs = slice(half * HALF, (half + 1) * HALF)
                    dve.wait_ge(s_mst, 2 * m + half + 1)
                    v.tensor_tensor(e2[:, cs], e2[:, cs], p_s[0][:, cs], ALU.mult).then_inc(s_md, 1)
                dve.wait_ge(s_ma, MA * m + 14)
                v.tensor_tensor(scl[:, :], e2, sch[:, :], ALU.subtract).then_inc(s_md, 1)
                dve.wait_ge(s_ma, MA * m + 16)
                v.scalar_tensor_tensor(zst[4][:, :], yrow, 1.0, zst[4][:, :], ALU.add, ALU.mult).then_inc(s_md, 1)
                dve.wait_ge(s_md, MD * m + 16)
                v.scalar_tensor_tensor(yrow, zst[3][:, :], 1.0, zst[4][:, :], ALU.add, ALU.mult).then_inc(s_md, 1)
                for c in range(NC):
                    if c < NC - 1:
                        dve.wait_ge(s_mu, (NC - 1) * m + c + 1)
                        if c:
                            dve.wait_ge(s_mcl, (NC - 1) * m + c)
                        v.scalar_tensor_tensor(cf[:, :], cf[:, :], dec[:, c:c + 1], p_s[1][:, (c % 2) * HALF:][:, 0:CV],
                                               ALU.mult, ALU.add).then_inc(s_mc, 1)
                        dve.wait_ge(s_mch, (NC - 1) * m + c + 1)
                        v.tensor_tensor(clo[(c + 1) % 2][:, :], cf[:, :], chi[(c + 1) % 2][:, :], ALU.subtract)\
                            .then_inc(s_mcl, 1)
                    dve.wait_ge(s_mx2, NC * m + c + 1)
                    dve.wait_ge(s_mt, NC * m + c + 1)
                    v.tensor_tensor(hn[:, c, :], ti2[c % 2][:, :], p_s[0][:, (c % 2) * HALF:][:, 0:CV], ALU.add)\
                        .then_inc(s_mh, 1)
                dve.wait_ge(s_mh, NC * (m + 1))
                v.scalar_tensor_tensor(den[:, :], hn[:, :, P], -1.0, hn[:, :, P], ALU.mult, ALU.max)\
                    .then_inc(s_md, 1)
                dve.wait_ge(s_md, MD * m + 18)
                v.tensor_tensor(den[:, :], den[:, :], ucol[:, :, 1], ALU.max).then_inc(s_md, 1)
                dve.wait_ge(s_md, MD * m + 19)
                v.reciprocal(den[:, :], den[:, :]).then_inc(s_md, 1)
                dve.wait_ge(s_md, MD * m + 20)
                v.tensor_tensor(hn[:, :, 0:P], hn[:, :, 0:P], bc(den[:, :], P), ALU.mult).then_inc(s_md, 1)
                dve.wait_ge(s_mht, m + 1)
                v.scalar_tensor_tensor(yrow, p_s[0][:, :], 0.25, yrow, ALU.mult, ALU.mult).then_inc(s_unit, 1)

            def rows(grp, n, b, weights=None):
                if grp == 0:
                    dve.wait_ge(s_oh, n + 1)
                    w = wo[:, bass.ds(n, 1), :, :].rearrange("p o j d -> p (o j) d")
                    v.tensor_tensor(w[:, 1, :], raw[b][:, :], w[:, 0, :], ALU.subtract).then_inc(s_ow, 1)
                dve.wait_ge(s_yh, n + (12 * grp + 1))
                v.tensor_tensor(ysl[b][:, :], yt[:, bass.ds(n, 1), grp * HALF:(grp + 1) * HALF]
                                .rearrange("p o s -> p (o s)"), ysh[b][:, :], ALU.subtract).then_inc(s_yl, 1)
                if weights:
                    dve.wait_ge(s_oh, n + 11)
                    w = wo[:, bass.ds(n - 2, 1), :, :].rearrange("p o j d -> p (o j) d")
                    if weights == "gate":
                        dve.wait_ge(s_pg, n - 1)
                        v.scalar_tensor_tensor(w[:, 1, :], raw[b][:, :], pcol[:, b:b + 1], w[:, 0, :], ALU.mult,
                                               ALU.subtract).then_inc(s_ow, 1)
                    else:
                        v.tensor_tensor(w[:, 1, :], raw[b][:, :], w[:, 0, :], ALU.subtract).then_inc(s_ow, 1)

            def ple_column(n, b):
                if not (isinstance(n, int) and n < 4):
                    dve.wait_ge(s_ow, n + 9)
                v.tensor_copy(pcol[:, b:b + 1], prm[:, 8:16][:, bass.ds(n - 2, 1)]).then_inc(s_pg, 1)

            def rglru(r, last=False):
                stt = v.scalar_tensor_tensor
                dve.wait_ge(s_unit, 8 + r + 1)
                v.tensor_copy(rcol[:, :], prm[:, 16:48].rearrange("p (q k) -> p q k", k=4)[:, :, bass.ds(r, 1)]
                              .rearrange("p q o -> p (q o)")).then_inc(s_rd, 1)
                dve.wait_ge(s_ra, RA * r + 1)
                for j in range(1, 4):
                    if j > 1:
                        dve.wait_ge(s_rd, RD * r + j)
                    stt(xc[:, j:], zst[0][:, 0:S - j], rcol[:, 3 - j:4 - j], xc[:, j:], ALU.mult, ALU.add)\
                        .then_inc(s_rd, 1)
                if last:
                    rows(0, 0, 0)
                dve.wait_ge(s_ra, RA * r + 2)
                stt(tg[:, :], tg[:, :], 1.0, zst[1][:, :], ALU.add, ALU.mult).then_inc(s_rd, 1)
                dve.wait_ge(s_ra, RA * r + 3)
                v.tensor_scalar(tr[:, :], tr[:, :], 1.0, rcol[:, 7:8], ALU.add, ALU.mult).then_inc(s_rd, 1)
                if last:
                    rows(0, 1, 1)
                dve.wait_ge(s_ra, RA * r + 6)
                v.tensor_scalar(tt[:, :], tt[:, :], 1e-18, None, ALU.max).then_inc(s_rd, 1)
                dve.wait_ge(s_ra, RA * r + 8)
                v.tensor_tensor(l1[:, :], l1[:, :], l2[:, :], ALU.subtract).then_inc(s_rd, 1)
                stt(xc[:, :], ti[:, :], 1.0, xc[:, :], ALU.add, ALU.mult).then_inc(s_rd, 1)
                if last:
                    rows(0, 2, 0)
                dve.wait_ge(s_rd, RD * r + 9)
                dve.wait_ge(s_ra, RA * r + 9)
                stt(xc[:, :], xc[:, :], 0.5, l1[:, :], ALU.mult, ALU.mult).then_inc(s_rd, 1)
                dve.wait_ge(s_rd, RD * r + 10)
                v.tensor_tensor_scan(ti[:, :], tr[:, :], xc[:, :], 0.0, ALU.mult, ALU.add).then_inc(s_rd, 1)
                dve.wait_ge(s_rd, RD * r + 11)
                stt(yt[:, bass.ds(8 + r, 1), :].rearrange("p o s -> p (o s)"), ti[:, :], 0.5, tg[:, :], ALU.mult,
                    ALU.mult).then_inc(s_unit, 1)

            dve.wait_ge(s_gm, 5)
            v.memset(qb[0][64:66, :].bitcast(F32), 1.0).then_inc(s_on, 1)
            v.memset(qb[1][0:2, :].bitcast(F32), 1.0).then_inc(s_on, 1)
            with dve.Fori(0, TURNS - 1) as a:
                fox(a)
            fox(TURNS - 1)
            dve.wait_ge(s_unit, 5)
            v.memset(vh2[:, :, P:P + 1].bitcast(F32), 1.0).then_inc(s_mone, 1)
            v.memset(vh2[:, :, P + 1:CV].bitcast(F32), 0.0).then_inc(s_mone, 1)
            v.memset(vl2[:, :, P:CV].bitcast(F32), 0.0).then_inc(s_mone, 1)
            with dve.Fori(0, TURNS - 1) as a:
                mlstm(a)
            mlstm(TURNS - 1)
            dve.wait_ge(s_unit, 9)
            v.memset(wad[:, :, :], 0.0).then_inc(s_rz, 1)
            with dve.Fori(0, TURNS - 1) as a:
                rglru(a)
            rglru(TURNS - 1, last=True)

            def save_h(i):
                dve.wait_ge(s_hx, 16 * SB)
                if i % 4 < 3:
                    dve.wait_ge(s_ob, 3 * (i // 4) + i % 4 + 1)
                else:
                    dve.wait_ge(s_om, 12 * (i // 4 + 1))
                v.tensor_tensor(ht[:, i, :], ht[:, i, :], ps[i % 4][:, :], ALU.add).then_inc(s_h, 1)

            rows(0, 3, 1)
            with dve.Fori(2, 5) as n:
                rows(0, 2 * n, 0)
                rows(0, 2 * n + 1, 1)
            rows(0, 10, 0)
            rows(0, 11, 1)
            rows(1, 0, 0)
            for i in range(4):
                save_h(i)
            rows(1, 1, 1)
            ple_column(2, 0)
            ple_column(3, 1)
            with dve.Fori(1, 4) as n:
                for b in range(2):
                    rows(1, 2 * n + b, b, "gate")
                    ple_column(2 * n + (b + 2), b)
            rows(1, 8, 0, "gate")
            rows(1, 9, 1, "gate")
            rows(1, 10, 0, "ple")
            rows(1, 11, 1, "ple")
            v.memset(hr[:, 2:3], 4.0 * EPS).then_inc(s_hr, 1)
            for i in range(4, 8):
                save_h(i)

            def lows(i, b):
                dve.wait_ge(s_qh, i + 1)
                if not (isinstance(i, int) and i < 2):
                    dve.wait_ge(s_gt2, 2 * (i - 1))
                v.tensor_tensor(htl[b][:, :, :].rearrange("p k s -> p (k s)"), ps[1][:, :],
                                hth[b][:, :, :].rearrange("p k s -> p (k s)"), ALU.subtract)
                v.tensor_tensor(ptl[b][:, :, :].rearrange("p k s -> p (k s)"), ps[0][:, 0:KP * P],
                                pth[b][:, :, :].rearrange("p k s -> p (k s)"), ALU.subtract).then_inc(s_ql, 1)

            def final(i, b):
                h = ht[:, bass.ds(i, 1), :].rearrange("p o d -> p (o d)")
                dve.wait_ge(s_th, i + 1)
                dve.wait_ge(s_gt2, 2 * i + 2)
                v.scalar_tensor_tensor(th[b][:, :], th[b][:, :], 1.0, ps[3][:, :], ALU.add, ALU.mult).then_inc(s_t1, 1)
                dve.wait_ge(s_t1, i + 1)
                v.scalar_tensor_tensor(h, th[b][:, :], 0.5, h, ALU.mult, ALU.add).then_inc(s_fin, 1)

            lows(0, 0)
            lows(1, 1)
            final(0, 0)
            with dve.Fori(1, 4) as n:
                for b in range(2):
                    lows(2 * n + b, b)
                    final(2 * n + (b - 1), 1 - b)
            final(7, 1)


def bc(ap, n):
    return ap.unsqueeze(2).broadcast_to([ap.shape[0], ap.shape[1], n])


_INS = ["x", "p", "norm_g", "w_in", "rg_conv_w", "rg_conv_b", "rg_wa", "rg_ba", "rg_wx", "rg_bx", "rg_lambda",
        "fox_b_f", "fox_q_g", "fox_k_g", "ml_b_i", "ml_b_f", "w_out", "ple_norm_g", "w_ple_gate", "w_ple"]


def kernel(**inputs):
    import numpy as _np
    import concourse.bacc as _bacc
    from concourse.bass_utils import run_bass_kernel_spmd as _run

    nc = _bacc.Bacc("TRN2", target_bir_lowering=False, num_devices=1)
    arrays, args = {}, []
    for name in _INS:
        a = _np.ascontiguousarray(inputs[name])
        arrays[f"in_{name}"] = a
        args.append(nc.dram_tensor(f"in_{name}", a.shape, mybir.dt.from_np(a.dtype), kind="ExternalInput").ap())
    args.append(nc.dram_tensor("out_0", (1, S, D), F32, kind="ExternalOutput").ap())
    hybrid(nc, *args)
    r = _run(nc, [arrays], core_ids=[0])
    return r.results[0]["out_0"]
```

```python
from contextlib import ExitStack

import concourse.bass as bass
from concourse import mybir

ALU = mybir.AluOpType
ACT = mybir.ActivationFunctionType
AX_X = mybir.AxisListType.X
F32 = mybir.dt.float32
FR = mybir.dt.float32r

P = 128
S = 1024
D = 1024
KD = D // P
HALF = 512
SB = S // P
PLE = 256
KP = PLE // P
EPS = 1e-6
KB = 1024

RG_W, FOX_W, ML_W = 512, 512, 512
FOX_H, FOX_D = 8, 64
ML_H = 4
CH = 128
NC = S // CH
CV = 130
RG_C = 8.0
NEG = -3.0e38

C_RX, C_RG = 0, 512
C_FQ, C_FK, C_FV, C_FF, C_FG = 1024, 1536, 2048, 2560, 2568
C_MQ, C_MK, C_MV, C_MI, C_MF, C_MO, C_MG = 3080, 3592, 4104, 4616, 4620, 4624, 5136

UNIT = {
    None: [],
    "F": [(C_FQ, 0), (C_FK, 1), (C_FV, 0), (C_FG, 1)],
    "M": [(C_MQ, 0), (C_MK, 1), (C_MV, 2), (C_MO, 0), (C_MG, 1)],
    "R": [(C_RX, 0), (C_RG, 1)],
}
TURNS = 4
FIRST = {None: 0, "F": 1, "M": 1 + TURNS * len(UNIT["F"]), "R": 1 + TURNS * (len(UNIT["F"]) + len(UNIT["M"]))}
BLOCKS = FIRST["R"] + TURNS * len(UNIT["R"])
BEFORE_ML, BEFORE_RG, UNITS = TURNS, 2 * TURNS, 3 * TURNS
YB = (RG_W + FOX_W + ML_W) // P
SPLIT_ROWS = YB + KD + KP
FOX_ROW = RG_W // P


def spread(total, weights):
    return [total * sum(weights[:n + 1]) // sum(weights) for n in range(len(weights))]


FOX_LEAD = 24
FOX_WEIGHTS = [1, 1, 1, 1, 3, 3, 3, 3] * 2
FOX_EARLY = [1, 1, 2, 2]
ML_LEAD = 24
PARAMS = 13
FA, FD = 13, 8
MA, MD = 16, 19
RA, RD = 17, 20


def ngroups(t):
    return sum(i % SB // 4 + 1 for i in range(t))


def uses(kind, turn, b):
    slot = UNIT[kind][b][1]
    n = 0
    for k in "FMR":
        mine = sum(1 for _, s in UNIT[k] if s == slot)
        if k == kind:
            return n + mine * turn + sum(1 for _, s in UNIT[k][:b + 1] if s == slot)
        n += mine * TURNS


def hybrid(nc, x, p, norm_g, w_in, conv_w, conv_b, wa, ba, wx, bx, lam, fox_b_f, q_g, k_g, ml_b_i, ml_b_f,
           w_out, ple_g, w_gate, w_ple, out):
    ctx = ExitStack()
    with ctx:
        BASE = 16512
        top = nc.sbuf_usable_end
        arena = ctx.enter_context(nc.sbuf_tensor("arena", [P, (top - BASE - 96) // 4], F32))

        def at(name, shape, dt, off):
            size = 4
            for n in shape[1:]:
                size *= n
            assert BASE + off + size <= top, (name, off, size)
            return nc.alloc_sbuf_tensor_at(name, shape, dt, offset=BASE + off)

        def sem(name):
            return ctx.enter_context(nc.semaphore(name))

        uh = at("uh", [P, KD, S], FR, 0)
        ul = at("ul", [P, KD, S], FR, 32 * KB)
        W0 = 64 * KB
        wraw = [at(f"wraw{i}", [P, KD, P], F32, W0 + 4 * KB * i) for i in range(3)]
        wh = [at(f"wh{i}", [P, KD, P], FR, W0 + 4 * KB * (3 + i)) for i in range(3)]
        wl = [at(f"wl{i}", [P, KD, P], FR, W0 + 4 * KB * (6 + i)) for i in range(3)]
        Y = 100 * KB
        yt = at("yt", [P, 12, S], F32, Y)
        Y1, Y2, Y0 = Y, Y + 16 * KB, Y + 32 * KB
        C = Y + 48 * KB
        ident = at("ident", [P, P], F32, C)
        identr = at("identr", [P, P], FR, C + 512)
        maskf = at("maskf", [P, P], F32, C + 1024)
        maskr = at("maskr", [P, P], FR, C + 1536)
        headmean = at("headmean", [P, P], F32, C + 2048)
        prm = at("prm", [P, 96], F32, C + 2560)
        gcol = at("gcol", [96, 2], F32, C + 2560 + 384)
        cols = at("cols", [P, NC, 4, 4], F32, C + 3072)
        tri = at("tri", [P, P], F32, C + 3584)
        SC = C + 4096
        zst = [at(f"zst{i}", [P, S], F32, SC + 4 * KB * i) for i in range(5)]
        S1 = SC + 20 * KB

        xt = at("xt", [P, SB, D], F32, Y)
        junk = at("junk", [P, 2, D], F32, S1 + 8 * KB)
        wgraw = at("wgraw", [P, KD, 16], F32, S1)
        wgh = at("wgh", [P, KD, 96], FR, S1 + 1 * KB)
        wgl = at("wgl", [P, KD, 96], FR, S1 + 4 * KB)
        xb = at("xb", [P, S], F32, Y1)
        ex = at("ex", [P, S], F32, Y1 + 4 * KB)
        lf = at("lf", [P, S], F32, Y1 + 8 * KB)
        nb = at("nb", [P, S], F32, Y1 + 12 * KB)
        ar = at("ar", [P, S], F32, Y2)
        gr = at("gr", [P, S], F32, Y2 + 4 * KB)
        rw = at("rw", [P, S], F32, Y2 + 8 * KB)
        dl = at("dl", [P, S], F32, Y2 + 12 * KB)
        rm = at("rm", [P, S], F32, S1 + 24 * KB)
        crow = at("crow", [64, S], FR, S1 + 8 * KB)
        mc = at("mc", [P, NC], F32, S1 + 32 * KB)
        vhl = at("vhl", [P, SB, 2, P], FR, Y0)
        qb = [at(f"qb{i}", [P, S], FR, Y0 + (8 + 4 * i) * KB) for i in range(2)]
        pr = [at(f"pr{i}", [P, S], F32, Y2 + 4 * KB * i) for i in range(2)]
        og = at("og", [P, S], F32, Y2 + 8 * KB)
        ot = at("ot", [P, S], F32, Y2 + 12 * KB)
        qs = [at(f"qs{i}", [P, S], FR, S1 + 4 * KB * i) for i in range(2)]
        ka = [at(f"ka{i}", [P, S], FR, S1 + 4 * KB * (2 + i)) for i in range(2)]
        kb = [at(f"kb{i}", [P, S], FR, S1 + 4 * KB * (4 + i)) for i in range(2)]
        pt = at("pt", [P, SB, 2 * P], FR, S1 + 24 * KB)
        rq = [at(f"rq{i}", [P, S], F32, S1 + (24 + 4 * i) * KB) for i in range(2)]
        SM = S1 + 32 * KB
        oc = at("oc", [P, 2 * P], F32, SM + 64 + 1024)
        sm = at("sm", [P, 16], F32, SM + 64 + 2048)
        qth, qtl, kth, ktl = [at(n, [P, S], FR, S1 + 4 * KB * i) for i, n in enumerate(("qth", "qtl", "kth", "ktl"))]
        vhl2 = at("vhl2", [P, NC, 2 * CV], FR, S1 + 16 * KB)
        vh2, vl2 = vhl2[:, :, 0:CV], vhl2[:, :, CV:]
        eg = at("eg", [P, NC, CH], F32, S1 + 24 * KB + 256)
        hn = at("hn", [P, NC, CV], F32, S1 + 24 * KB + 256)
        kwh = at("kwh", [P, NC, P], FR, S1 + 28 * KB + 512)
        ucol = at("ucol", [P, NC, 4], F32, S1 + 35 * KB)
        dec = at("dec", [P, NC], F32, S1 + 35 * KB + 128)
        den = at("den", [P, NC], F32, S1 + 35 * KB + 192)
        kwl = at("kwl", [P, NC, P], FR, Y0)
        sch = at("sch", [P, S], FR, Y0 + 4 * KB)
        scl = at("scl", [P, S], FR, Y0 + 8 * KB)
        cf = at("cf", [P, CV], F32, Y0 + 12 * KB)
        chl = [at(f"chl{i}", [P, 2 * CV], FR, Y0 + 12 * KB + 544 * (1 + 2 * i)) for i in range(2)]
        chi, clo = [t[:, 0:CV] for t in chl], [t[:, CV:] for t in chl]
        ti2 = [at(f"ti{i}", [P, CV], F32, Y0 + 12 * KB + 544 * (5 + i)) for i in range(2)]
        xc, tr, ti, tt, l1, l2, tg = [at(n, [P, S], F32, S1 + 4 * KB * i) for i, n in
                                      enumerate(("xc", "tr", "ti", "tt", "l1", "l2", "tg"))]
        wad = at("wad", [P, 2, P], F32, S1 + 33 * KB)
        rcol = at("rcol", [P, 8], F32, S1 + 35 * KB + 256)
        wo = at("wo", [P, 12, 2, D], FR, 0)
        raw = zst[2:4]
        ysh = [at("ysh0", [P, HALF], FR, 96 * KB), at("ysh1", [P, HALF], FR, SC)]
        ysl = [at("ysl0", [P, HALF], FR, 98 * KB), at("ysl1", [P, HALF], FR, SC + 2 * KB)]
        ht = at("ht", [P, SB, D], F32, S1)
        junk2 = at("junk2", [P, D], F32, Y)
        hth = [at(f"hth{i}", [P, KD, P], FR, Y + (8 + 4 * i) * KB) for i in range(2)]
        htl = [at(f"htl{i}", [P, KD, P], FR, Y + (16 + 4 * i) * KB) for i in range(2)]
        th = [at(f"th{i}", [P, D], F32, Y + (24 + 4 * i) * KB) for i in range(2)]
        praw = at("praw", [P, SB, PLE], F32, Y + 32 * KB)
        pth = [at(f"pth{i}", [P, KP, P], FR, Y + (40 + i) * KB) for i in range(2)]
        ptl = [at(f"ptl{i}", [P, KP, P], FR, Y + (42 + i) * KB) for i in range(2)]
        pcol = at("pcol", [P, 2], F32, C + 2560 + 448)
        hr = at("hr", [P, 4], F32, C + 2560 + 480)
        tick = at("tick", [P, 4], F32, C + 2560 + 416)

        ps = [ctx.enter_context(nc.psum_tensor(f"ps{i}", [P, 2 * HALF], F32)) for i in range(4)]
        pz = [ps[0][:, 0:HALF], ps[0][:, HALF:]]
        p_s = [ps[1], ps[2]]
        p_t, p_o = ps[3][:, 0:HALF], ps[3][:, HALF:]

        c_dram = nc.dram_tensor("c_scratch", [FOX_H, 2, S], F32).ap()
        g_dram = nc.dram_tensor("g_scratch", [ML_H, S], F32).ap()
        wl_dram = nc.dram_tensor("wl_scratch", [ML_H, NC], F32).ap()
        w_cols = w_in.rearrange("l (k p) n -> (l p) k n", p=P)

        s_par, s_gb0, s_gb = sem("params_loaded"), sem("gate_bias_cleared"), sem("gate_bias_loaded")
        s_x = [sem(f"x_loaded{i}") for i in range(SB)]
        s_ng = sem("norm_weights_loaded")
        s_id0, s_id = sem("consts_cleared"), sem("consts_ready")
        s_cc = sem("const_casts_ready")
        s_ssq, s_ln, s_rstd, s_xn = sem("sumsq_ready"), sem("rstd_ln"), sem("rstd_ready"), sem("x_scaled")
        s_xT, s_uh, s_ul = sem("xT_ready"), sem("uh_ready"), sem("ul_ready")
        s_wd = [sem(f"w_loaded{i}") for i in range(3)]
        s_wgd, s_wgz, s_wgh, s_wg = (sem("wg_loaded"), sem("wg_cleared"), sem("wg_hi_ready"), sem("wg_ready"))
        s_wh, s_ws = sem("w_hi_ready"), sem("w_split")
        s_z, s_ze = sem("z_half_done"), sem("z_half_saved")
        s_ga, s_gd, s_gm = sem("gate_act"), sem("gate_dve"), sem("gate_memsets")
        s_hm, s_gv = sem("head_mean_ready"), sem("gate_rows_cleared")
        s_gl = sem("minus_m_ready")
        s_gt, s_gc = sem("gate_cols_transposed"), sem("gate_cols_ready")
        s_gw = sem("gate_rows_saved")
        s_pc, s_lam, s_lam0 = sem("param_steps"), sem("lambda_steps"), sem("lambda_abs")
        s_fa, s_fd = sem("fox_prep_act"), sem("fox_prep_dve")
        s_ms, s_vt = sem("fox_meansq"), sem("fox_v_transposed")
        s_on, s_ck = sem("fox_ones_ready"), sem("fox_c_loaded")
        s_vh, s_vl = sem("fox_v_hi"), sem("fox_v_lo")
        s_og = sem("fox_gate_ready")
        s_sc, s_nm, s_mx, s_ex = sem("scores_ready"), sem("negmax_ready"), sem("max_ready"), sem("probs_ready")
        s_rc, s_pn = sem("recip_ready"), sem("probs_scaled")
        s_pt, s_ph, s_pl = sem("probsT_ready"), sem("probsT_hi"), sem("probsT_lo")
        s_pv, s_oc, s_oa, s_ot = sem("pv_done"), sem("pv_copied"), sem("pv_added"), sem("o_ready")
        s_unit = sem("unit_finished")
        s_ma, s_md, s_mg = sem("ml_act"), sem("ml_dve"), sem("ml_rows_loaded")
        s_mo = sem("ml_output_gates")
        s_mone, s_me = sem("ml_ones_ready"), sem("ml_exponents_bounded")
        s_mkt, s_mvt, s_mst = sem("ml_kT"), sem("ml_vT"), sem("ml_scoresT")
        s_mu, s_mx2, s_mi = sem("ml_update"), sem("ml_intra"), sem("ml_inter")
        s_mc, s_mch, s_mcl, s_mt, s_mh = (sem("ml_state"), sem("ml_state_hi"), sem("ml_state_lo"),
                                          sem("ml_inter_scaled"), sem("ml_h"))
        s_mcp, s_mhp = sem("ml_state_half_added"), sem("ml_h_parts_added")
        s_mht = sem("ml_hT")
        s_ra, s_rd, s_rg, s_rw = sem("rg_act"), sem("rg_dve"), sem("rg_gates"), sem("rg_weights_loaded")
        s_rz = sem("rg_weights_cleared")
        s_oh, s_ow = sem("wo_hi"), sem("wo_split")
        s_od = [sem(f"wo_loaded{i}") for i in range(3)]
        s_yh, s_yl, s_om = sem("y_hi"), sem("y_lo"), sem("out_row_block_multiplied")
        s_hx, s_h, s_pp = sem("h_x_loaded"), sem("h_ready"), sem("p_loaded")
        s_pg, s_ob, s_hr = sem("ple_norm_column"), sem("out_block_done"), sem("h_eps_ready")
        s_q1, s_q2, s_q3 = sem("h_sumsq"), sem("h_ln"), sem("h_rstd")
        s_qt, s_qp, s_qh, s_ql = sem("hT_ready"), sem("pT_ready"), sem("hT_pT_hi"), sem("hT_pT_lo")
        s_gp, s_th, s_t1, s_fin = sem("gate_product"), sem("tanh_ready"), sem("gated"), sem("final_ready")
        s_out = sem("out_saved")

        block = ctx.enter_context(nc.Block())

        def blocks(kind, turn):
            n = len(UNIT[kind])
            return [(FIRST[kind] + n * turn + b, slot, c0 + P * turn) for b, (c0, slot) in enumerate(UNIT[kind])]

        @block.sync
        def _(sp):
            for i in range(SB):
                sp.dma_start(xt[:, i, :], x[0, i * P:(i + 1) * P, :]).then_inc(s_x[i], 16)
                if i == 3:
                    with nc.allow_non_contiguous_dma(reason="small parameter columns"):
                        sp.dma_start(prm[:, 0:8], norm_g.rearrange("l (k p) -> (l p) k", p=P)).then_inc(s_ng, 16)
            with nc.allow_non_contiguous_dma(reason="small parameter columns"):
                def col(c, n, src):
                    sp.dma_start(prm[:, c:c + n], src.rearrange("l (k p) -> (l p) k", p=P)).then_inc(s_par, 16)
                sp.dma_start(wgraw[:, :, 0:8], w_cols[:, :, C_FF:C_FF + 8]).then_inc(s_wgd, 16)
                sp.dma_start(wgraw[:, :, 8:16], w_cols[:, :, C_MI:C_MI + 8]).then_inc(s_wgd, 16)
                sp.wait_ge(s_gb0, 1)
                sp.dma_start(gcol[0:8, 0:1], fox_b_f.rearrange("l d -> d l")).then_inc(s_gb, 16)
                sp.dma_start(gcol[64:68, 0:1], ml_b_f.rearrange("l d -> d l")).then_inc(s_gb, 16)
                sp.dma_start(gcol[64:68, 1:2], ml_b_i.rearrange("l d -> d l")).then_inc(s_gb, 16)
                for j in range(4):
                    col(16 + 4 * j, 4, conv_w[:, j, :])
                col(32, 4, conv_b)
                col(36, 4, ba)
                col(40, 4, bx)
                col(44, 4, lam)
                col(8, 8, ple_g)
                for h in range(2):
                    sp.dma_start(prm[64 * h:64 * h + 64, 48:49], q_g.rearrange("l d -> d l")).then_inc(s_par, 16)
                    sp.dma_start(prm[64 * h:64 * h + 64, 49:50], k_g.rearrange("l d -> d l")).then_inc(s_par, 16)

            def load_blocks(kind, turn):
                for b, (B, slot, col) in enumerate(blocks(kind, turn)):
                    if not (isinstance(B, int) and B < 3):
                        sp.wait_ge(s_ws, B - 2)
                    sp.dma_start(wraw[slot][:, :, :], w_cols[:, :, bass.ds(col, P)]).then_inc(s_wd[slot], 16)

            def load_gates(r):
                if isinstance(r, int):
                    sp.wait_ge(s_rz, 1)
                else:
                    sp.wait_ge(s_rg, 4 * r)
                for gate, w in enumerate((wa, wx)):
                    for b in range(2):
                        sp.dma_start(wad[64 * b:64 * b + 64, gate, 64 * b:64 * b + 64],
                                     w[0, bass.ds(2 * r + b, 1), :, :].rearrange("o c d -> (o c) d")).then_inc(s_rw, 16)

            for kind in "FMR":
                load_blocks(kind, 0)
                if kind == "R":
                    load_gates(0)
                with sp.Fori(1, TURNS) as turn:
                    load_blocks(kind, turn)
                    if kind == "R":
                        load_gates(turn)

            def load_rows(src, n):
                for b in range(2):
                    if not isinstance(n, int) or n:
                        sp.wait_ge(s_ow, 2 * n + b - 1)
                    sp.dma_start(raw[b][:, :], src(b)).then_inc(s_od[b], 16)

            sp.wait_ge(s_unit, BEFORE_RG + 1)
            load_rows(lambda b: w_out[0, (FOX_ROW + b) * P:(FOX_ROW + b + 1) * P, :], 0)
            with sp.Fori(1, 4) as n:
                load_rows(lambda b: w_out[0, bass.ds((2 * n + (FOX_ROW + b)) * P, P), :], n)
            with sp.Fori(4, 6) as n:
                load_rows(lambda b: w_out[0, bass.ds((2 * n - (8 - b)) * P, P), :], n)
            sp.wait_ge(s_unit, UNITS + 1)
            for i in range(SB):
                sp.dma_start(ht[:, i, :], x[0, i * P:(i + 1) * P, :]).then_inc(s_hx, 16)
            with sp.Fori(6, 10) as n:
                load_rows(lambda b: w_gate[0, bass.ds((2 * n - (12 - b)) * P, P), :], n)
            load_rows(lambda b: w_ple[0, b * P:(b + 1) * P, :], 10)
            sp.wait_ge(s_yl, 2 * YB)
            sp.wait_ge(s_yh, 2 * YB)
            sp.dma_start(praw[:, :, :], p[0, 0].rearrange("(i q) c -> q i c", q=P)).then_inc(s_pp, 16)
            with sp.Fori(0, SB) as i:
                sp.wait_ge(s_fin, i + 1)
                sp.dma_start(out[0, bass.ds(i * P, P), :], ht[:, bass.ds(i, 1), :].rearrange("p o d -> p (o d)"))\
                    .then_inc(s_out, 16)
            sp.wait_ge(s_out, 16 * SB)

        @block.gpsimd
        def _(g):
            g.memset(gcol[:, :], 0.0).then_inc(s_gb0, 1)
            g.memset(ident[:, :], 0.0).then_inc(s_id0, 1)
            g.memset(maskf[:, :], 0.0).then_inc(s_id0, 1)
            g.memset(tri[:, :], 1.0).then_inc(s_id0, 1)
            g.memset(prm[:, 52:53], EPS)
            g.memset(tick[:, :], 0.0)
            g.memset(prm[:, 53:54], 1.0)
            g.wait_ge(s_id0, 3)
            g.affine_select(out=ident[:, :], in_=ident[:, :], compare_op=ALU.not_equal, fill=1.0, base=0,
                            pattern=[[-1, P]], channel_multiplier=1).then_inc(s_id, 1)
            g.affine_select(out=maskf[:, :], in_=maskf[:, :], compare_op=ALU.is_ge, fill=NEG, base=0,
                            pattern=[[-1, P]], channel_multiplier=1).then_inc(s_id, 1)
            g.affine_select(out=tri[:, :], in_=tri[:, :], compare_op=ALU.is_ge, fill=0.0, base=0,
                            pattern=[[1, P]], channel_multiplier=-1).then_inc(s_id, 1)
            g.memset(wgh[:, :, :].bitcast(F32), 0.0).then_inc(s_wgz, 1)
            g.memset(wgl[:, :, :].bitcast(F32), 0.0).then_inc(s_wgz, 1)
            g.wait_ge(s_wgd, 32)
            g.wait_ge(s_wgz, 2)
            parts = [(0, 0, 8), (32, 8, 4), (64, 12, 4)]
            for to, frm, n in parts:
                last = g.tensor_copy(wgh[:, :, to:to + n], wgraw[:, :, frm:frm + n])
            last.then_inc(s_wgh, 1)
            g.wait_ge(s_wgh, 1)
            for to, frm, n in parts:
                last = g.tensor_tensor(wgl[:, :, to:to + n], wgraw[:, :, frm:frm + n], wgh[:, :, to:to + n],
                                       ALU.subtract)
            last.then_inc(s_wg, 1)

            def clear_rows():
                g.wait_ge(s_xT, 16)
                g.memset(rw[:, :], 0.0).then_inc(s_gm, 1)
                for h in range(2):
                    g.memset(qb[h][:, :].bitcast(F32), 0.0).then_inc(s_gm, 1)
                    g.memset(kb[h][:, :].bitcast(F32), 0.0).then_inc(s_gm, 1)

            def split(kind, turn):
                for b, (B, slot, _) in enumerate(blocks(kind, turn)):
                    g.wait_ge(s_wd[slot], 16 * uses(kind, turn, b))
                    if not (isinstance(B, int) and B < 3):
                        g.wait_ge(s_z, 2 * (B - 1))
                    g.tensor_tensor(tick[:, 2:3], tick[:, 0:1], tick[:, 1:2], ALU.add)
                    g.tensor_copy(wh[slot][:, :, :], wraw[slot][:, :, :]).then_inc(s_wh, 1)
                    g.wait_ge(s_wh, B)
                    g.tensor_tensor(wl[slot][:, :, :], wraw[slot][:, :, :], wh[slot][:, :, :],
                                    ALU.subtract).then_inc(s_ws, 1)
                    if isinstance(B, int) and B == 2:
                        clear_rows()

            for kind in "FMR":
                split(kind, 0)
                with g.Fori(1, TURNS) as turn:
                    split(kind, turn)

        @block.tensor
        def _(pe):
            mm = nc.tensor.matmul

            def z_steps(kind, turn):
                for b, (B, slot, _) in enumerate(blocks(kind, turn)):
                    for half in range(2):
                        if half == 0:
                            pe.wait_ge(s_ws, B)
                        pe.wait_ge(s_ze, 2 * B + half - 1)
                        for k in range(KD):
                            cs = slice(half * HALF, (half + 1) * HALF)
                            mm(pz[half], wh[slot][:, k, :], uh[:, k, cs], start=(k == 0), stop=False)
                            mm(pz[half], wh[slot][:, k, :], ul[:, k, cs], start=False, stop=False)
                            last = mm(pz[half], wl[slot][:, k, :], uh[:, k, cs], start=False, stop=(k == KD - 1))
                            if k == KD - 1:
                                last.then_inc(s_z, 1)
                            yield

            def run(steps, n):
                for _ in range(n):
                    if next(steps, 0) == 0:
                        break

            pe.wait_ge(s_id, 2)
            for half in range(2):
                pe.wait_ge(s_xn, 4 * half + 4)
                for k in range(KD):
                    n = half * KD + k
                    if n >= 6:
                        pe.wait_ge(s_ul, n - 5)
                    bank = ps[1 + n % 6 // 2][:, n % 2 * HALF:(n % 2 + 1) * HALF]
                    for i in range(4):
                        last = nc.tensor.transpose(bank[:, i * P:(i + 1) * P],
                                                   xt[:, 4 * half + i, k * P:(k + 1) * P], ident[:, :])
                    last.then_inc(s_xT, 1)
                cs = slice(half * HALF, (half + 1) * HALF)
                pe.wait_ge(s_wg, 1)
                for k in range(KD):
                    pe.wait_ge(s_ul, half * KD + k + 1)
                    mm(pz[half][0:96], wgh[:, k, :], uh[:, k, cs], start=(k == 0), stop=False)
                    mm(pz[half][0:96], wgh[:, k, :], ul[:, k, cs], start=False, stop=False)
                    last = mm(pz[half][0:96], wgl[:, k, :], uh[:, k, cs], start=False, stop=(k == KD - 1))
                last.then_inc(s_z, 1)

            first = z_steps("F", 0)
            run(first, 48)
            pe.wait_ge(s_ga, 10)
            for half in range(2):
                bank = (p_t, p_o)[half]
                for c in range(4):
                    last = nc.tensor.transpose(bank[:, c * P:(c + 1) * P], rw[:, (4 * half + c) * CH:][:, 0:CH],
                                               ident[:, :])
                last.then_inc(s_gt, 1)
            run(first, 64)

            def fox(a, kind, turn):
                steps = z_steps(kind, turn)
                total = 16 * len(UNIT[kind])
                run(steps, 6)
                pe.wait_ge(s_unit, a + 1)
                pe.wait_ge(s_gc, 2)
                pe.wait_ge(s_ze, 2 * (FIRST["F"] + 4 * a + 2) + 2)
                for half in range(2):
                    bank = (p_t, p_o)[half]
                    for i in range(4):
                        last = nc.tensor.transpose(bank[:, i * P:(i + 1) * P],
                                                   zst[2][:, (4 * half + i) * P:][:, 0:P], ident[:, :])
                    last.then_inc(s_vt, 1)
                pe.wait_ge(s_hm, 3)
                for n in range(2):
                    pe.wait_ge(s_fa, FA * a + 1 + n)
                    for half in range(2):
                        cs = slice(half * HALF, (half + 1) * HALF)
                        last = mm(p_s[n][:, cs], headmean[:, :], pr[n][:, cs], start=True, stop=True)
                    last.then_inc(s_ms, 1)
                    run(steps, 3)
                run(steps, min(FOX_LEAD, total) - 12)

                def scores(t):
                    h, i = t // SB, t % SB
                    n = (i + 1) * P
                    if t == 0:
                        pe.wait_ge(s_on, 2)
                        pe.wait_ge(s_fa, FA * a + 13)
                        pe.wait_ge(s_fd, FD * a + 8)
                        pe.wait_ge(s_ck, 32 * (a + 1))
                    if t >= 2:
                        pe.wait_ge(s_ex, 16 * a + t - 1)
                    bank = p_s[t % 2]
                    for c0 in range(0, n, HALF):
                        c1 = min(c0 + HALF, n)
                        o = bank[:, c0:c1]
                        diag = c1 == n
                        mm(o, qs[h][:, i * P:(i + 1) * P], ka[h][:, c0:c1], start=True, stop=False)
                        if diag:
                            mm(bank[:, n - P:n], identr[:, :], maskr[:, :], start=False, stop=False)
                        last = mm(o, qb[h][:, i * P:(i + 1) * P], kb[h][:, c0:c1], start=False, stop=True)
                    last.then_inc(s_sc, 1)

                upto = spread(total - min(FOX_LEAD, total), FOX_WEIGHTS)
                scores(0)
                scores(1)
                for t in range(16):
                    h, i = t // SB, t % SB
                    groups = i // 4 + 1
                    todo, early = upto[t] - (upto[t - 1] if t else 0), 0
                    pe.wait_ge(s_pn, 16 * a + t + 1)
                    for g in range(groups):
                        n_g = 24 * a + 12 * h + max(0, i - 4) * 2 + min(i, 4) + g
                        if t == 0 and g == 0:
                            pe.wait_ge(s_vl, 2 * a + 2)
                        else:
                            pe.wait_ge(s_pl, n_g)
                        for j in range(4 * g, min(4 * g + 4, i + 1)):
                            last = nc.tensor.transpose(p_t[:, (j % 4) * P:(j % 4 + 1) * P],
                                                       pr[t % 2][:, j * P:(j + 1) * P], ident[:, :])
                        last.then_inc(s_pt, 1)
                        if g == 0 and t + 2 < 16:
                            scores(t + 2)
                        if g == 0 and groups == 2:
                            early = min(todo, FOX_EARLY[i - 4])
                            run(steps, early)
                    run(steps, todo - early)
                    n_g += 1
                    pe.wait_ge(s_ph, n_g)
                    pe.wait_ge(s_pl, n_g)
                    if t:
                        pe.wait_ge(s_oa, 16 * a + t)
                    for j in range(i + 1):
                        last = mm(p_o[:, 0:2 * P], vhl[:, j, h, :], pt[:, j, :], start=(j == 0), stop=(j == i))
                    last.then_inc(s_pv, 1)
                run(steps, 100)

            def mlstm(m, kind, turn):
                steps = z_steps(kind, turn)
                total = 16 * len(UNIT[kind])
                done = min(ML_LEAD, total - 8)
                upto = spread(total - done, [1] * NC)
                run(steps, 4)
                pe.wait_ge(s_unit, BEFORE_ML + m + 1)
                pe.wait_ge(s_md, MD * m + 1)
                for half in range(2):
                    for i in range(4 * half, 4 * half + 4):
                        last = nc.tensor.transpose(p_s[1][:, i * P:(i + 1) * P], zst[1][:, i * P:(i + 1) * P],
                                                   ident[:, :])
                last.then_inc(s_mkt, 1)
                run(steps, done // 3 - 4)
                for half in range(2):
                    bank = (p_t, p_o)[half]
                    for i in range(4):
                        last = nc.tensor.transpose(bank[:, i * P:(i + 1) * P],
                                                   zst[2][:, (4 * half + i) * P:][:, 0:P], ident[:, :])
                    last.then_inc(s_mvt, 1)
                run(steps, done // 3)
                pe.wait_ge(s_ma, MA * m + 2)
                pe.wait_ge(s_md, MD * m + 7)
                for c in range(NC):
                    o = p_s[0][:, c * CH:(c + 1) * CH]
                    cs = slice(c * CH, (c + 1) * CH)
                    mm(o, kth[:, cs], qth[:, cs], start=True, stop=False)
                    mm(o, kth[:, cs], qtl[:, cs], start=False, stop=False)
                    last = mm(o, ktl[:, cs], qth[:, cs], start=False, stop=True)
                    if c % 4 == 3:
                        last.then_inc(s_mst, 1)
                run(steps, done - 2 * (done // 3))
                for c in range(NC):
                    cs = slice(c * CH, (c + 1) * CH)
                    todo = upto[c] - (upto[c - 1] if c else 0)
                    if c == 0:
                        pe.wait_ge(s_md, MD * m + 11)
                        pe.wait_ge(s_ma, MA * m + 13)
                        pe.wait_ge(s_mone, 3)
                    elif c > 1:
                        pe.wait_ge(s_mc, (NC - 1) * m + c - 1)
                    if c < NC - 1:
                        o = p_s[1][:, (c % 2) * HALF:][:, 0:2 * CV]
                        mm(o, kwh[:, c, :], vhl2[:, c, :], start=True, stop=False)
                        mm(o, kwl[:, c, :], vhl2[:, c, :], start=False, stop=True).then_inc(s_mu, 1)
                    if c == 0:
                        pe.wait_ge(s_md, MD * m + 15)
                    elif c > 1:
                        pe.wait_ge(s_mh, NC * m + c - 1)
                    o = p_s[0][:, (c % 2) * HALF:][:, 0:2 * CV]
                    mm(o, sch[:, cs], vhl2[:, c, :], start=True, stop=False)
                    mm(o, scl[:, cs], vhl2[:, c, :], start=False, stop=True).then_inc(s_mx2, 1)
                    run(steps, todo // 2)
                    if c:
                        pe.wait_ge(s_mcl, (NC - 1) * m + c)
                        if c > 1:
                            pe.wait_ge(s_mt, NC * m + c - 1)
                    o = (p_t, p_o)[c % 2][:, 0:2 * CV]
                    mm(o, qth[:, cs], chl[c % 2][:, :], start=True, stop=False)
                    mm(o, qtl[:, cs], chl[c % 2][:, :], start=False, stop=True).then_inc(s_mi, 1)
                    run(steps, todo - todo // 2)
                pe.wait_ge(s_md, MD * m + 19)
                for i in range(NC):
                    last = nc.tensor.transpose(p_s[0][:, i * P:(i + 1) * P], hn[:, i, 0:P], ident[:, :])
                last.then_inc(s_mht, 1)
                run(steps, 100)

            def rglru(r, kind, turn):
                steps = z_steps(kind, turn)
                run(steps, 8)
                pe.wait_ge(s_unit, BEFORE_RG + r + 1)
                pe.wait_ge(s_rw, 64 * (r + 1))
                for half in range(2):
                    cs = slice(half * HALF, (half + 1) * HALF)
                    pe.wait_ge(s_rd, RD * r + 4 + 3 * half)
                    for gate in range(2):
                        mm(p_s[gate][:, cs], wad[:, gate, :], xc[:, cs], start=True, stop=True).then_inc(s_rg, 1)
                    run(steps, 3)
                run(steps, 100)

            with pe.Fori(0, TURNS - 1) as a:
                fox(a, "F", a + 1)
            fox(TURNS - 1, "M", 0)
            with pe.Fori(0, TURNS - 1) as a:
                mlstm(a, "M", a + 1)
            mlstm(TURNS - 1, "R", 0)
            with pe.Fori(0, TURNS - 1) as a:
                rglru(a, "R", a + 1)
            rglru(TURNS - 1, None, 0)

            def h_transposes(i):
                if i == 0:
                    pe.wait_ge(s_h, 5)
                else:
                    pe.wait_ge(s_ql, i)
                for k in range(KD):
                    last = nc.tensor.transpose(ps[0][:, k * P:(k + 1) * P], ht[:, i, k * P:(k + 1) * P], ident[:, :])
                last.then_inc(s_qt, 1)

            def p_transposes(i):
                if i == 0:
                    pe.wait_ge(s_h, 6)
                    pe.wait_ge(s_pp, 16)
                for k in range(KP):
                    last = nc.tensor.transpose(ps[1][:, k * P:(k + 1) * P], praw[:, i, k * P:(k + 1) * P], ident[:, :])
                last.then_inc(s_qp, 1)

            def row_block(grp, n, b):
                first, final = isinstance(n, int) and n == 0, isinstance(n, int) and n == 11
                if grp == 0:
                    pe.wait_ge(s_ow, n + 1)
                pe.wait_ge(s_yl, n + (12 * grp + 1))
                for i in range(4):
                    if first and grp == 0:
                        if i == 0:
                            pe.wait_ge(s_ze, 2 * BLOCKS)
                        if i == 1:
                            pe.wait_ge(s_ra, RA * (TURNS - 1) + 7)
                    if first and grp == 1:
                        pe.wait_ge(s_h, i + 1)
                    if final and grp == 1 and i == 3:
                        h_transposes(0)
                    sl = slice(i * P, (i + 1) * P)
                    for dh in range(2):
                        cs = slice(dh * HALF, (dh + 1) * HALF)
                        o = ps[i][:, cs]
                        w_hi, w_lo = [wo[:, bass.ds(n, 1), j, cs].rearrange("p o d -> p (o d)") for j in range(2)]
                        mm(o, ysh[b][:, sl], w_hi, start=first, stop=False)
                        mm(o, ysh[b][:, sl], w_lo, start=False, stop=False)
                        last = mm(o, ysl[b][:, sl], w_hi, start=False, stop=final)
                    if final and i < 3:
                        last.then_inc(s_ob, 1)
                last.then_inc(s_om, 1)

            for grp in range(2):
                row_block(grp, 0, 0)
                row_block(grp, 1, 1)
                with pe.Fori(1, 5) as n:
                    row_block(grp, 2 * n, 0)
                    row_block(grp, 2 * n + 1, 1)
                row_block(grp, 10, 0)
                row_block(grp, 11, 1)

            def gated(i, b):
                if i == 0:
                    pe.wait_ge(s_ow, SPLIT_ROWS)
                    pe.wait_ge(s_h, 8)
                pe.wait_ge(s_ql, i + 1)
                for dst, hi, lo, k0, nk, free in ((ps[2], hth, htl, 0, KD, s_th), (ps[3], pth, ptl, KD, KP, s_t1)):
                    if i:
                        pe.wait_ge(free, i)
                    for half in range(2):
                        cs = slice(half * HALF, (half + 1) * HALF)
                        for k in range(nk):
                            mm(dst[:, cs], hi[b][:, k, :], wo[:, k0 + k, 0, cs], start=(k == 0), stop=False)
                            mm(dst[:, cs], hi[b][:, k, :], wo[:, k0 + k, 1, cs], start=False, stop=False)
                            last = mm(dst[:, cs], lo[b][:, k, :], wo[:, k0 + k, 0, cs], start=False,
                                      stop=(k == nk - 1))
                    last.then_inc(s_gp, 1)

            p_transposes(0)
            for i in range(SB):
                if i < SB - 1:
                    h_transposes(i + 1)
                    p_transposes(i + 1)
                gated(i, i % 2)

        @block.scalar
        def _(act):
            af = nc.scalar.activation
            nc.scalar.preload_act_table_set("natural_log_exp_and_others")
            act.wait_ge(s_id, 1)
            hi_after = {4: (0, 2), 5: (2, 4), 6: (4, 6), 7: (6, 16)}
            for i in range(SB):
                r = prm[:, 80 + i:81 + i]
                act.wait_ge(s_x[i], 16)
                if i >= 2:
                    act.wait_ge(s_ssq, i - 1)
                af(junk[:, i % 2, :], xt[:, i, :], ACT.Square, accum_out=r).then_inc(s_ssq, 1)
                act.wait_ge(s_ssq, i + 1)
                af(r, r, ACT.Ln, bias=prm[:, 52:53], scale=1.0 / D).then_inc(s_ln, 1)
                act.wait_ge(s_ln, i + 1)
                af(r, r, ACT.Exp, scale=-0.5).then_inc(s_rstd, 1)
                if i == 4:
                    act.wait_ge(s_ng, 16)
                for n in range(*hi_after.get(i, (0, 0))):
                    half, k = n // KD, n % KD
                    act.wait_ge(s_xT, n + 1)
                    bank = ps[1 + n % 6 // 2][:, n % 2 * HALF:(n % 2 + 1) * HALF]
                    af(uh[:, k, half * HALF:(half + 1) * HALF], bank, ACT.Identity, scale=prm[:, k:k + 1])\
                        .then_inc(s_uh, 1)
            act.wait_ge(s_par, PARAMS * 16)
            act.wait_ge(s_id, 2)
            af(identr[:, :], ident[:, :], ACT.Copy).then_inc(s_cc, 1)
            af(maskr[:, :], maskf[:, :], ACT.Copy).then_inc(s_cc, 1)

            af(prm[:, 76:80], prm[:, 44:48], ACT.Abs).then_inc(s_lam0, 1)
            act.wait_ge(s_lam0, 1)
            af(prm[:, 56:60], prm[:, 76:80], ACT.Exp, scale=-1.0).then_inc(s_lam, 1)
            act.wait_ge(s_pc, 3)
            af(prm[:, 64:68], prm[:, 60:64], ACT.Ln).then_inc(s_lam, 1)

            act.wait_ge(s_gb, 48)
            act.wait_ge(s_xT, 16)
            for half in range(2):
                cs = slice(half * HALF, (half + 1) * HALF)
                act.wait_ge(s_z, half + 1)
                af(xb[0:96, cs], pz[half][0:96], ACT.Identity, bias=gcol[:, 0:1]).then_inc(s_ga, 1)
                af(ar[64:68, cs], pz[half][32:36], ACT.Copy).then_inc(s_ze, 1)
            act.wait_ge(s_ga, 2)
            af(ex[0:96, :], xb[0:96, :], ACT.Abs).then_inc(s_ga, 1)
            act.wait_ge(s_ga, 3)
            af(ex[0:96, :], ex[0:96, :], ACT.Exp, scale=-1.0).then_inc(s_ga, 1)
            act.wait_ge(s_ga, 4)
            af(ex[0:96, :], ex[0:96, :], ACT.Ln, bias=prm[0:96, 53:54]).then_inc(s_ga, 1)

            def save(kind, turn, upto, state, frees=None):
                while state[0] < upto // 8:
                    n = state[0]
                    b, half = n // 2, n % 2
                    B = FIRST[kind] + len(UNIT[kind]) * turn + b
                    act.wait_ge(s_z, 2 * B + half + 1)
                    if half == 0 and frees:
                        act.wait_ge(*frees[b])
                    af(zst[b][:, half * HALF:(half + 1) * HALF], pz[half], ACT.Copy).then_inc(s_ze, 1)
                    state[0] += 1

            st = [0]
            save("F", 0, 32, st)
            act.wait_ge(s_gm, 1)
            act.wait_ge(s_gd, 3)
            af(rw[0:4, :], ar[64:68, :], ACT.Copy).then_inc(s_ga, 1)
            act.wait_ge(s_gd, 2)
            af(crow[0:8, :], nb[0:8, :], ACT.Copy).then_inc(s_ga, 1)
            act.wait_ge(s_gd, 7)
            af(rw[64:68, :], ex[64:68, :], ACT.Exp).then_inc(s_ga, 1)
            act.wait_ge(s_gd, 8)
            af(rw[96:100, :], xb[64:68, :], ACT.Exp).then_inc(s_ga, 1)
            act.wait_ge(s_gd, 9)
            af(rw[32:36, :], lf[64:68, :], ACT.Exp).then_inc(s_ga, 1)
            act.wait_ge(s_ga, 8)
            with nc.allow_non_contiguous_dma(reason="last token of each chunk"):
                act.dma_start(g_dram, gr[64:68, :]).then_inc(s_gw, 16)
                act.dma_start(wl_dram, rw[64:68, :].rearrange("p (c t) -> p c t", t=CH)[:, :, CH - 1])\
                    .then_inc(s_gw, 16)
            for half in range(2):
                act.wait_ge(s_gt, half + 1)
                af(cols[:, 4 * half:4 * half + 4, :, :],
                   (p_t, p_o)[half].rearrange("p (c q r) -> p c q r", c=4, q=4)[:, :, :, 0:4], ACT.Copy)\
                    .then_inc(s_gc, 1)
            act.wait_ge(s_unit, 1)
            act.dma_start(c_dram[:, 0, :], crow[0:8, :].bitcast(F32)).then_inc(s_gw, 16)
            act.dma_start(c_dram[:, 1, :], crow[32:40, :].bitcast(F32)).then_inc(s_gw, 16)
            save("F", 0, 64, st)

            def fox(a, kind, turn):
                state = [0]
                total = 16 * len(UNIT[kind])
                frees = [(s_fd, FD * a + 1), (s_fd, FD * a + 4), (s_vt, 2 * a + 2), (s_og, a + 1), (s_ga, 1)]
                act.wait_ge(s_unit, a + 1)
                act.wait_ge(s_gc, 2)
                act.wait_ge(s_gw, 64)
                act.wait_ge(s_gm, 5)
                for h, row in enumerate((64, 0)):
                    act.dma_start(kb[h][row:row + 2, :].bitcast(F32), c_dram[bass.ds(2 * a + h, 1), :, :]
                                  .rearrange("o r s -> (o r) s")).then_inc(s_ck, 16)
                for n in range(2):
                    act.wait_ge(s_ze, 2 * (FIRST["F"] + 4 * a + n) + 2)
                    af(pr[n][:, :], zst[n][:, :], ACT.Square).then_inc(s_fa, 1)
                act.wait_ge(s_ze, 2 * (FIRST["F"] + 4 * a + 3) + 2)
                af(og[:, :], zst[3][:, :], ACT.Tanh, scale=0.5).then_inc(s_fa, 1)
                for half in range(2):
                    act.wait_ge(s_vt, 2 * a + half + 1)
                    src = (p_t, p_o)[half].rearrange("p (i h d) -> p i h d", i=4, h=2)
                    af(vhl[:, 4 * half:4 * half + 4, 0, 0:64], src[:, :, 0, :], ACT.Copy)
                    af(vhl[:, 4 * half:4 * half + 4, 1, 64:128], src[:, :, 1, :], ACT.Copy).then_inc(s_vh, 1)
                nc.scalar.preload_act_table_set("natural_log_exp_and_others")
                for n in range(2):
                    act.wait_ge(s_ms, 2 * a + n + 1)
                    af(rq[n][:, :], p_s[n][:, :], ACT.Ln, bias=prm[:, 52:53]).then_inc(s_fa, 1)
                    act.wait_ge(s_fa, FA * a + 4 + 2 * n)
                    af(rq[n][:, :], rq[n][:, :], ACT.Exp, scale=-0.5).then_inc(s_fa, 1)
                act.wait_ge(s_fd, FD * a + 1)
                save(kind, turn, min(8, total), state, frees)
                af(qs[0][0:64, :], rq[0][0:64, :], ACT.Copy).then_inc(s_fa, 1)
                af(qs[1][64:128, :], rq[0][64:128, :], ACT.Copy).then_inc(s_fa, 1)
                act.wait_ge(s_fd, FD * a + 4)
                af(ka[0][0:64, :], rq[1][0:64, :], ACT.Copy).then_inc(s_fa, 1)
                save(kind, turn, min(16, total), state, frees)
                af(ka[1][64:128, :], rq[1][64:128, :], ACT.Copy).then_inc(s_fa, 1)
                af(ka[0][64:128, :], rq[1][0:64, :], ACT.Copy).then_inc(s_fa, 1)
                af(ka[1][0:64, :], rq[1][64:128, :], ACT.Copy).then_inc(s_fa, 1)
                save(kind, turn, min(FOX_LEAD, total), state, frees)
                done = min(FOX_LEAD, total)
                upto = spread(total - done, FOX_WEIGHTS)

                def probs(t):
                    h, i = t // SB, t % SB
                    n = (i + 1) * P
                    act.wait_ge(s_nm, 16 * a + t + 1)
                    if t >= 2:
                        act.wait_ge(s_pt, 24 * a + ngroups(t - 1))
                    af(pr[t % 2][:, 0:n], p_s[t % 2][:, 0:n], ACT.Exp, bias=sm[:, t % 2:t % 2 + 1],
                       accum_out=sm[:, 2 + t % 2:3 + t % 2]).then_inc(s_ex, 1)

                probs(0)
                for t in range(16):
                    h, i = t // SB, t % SB
                    for g in range(i // 4 + 1):
                        n_g = 24 * a + ngroups(t) + g
                        act.wait_ge(s_pt, n_g + 1)
                        if g == 0 and t:
                            act.wait_ge(s_pv, 16 * a + t)
                        j0, j1 = 4 * g, min(4 * g + 4, i + 1)
                        af(pt[:, j0:j1, 0:P], p_t[:, 0:(j1 - j0) * P].rearrange("p (j q) -> p j q", q=P), ACT.Copy)\
                            .then_inc(s_ph, 1)
                        if g == 0 and t < 15:
                            probs(t + 1)
                    act.wait_ge(s_pv, 16 * a + t + 1)
                    if t:
                        act.wait_ge(s_ot, 16 * a + t)
                    hi, lo = (slice(0, 64), slice(64, 128)) if h == 0 else (slice(64, 128), slice(0, 64))
                    af(oc[hi, :], p_o[lo, 0:2 * P], ACT.Copy).then_inc(s_oc, 1)
                    save(kind, turn, done + upto[t], state, frees)

            def mlstm(m, kind, turn):
                state = [0]
                total = 16 * len(UNIT[kind])
                done = min(ML_LEAD, total - 8)
                upto = spread(total - done, [1] * NC)
                frees = [(s_md, MD * m + 6), (s_md, MD * m + 11), (s_mvt, 2 * m + 2), (s_mo, 2 * m + 2),
                         (s_mo, 2 * m + 2)]
                B0 = FIRST["M"] + 5 * m
                act.wait_ge(s_unit, BEFORE_ML + m + 1)
                act.dma_start(eg[:, :, :].rearrange("p c t -> p (c t)"),
                              g_dram[bass.ds(m, 1), :].broadcast_to([P, S])).then_inc(s_mg, 16)
                act.dma_start(dec[:, :], wl_dram[bass.ds(m, 1), :].broadcast_to([P, NC])).then_inc(s_mg, 16)
                act.wait_ge(s_ze, 2 * B0 + 2)
                af(qth[:, :], zst[0][:, :], ACT.Copy).then_inc(s_ma, 1)
                act.wait_ge(s_md, MD * m + 1)
                af(kth[:, :], zst[1][:, :], ACT.Copy).then_inc(s_ma, 1)
                for half in range(2):
                    act.wait_ge(s_mvt, 2 * m + half + 1)
                    af(vh2[:, 4 * half:4 * half + 4, 0:P], (p_t, p_o)[half].rearrange("p (c e) -> p c e", e=P),
                       ACT.Copy).then_inc(s_ma, 1)
                save(kind, turn, min(8, total), state, frees)
                act.wait_ge(s_me, m + 1)
                for c in range(NC):
                    af(eg[:, c, :], eg[:, c, :], ACT.Exp, bias=ucol[:, c, 0:1], scale=-1.0).then_inc(s_ma, 1)
                save(kind, turn, min(16, total), state, frees)
                act.wait_ge(s_md, MD * m + 10)
                af(kwh[:, :, :].rearrange("p c d -> p (c d)"), zst[1][:, :], ACT.Copy).then_inc(s_ma, 1)
                act.wait_ge(s_md, MD * m + 14)
                af(sch[:, :], eg[:, :, :].rearrange("p c t -> p (c t)"), ACT.Copy).then_inc(s_ma, 1)
                act.wait_ge(s_ze, 2 * (B0 + 4) + 2)
                af(zst[3][:, :], zst[3][:, :], ACT.Tanh, scale=0.5).then_inc(s_ma, 1)
                af(yt[:, bass.ds(4 + m, 1), :].rearrange("p o s -> p (o s)"), zst[4][:, :], ACT.Tanh, scale=0.5)\
                    .then_inc(s_ma, 1)
                save(kind, turn, done, state, frees)
                for c in range(NC):
                    if c < NC - 1:
                        act.wait_ge(s_mc, (NC - 1) * m + c + 1)
                        if c > 0:
                            act.wait_ge(s_mi, NC * m + c)
                        af(chi[(c + 1) % 2][:, :], cf[:, :], ACT.Copy).then_inc(s_mch, 1)
                    act.wait_ge(s_mi, NC * m + c + 1)
                    if c > 1:
                        act.wait_ge(s_mh, NC * m + c - 1)
                    af(ti2[c % 2][:, :], (p_t, p_o)[c % 2][:, 0:CV], ACT.Identity, scale=ucol[:, c, 2:3])\
                        .then_inc(s_mt, 1)
                    save(kind, turn, done + upto[c], state, frees)
                save(kind, turn, total, state, frees)

            def loads(n, b):
                return 8 * (n - b) + 16

            def rows(grp, n, b, weights=None):
                first = isinstance(n, int) and n == 0
                if grp == 0:
                    if first:
                        act.wait_ge(s_z, 2 * BLOCKS)
                    if isinstance(n, int) and n == 1:
                        act.wait_ge(s_rd, RD * (TURNS - 1) + 7)
                    act.wait_ge(s_od[b], loads(n, b))
                    af(wo[:, bass.ds(n, 1), 0, :].rearrange("p o d -> p (o d)"), raw[b][:, :], ACT.Copy)\
                        .then_inc(s_oh, 1)
                if isinstance(n, int) and n == 11:
                    act.wait_ge(s_unit, UNITS + 1)
                if not (isinstance(n, int) and n < 2) or grp:
                    act.wait_ge(s_om, n + (12 * grp - 1))
                af(ysh[b][:, :], yt[:, bass.ds(n, 1), grp * HALF:(grp + 1) * HALF].rearrange("p o s -> p (o s)"),
                   ACT.Copy).then_inc(s_yh, 1)
                if weights:
                    act.wait_ge(s_od[b], loads(n + 10, b))
                    to = wo[:, bass.ds(n - 2, 1), 0, :].rearrange("p o d -> p (o d)")
                    if weights == "gate":
                        act.wait_ge(s_pg, n - 1)
                        af(to, raw[b][:, :], ACT.Identity, scale=pcol[:, b:b + 1]).then_inc(s_oh, 1)
                    else:
                        af(to, raw[b][:, :], ACT.Copy).then_inc(s_oh, 1)

            def rglru(r, kind, turn):
                state = [0]
                total = 16 * len(UNIT[kind])
                B0 = FIRST["R"] + 2 * r
                frees = [(s_rd, RD * r + 7), (s_rd, RD * r + 8)]
                halves = [slice(0, HALF), slice(HALF, S)]
                act.wait_ge(s_unit, BEFORE_RG + r + 1)
                act.wait_ge(s_rd, RD * r + 1)
                for half, cs in enumerate(halves):
                    act.wait_ge(s_ze, 2 * B0 + half + 1)
                    af(xc[:, cs], zst[0][:, cs], ACT.Identity, bias=rcol[:, 4:5], scale=rcol[:, 3:4]).then_inc(s_ra, 1)
                if kind is None:
                    rows(0, 0, 0)
                act.wait_ge(s_ze, 2 * B0 + 4)
                af(tg[:, :], zst[1][:, :], ACT.Tanh, scale=0.5).then_inc(s_ra, 1)
                save(kind, turn, min(8, total), state, frees)
                for half, cs in enumerate(halves):
                    for gate, o in enumerate((tr, ti)):
                        act.wait_ge(s_rg, 4 * r + 2 * half + gate + 1)
                        af(o[:, cs], p_s[gate][:, cs], ACT.Tanh, bias=rcol[:, 5 + gate:6 + gate], scale=0.5)\
                            .then_inc(s_ra, 1)
                if kind is None:
                    rows(0, 1, 1)
                for half, cs in enumerate(halves):
                    act.wait_ge(s_rd, RD * r + 9 + 2 * half)
                    af(tt[:, cs], tr[:, cs], ACT.Tanh).then_inc(s_ra, 1)
                save(kind, turn, min(16, total), state, frees)
                for half, cs in enumerate(halves):
                    act.wait_ge(s_ra, RA * r + 8 + half)
                    af(tr[:, cs], tr[:, cs], ACT.Exp, scale=-1.0).then_inc(s_ra, 1)
                nc.scalar.preload_act_table_set("natural_log_exp_and_others")
                for half, cs in enumerate(halves):
                    act.wait_ge(s_rd, RD * r + 13 + half)
                    af(l1[:, cs], tt[:, cs], ACT.Ln, scale=2.0).then_inc(s_ra, 1)
                    af(l2[:, cs], tt[:, cs], ACT.Ln, bias=prm[:, 53:54]).then_inc(s_ra, 1)
                save(kind, turn, min(24, total), state, frees)
                if kind is None:
                    rows(0, 2, 0)
                for half, cs in enumerate(halves):
                    act.wait_ge(s_rd, RD * r + 15 + half)
                    af(l1[:, cs], l1[:, cs], ACT.Exp, scale=0.5).then_inc(s_ra, 1)
                save(kind, turn, total, state, frees)

            with act.Fori(0, TURNS - 1) as a:
                fox(a, "F", a + 1)
            fox(TURNS - 1, "M", 0)
            with act.Fori(0, TURNS - 1) as a:
                mlstm(a, "M", a + 1)
            mlstm(TURNS - 1, "R", 0)
            with act.Fori(0, TURNS - 1) as a:
                rglru(a, "R", a + 1)
            rglru(TURNS - 1, None, 0)

            rows(0, 3, 1)
            with act.Fori(2, 5) as n:
                rows(0, 2 * n, 0)
                rows(0, 2 * n + 1, 1)
            rows(0, 10, 0)
            rows(0, 11, 1)
            rows(1, 0, 0)
            rows(1, 1, 1)
            with act.Fori(1, 5) as n:
                rows(1, 2 * n, 0, "gate")
                rows(1, 2 * n + 1, 1, "gate")
            rows(1, 10, 0, "ple")
            rows(1, 11, 1, "ple")

            def halves(i, b):
                act.wait_ge(s_qt, i + 1)
                if isinstance(i, int) and i == 0:
                    act.wait_ge(s_yl, 2 * YB)
                    act.wait_ge(s_yh, 2 * YB)
                if not (isinstance(i, int) and i < 2):
                    act.wait_ge(s_gp, 2 * (i - 1))
                af(hth[b][:, :, :].rearrange("p k s -> p (k s)"), ps[0][:, :], ACT.Copy)
                act.wait_ge(s_qp, i + 1)
                af(pth[b][:, :, :].rearrange("p k s -> p (k s)"), ps[1][:, 0:KP * P], ACT.Copy).then_inc(s_qh, 1)

            def stats(i, b):
                c = hr[:, b:b + 1]
                if not (isinstance(i, int) and i < 2):
                    act.wait_ge(s_th, i - 1)
                if not (isinstance(i, int) and i == 0):
                    act.wait_ge(s_q1, i)
                af(junk2[:, :], ht[:, bass.ds(i, 1), :].rearrange("p o d -> p (o d)"), ACT.Square, accum_out=c)\
                    .then_inc(s_q1, 1)
                act.wait_ge(s_q1, i + 1)
                af(c, c, ACT.Ln, bias=hr[:, 2:3], scale=4.0 / D).then_inc(s_q2, 1)
                act.wait_ge(s_q2, i + 1)
                af(c, c, ACT.Exp, scale=-0.5).then_inc(s_q3, 1)

            def gate(i, b):
                act.wait_ge(s_gp, 2 * i + 1)
                act.wait_ge(s_q3, i + 1)
                if not (isinstance(i, int) and i < 2):
                    act.wait_ge(s_fin, i - 1)
                af(th[b][:, :], ps[2][:, :], ACT.Tanh, scale=hr[:, b:b + 1]).then_inc(s_th, 1)

            halves(0, 0)
            act.wait_ge(s_hr, 1)
            stats(0, 0)
            halves(1, 1)
            stats(1, 1)
            gate(0, 0)
            with act.Fori(1, 4) as n:
                for b in range(2):
                    halves(2 * n + b, b)
                    stats(2 * n + b, b)
                    gate(2 * n + (b - 1), 1 - b)
            gate(7, 1)

        @block.vector
        def _(dve):
            v = nc.vector
            v.memset(headmean[:, :], 0.0).then_inc(s_hm, 1)
            dve.wait_ge(s_hm, 1)
            v.memset(headmean[0:64, 0:64], 1.0 / FOX_D).then_inc(s_hm, 1)
            v.memset(headmean[64:128, 64:128], 1.0 / FOX_D).then_inc(s_hm, 1)
            lo_after = {4: (0, 2), 5: (2, 4), 6: (4, 6), 7: (6, 16)}
            for i in range(SB):
                dve.wait_ge(s_rstd, i + 1)
                v.tensor_scalar(xt[:, i, :], xt[:, i, :], prm[:, 80 + i:81 + i], None, ALU.mult).then_inc(s_xn, 1)
                if i == 4:
                    dve.wait_ge(s_ng, 16)
                for n in range(*lo_after.get(i, (0, 0))):
                    half, k = n // KD, n % KD
                    cs = slice(half * HALF, (half + 1) * HALF)
                    dve.wait_ge(s_uh, n + 1)
                    bank = ps[1 + n % 6 // 2][:, n % 2 * HALF:(n % 2 + 1) * HALF]
                    v.scalar_tensor_tensor(ul[:, k, cs], bank, prm[:, k:k + 1], uh[:, k, cs], ALU.mult, ALU.subtract)\
                        .then_inc(s_ul, 1)
            dve.wait_ge(s_par, PARAMS * 16)
            v.tensor_scalar(prm[:, 54:55], prm[:, 48:49], FOX_D ** -0.5, None, ALU.mult).then_inc(s_pc, 1)
            dve.wait_ge(s_ssq, 2)
            v.memset(rm[0:96, :], 1.0).then_inc(s_gv, 1)
            v.memset(mc[64:96, :], 0.0).then_inc(s_gv, 1)
            v.memset(dl[64:96, :], 0.0).then_inc(s_gv, 1)
            dve.wait_ge(s_gv, 3)
            v.memset(rm[64:96, :].rearrange("p (c t) -> p c t", t=CH)[:, :, 0:1], 0.0).then_inc(s_gv, 1)
            pc = [0]

            def small(ins):
                pc[0] += 1
                ins.then_inc(s_pc, 1)
                dve.wait_ge(s_pc, 1 + pc[0])

            t = lambda n: prm[:, 56 + 4 * n:60 + 4 * n]
            small(v.tensor_scalar(prm[:, 36:44], prm[:, 36:44], 0.5, None, ALU.mult))
            dve.wait_ge(s_lam, 1)
            small(v.tensor_scalar(t(1), t(0), 1.0, None, ALU.add))
            dve.wait_ge(s_lam, 2)
            small(v.tensor_scalar(t(1), t(1), -1.0, None, ALU.add))
            small(v.tensor_scalar(t(3), t(1), 0.0, None, ALU.is_equal))
            small(v.tensor_tensor(t(1), t(1), t(3), ALU.add))
            small(v.tensor_tensor(t(2), t(2), t(3), ALU.add))
            small(v.reciprocal(t(4), t(1)))
            small(v.tensor_tensor(t(2), t(2), t(4), ALU.mult))
            small(v.tensor_tensor(t(2), t(2), t(0), ALU.mult))
            small(v.tensor_scalar(t(3), prm[:, 44:48], -1.0, 0.0, ALU.mult, ALU.max))
            small(v.tensor_tensor(t(2), t(2), t(3), ALU.add))
            small(v.tensor_scalar(prm[:, 44:48], t(2), RG_C / 2, None, ALU.mult))
            dve.wait_ge(s_ga, 5)
            v.scalar_tensor_tensor(lf[0:96, :], xb[0:96, :], 0.0, ex[0:96, :], ALU.min, ALU.subtract)\
                .then_inc(s_gd, 1)
            dve.wait_ge(s_gd, 1)
            dve.wait_ge(s_gv, 4)
            v.tensor_tensor_scan(nb[0:96, :], rm[0:96, :], lf[0:96, :], 0.0, ALU.mult, ALU.subtract)\
                .then_inc(s_gd, 1)
            dve.wait_ge(s_gd, 2)
            dve.wait_ge(s_ze, 2)
            v.scalar_tensor_tensor(ar[64:68, :], ar[64:68, :], gcol[64:68, 1:2], nb[64:68, :], ALU.add, ALU.add)\
                .then_inc(s_gd, 1)
            last_of = lambda t: t[64:68, :].rearrange("p (c t) -> p c t", t=CH)[:, :, CH - 1]
            dve.wait_ge(s_gd, 3)
            v.tensor_scalar(dl[64:68, :].rearrange("p (c t) -> p c t", t=CH)[:, 1:, 0], last_of(nb)[:, 0:NC - 1], -1.0,
                            None, ALU.mult).then_inc(s_gd, 1)
            dve.wait_ge(s_gd, 4)
            v.tensor_tensor_scan(gr[64:68, :], dl[64:68, :], ar[64:68, :], 0.0, ALU.add, ALU.max).then_inc(s_gd, 1)
            dve.wait_ge(s_gd, 5)
            v.tensor_tensor(mc[64:68, 1:NC], last_of(gr)[:, 0:NC - 1], last_of(nb)[:, 0:NC - 1], ALU.subtract)\
                .then_inc(s_gd, 1)
            dve.wait_ge(s_gd, 6)
            ch = lambda t: t[64:68, :].rearrange("p (c t) -> p c t", t=CH)
            v.tensor_tensor(ch(ex), bc(mc[64:68, :], CH), ch(gr), ALU.subtract).then_inc(s_gd, 1)
            v.tensor_tensor(ch(xb), ch(ar), bc(last_of(gr), CH), ALU.subtract).then_inc(s_gd, 1)
            v.tensor_tensor(lf[64:68, :], nb[64:68, :], gr[64:68, :], ALU.subtract).then_inc(s_gl, 1)
            dve.wait_ge(s_gl, 1)
            v.tensor_scalar(lf[64:68, :], lf[64:68, :], 88.0, None, ALU.min).then_inc(s_gd, 1)
            dve.wait_ge(s_ga, 7)
            v.tensor_tensor(crow[32:40, :], nb[0:8, :], crow[0:8, :], ALU.subtract).then_inc(s_unit, 1)

            def fox(a):
                dve.wait_ge(s_unit, a + 1)
                for half in range(2):
                    dve.wait_ge(s_vh, 2 * a + half + 1)
                    src = (p_t, p_o)[half].rearrange("p (i h d) -> p i h d", i=4, h=2)
                    dst = vhl[:, 4 * half:4 * half + 4, :, :]
                    v.tensor_tensor(dst[:, :, 0, 64:128], src[:, :, 0, :], dst[:, :, 0, 0:64], ALU.subtract)
                    v.tensor_tensor(dst[:, :, 1, 0:64], src[:, :, 1, :], dst[:, :, 1, 64:128], ALU.subtract)\
                        .then_inc(s_vl, 1)
                dve.wait_ge(s_fa, FA * a + 3)
                v.scalar_tensor_tensor(og[:, :], og[:, :], 1.0, zst[3][:, :], ALU.add, ALU.mult).then_inc(s_og, 1)
                head = (slice(0, 64), slice(64, 128))
                for n, g in ((0, 54), (1, 49)):
                    dve.wait_ge(s_fa, FA * a + 5 + 2 * n)
                    v.scalar_tensor_tensor(rq[n][:, :], zst[n][:, :], prm[:, g:g + 1], rq[n][:, :], ALU.mult, ALU.mult)\
                        .then_inc(s_fd, 1)
                    if n == 0:
                        dve.wait_ge(s_fd, FD * a + 1)
                        for h in range(2):
                            v.tensor_copy(qb[h][head[h], :], rq[0][head[h], :]).then_inc(s_fd, 1)
                dve.wait_ge(s_fd, FD * a + 4)
                for h in range(2):
                    dve.wait_ge(s_fa, FA * a + 8 + h)
                    v.tensor_tensor(qs[h][head[1 - h], :], rq[0][head[h], :], qs[h][head[h], :], ALU.subtract)\
                        .then_inc(s_fd, 1)
                for h in range(2):
                    dve.wait_ge(s_fa, FA * a + 10 + h)
                    v.tensor_tensor(kb[h][head[h], :], rq[1][head[h], :], ka[h][head[h], :], ALU.subtract)\
                        .then_inc(s_fd, 1)

                def maxima(t):
                    n = (t % SB + 1) * P
                    dve.wait_ge(s_sc, 16 * a + t + 1)
                    v.tensor_reduce(sm[:, 4 + t % 2:5 + t % 2], p_s[t % 2][:, 0:n], AX_X, ALU.max).then_inc(s_mx, 1)
                    dve.wait_ge(s_mx, 16 * a + t + 1)
                    v.tensor_scalar(sm[:, t % 2:t % 2 + 1], sm[:, 4 + t % 2:5 + t % 2], -1.0, None, ALU.mult)\
                        .then_inc(s_nm, 1)

                def scale(t):
                    n = (t % SB + 1) * P
                    dve.wait_ge(s_ex, 16 * a + t + 1)
                    v.reciprocal(sm[:, 6 + t % 2:7 + t % 2], sm[:, 2 + t % 2:3 + t % 2]).then_inc(s_rc, 1)
                    dve.wait_ge(s_rc, 16 * a + t + 1)
                    v.tensor_scalar(pr[t % 2][:, 0:n], pr[t % 2][:, 0:n], sm[:, 6 + t % 2:7 + t % 2], None, ALU.mult)\
                        .then_inc(s_pn, 1)

                maxima(0)
                scale(0)
                maxima(1)
                for t in range(16):
                    h, i = t // SB, t % SB
                    for g in range(i // 4 + 1):
                        n_g = 24 * a + ngroups(t) + g
                        dve.wait_ge(s_ph, n_g + 1)
                        j0, j1 = 4 * g, min(4 * g + 4, i + 1)
                        v.tensor_tensor(pt[:, j0:j1, P:], p_t[:, 0:(j1 - j0) * P].rearrange("p (j q) -> p j q", q=P),
                                        pt[:, j0:j1, 0:P], ALU.subtract).then_inc(s_pl, 1)
                        if g == 0 and i >= 4 and t + 2 < 16:
                            maxima(t + 2)
                    if t < 15:
                        scale(t + 1)
                    if i < 4:
                        maxima(t + 2)
                    hi = slice(0, 64) if h == 0 else slice(64, 128)
                    dve.wait_ge(s_oc, 16 * a + t + 1)
                    v.tensor_tensor(oc[hi, :], p_o[hi, 0:2 * P], oc[hi, :], ALU.add).then_inc(s_oa, 1)
                    dve.wait_ge(s_oa, 16 * a + t + 1)
                    v.tensor_tensor(ot[hi, i * P:(i + 1) * P], oc[hi, 0:P], oc[hi, P:], ALU.add).then_inc(s_ot, 1)
                dve.wait_ge(s_ot, 16 * a + 16)
                dve.wait_ge(s_og, a + 1)
                v.scalar_tensor_tensor(yt[:, bass.ds(a, 1), :].rearrange("p o s -> p (o s)"), ot[:, :], 0.5,
                                       og[:, :], ALU.mult, ALU.mult).then_inc(s_unit, 1)

            def mlstm(m, final_unit=False):
                B0 = FIRST["M"] + 5 * m
                yrow = yt[:, bass.ds(4 + m, 1), :].rearrange("p o s -> p (o s)")
                e2 = eg[:, :, :].rearrange("p c t -> p (c t)")
                dve.wait_ge(s_unit, BEFORE_ML + m + 1)
                dve.wait_ge(s_ze, 2 * (B0 + 1) + 2)
                v.tensor_scalar(zst[1][:, :], zst[1][:, :], CH ** -0.5, None, ALU.mult).then_inc(s_md, 1)
                v.tensor_copy(ucol[:, :, :], cols[:, :, :, bass.ds(m, 1)].rearrange("p c q o -> p c (q o)"))\
                    .then_inc(s_md, 1)
                v.memset(cf[:, :], 0.0).then_inc(s_md, 1)
                v.memset(chi[0][:, :].bitcast(F32), 0.0).then_inc(s_md, 1)
                v.memset(clo[0][:, :].bitcast(F32), 0.0).then_inc(s_md, 1)
                dve.wait_ge(s_ma, MA * m + 1)
                v.tensor_tensor(qtl[:, :], zst[0][:, :], qth[:, :], ALU.subtract).then_inc(s_md, 1)
                dve.wait_ge(s_ma, MA * m + 2)
                v.tensor_tensor(ktl[:, :], zst[1][:, :], kth[:, :], ALU.subtract).then_inc(s_md, 1)
                for half in range(2):
                    dve.wait_ge(s_ma, MA * m + 3 + half)
                    v.tensor_tensor(vl2[:, 4 * half:4 * half + 4, 0:P], (p_t, p_o)[half].rearrange(
                        "p (c e) -> p c e", e=P), vh2[:, 4 * half:4 * half + 4, 0:P], ALU.subtract).then_inc(s_md, 1)
                dve.wait_ge(s_mg, 32 * (m + 1))
                dve.wait_ge(s_md, MD * m + 2)
                v.tensor_tensor(eg[:, :, :], eg[:, :, :], bc(ucol[:, :, 0], CH), ALU.max).then_inc(s_me, 1)
                dve.wait_ge(s_mkt, m + 1)
                dve.wait_ge(s_md, MD * m + 7)
                v.tensor_tensor(zst[1][:, :].rearrange("p (c d) -> p c d", d=P), p_s[1][:, :].rearrange(
                    "p (c d) -> p c d", d=P), bc(ucol[:, :, 3], P), ALU.mult).then_inc(s_md, 1)
                dve.wait_ge(s_ma, MA * m + 13)
                v.tensor_tensor(kwl[:, :, :].rearrange("p c d -> p (c d)"), zst[1][:, :],
                                kwh[:, :, :].rearrange("p c d -> p (c d)"), ALU.subtract).then_inc(s_md, 1)
                v.tensor_tensor(eg[:, :, :], eg[:, :, :], tri[:, :].unsqueeze(1).broadcast_to([P, NC, CH]),
                                ALU.mult).then_inc(s_md, 1)
                dve.wait_ge(s_md, MD * m + 12)
                for half in range(2):
                    cs = slice(half * HALF, (half + 1) * HALF)
                    dve.wait_ge(s_mst, 2 * m + half + 1)
                    v.tensor_tensor(e2[:, cs], e2[:, cs], p_s[0][:, cs], ALU.mult).then_inc(s_md, 1)
                dve.wait_ge(s_ma, MA * m + 14)
                v.tensor_tensor(scl[:, :], e2, sch[:, :], ALU.subtract).then_inc(s_md, 1)
                def gates():
                    dve.wait_ge(s_ma, MA * m + 16)
                    v.scalar_tensor_tensor(zst[4][:, :], yrow, 1.0, zst[4][:, :], ALU.add, ALU.mult).then_inc(s_mo, 1)
                    dve.wait_ge(s_mo, 2 * m + 1)
                    v.scalar_tensor_tensor(yrow, zst[3][:, :], 1.0, zst[4][:, :], ALU.add, ALU.mult).then_inc(s_mo, 1)

                if not final_unit:
                    gates()

                def outputs(c):
                    own, old = p_s[0][:, (c % 2) * HALF:][:, 0:2 * CV], (p_t, p_o)[c % 2][:, 0:2 * CV]
                    dve.wait_ge(s_mt, NC * m + c + 1)
                    v.scalar_tensor_tensor(hn[:, c, :], old[:, CV:], ucol[:, c, 2:3], ti2[c % 2][:, :], ALU.mult,
                                           ALU.add).then_inc(s_mhp, 1)
                    yield
                    dve.wait_ge(s_mhp, 2 * NC * m + 2 * c + 1)
                    dve.wait_ge(s_mx2, NC * m + c + 1)
                    v.tensor_tensor(hn[:, c, :], hn[:, c, :], own[:, 0:CV], ALU.add).then_inc(s_mhp, 1)
                    yield
                    dve.wait_ge(s_mhp, 2 * NC * m + 2 * c + 2)
                    v.tensor_tensor(hn[:, c, :], hn[:, c, :], own[:, CV:], ALU.add).then_inc(s_mh, 1)
                    yield

                for c in range(NC - 1):
                    last = outputs(c - 1) if c else iter(())
                    add = p_s[1][:, (c % 2) * HALF:][:, 0:2 * CV]
                    dve.wait_ge(s_mu, (NC - 1) * m + c + 1)
                    if c:
                        dve.wait_ge(s_mcl, (NC - 1) * m + c)
                    v.scalar_tensor_tensor(cf[:, :], cf[:, :], dec[:, c:c + 1], add[:, 0:CV], ALU.mult, ALU.add)\
                        .then_inc(s_mcp, 1)
                    next(last, None)
                    dve.wait_ge(s_mcp, (NC - 1) * m + c + 1)
                    v.tensor_tensor(cf[:, :], cf[:, :], add[:, CV:], ALU.add).then_inc(s_mc, 1)
                    next(last, None)
                    next(last, None)
                    dve.wait_ge(s_mch, (NC - 1) * m + c + 1)
                    v.tensor_tensor(clo[(c + 1) % 2][:, :], cf[:, :], chi[(c + 1) % 2][:, :], ALU.subtract)\
                        .then_inc(s_mcl, 1)
                for c in (NC - 2, NC - 1):
                    for _ in outputs(c):
                        pass
                dve.wait_ge(s_mh, NC * (m + 1))
                v.scalar_tensor_tensor(den[:, :], hn[:, :, P], -1.0, hn[:, :, P], ALU.mult, ALU.max)\
                    .then_inc(s_md, 1)
                dve.wait_ge(s_md, MD * m + 16)
                v.tensor_tensor(den[:, :], den[:, :], ucol[:, :, 1], ALU.max).then_inc(s_md, 1)
                dve.wait_ge(s_md, MD * m + 17)
                v.reciprocal(den[:, :], den[:, :]).then_inc(s_md, 1)
                dve.wait_ge(s_md, MD * m + 18)
                v.tensor_tensor(hn[:, :, 0:P], hn[:, :, 0:P], bc(den[:, :], P), ALU.mult).then_inc(s_md, 1)
                if final_unit:
                    gates()
                dve.wait_ge(s_mo, 2 * m + 2)
                dve.wait_ge(s_mht, m + 1)
                v.scalar_tensor_tensor(yrow, p_s[0][:, :], 0.25, yrow, ALU.mult, ALU.mult).then_inc(s_unit, 1)

            def rows(grp, n, b, weights=None):
                if grp == 0:
                    dve.wait_ge(s_oh, n + 1)
                    w = wo[:, bass.ds(n, 1), :, :].rearrange("p o j d -> p (o j) d")
                    v.tensor_tensor(w[:, 1, :], raw[b][:, :], w[:, 0, :], ALU.subtract).then_inc(s_ow, 1)
                dve.wait_ge(s_yh, n + (12 * grp + 1))
                v.tensor_tensor(ysl[b][:, :], yt[:, bass.ds(n, 1), grp * HALF:(grp + 1) * HALF]
                                .rearrange("p o s -> p (o s)"), ysh[b][:, :], ALU.subtract).then_inc(s_yl, 1)
                if weights:
                    dve.wait_ge(s_oh, n + 11)
                    w = wo[:, bass.ds(n - 2, 1), :, :].rearrange("p o j d -> p (o j) d")
                    if weights == "gate":
                        dve.wait_ge(s_pg, n - 1)
                        v.scalar_tensor_tensor(w[:, 1, :], raw[b][:, :], pcol[:, b:b + 1], w[:, 0, :], ALU.mult,
                                               ALU.subtract).then_inc(s_ow, 1)
                    else:
                        v.tensor_tensor(w[:, 1, :], raw[b][:, :], w[:, 0, :], ALU.subtract).then_inc(s_ow, 1)

            def ple_column(n, b):
                if not (isinstance(n, int) and n < 4):
                    dve.wait_ge(s_ow, n + 9)
                v.tensor_copy(pcol[:, b:b + 1], prm[:, 8:16][:, bass.ds(n - 2, 1)]).then_inc(s_pg, 1)

            def rglru(r, last=False):
                stt = v.scalar_tensor_tensor
                dve.wait_ge(s_unit, BEFORE_RG + r + 1)
                v.tensor_copy(rcol[:, :], prm[:, 16:48].rearrange("p (q k) -> p q k", k=4)[:, :, bass.ds(r, 1)]
                              .rearrange("p q o -> p (q o)")).then_inc(s_rd, 1)
                halves = [slice(0, HALF), slice(HALF, S)]
                for half in range(2):
                    dve.wait_ge(s_ra, RA * r + 1 + half)
                    for j in range(1, 4):
                        if j > 1:
                            dve.wait_ge(s_rd, RD * r + 3 * half + j)
                        lo, hi = (j, HALF) if half == 0 else (HALF, S)
                        stt(xc[:, lo:hi], zst[0][:, lo - j:hi - j], rcol[:, 3 - j:4 - j], xc[:, lo:hi], ALU.mult,
                            ALU.add).then_inc(s_rd, 1)
                if last:
                    rows(0, 0, 0)
                dve.wait_ge(s_ra, RA * r + 3)
                stt(tg[:, :], tg[:, :], 1.0, zst[1][:, :], ALU.add, ALU.mult).then_inc(s_rd, 1)
                for half, cs in enumerate(halves):
                    dve.wait_ge(s_ra, RA * r + 4 + 2 * half)
                    v.tensor_scalar(tr[:, cs], tr[:, cs], 1.0, rcol[:, 7:8], ALU.add, ALU.mult).then_inc(s_rd, 1)
                    dve.wait_ge(s_ra, RA * r + 5 + 2 * half)
                    stt(xc[:, cs], ti[:, cs], 1.0, xc[:, cs], ALU.add, ALU.mult).then_inc(s_rd, 1)
                if last:
                    rows(0, 1, 1)
                for half, cs in enumerate(halves):
                    dve.wait_ge(s_ra, RA * r + 8 + half)
                    v.tensor_scalar(tt[:, cs], tt[:, cs], 1e-18, None, ALU.max).then_inc(s_rd, 1)
                for half, cs in enumerate(halves):
                    dve.wait_ge(s_ra, RA * r + 13 + 2 * half)
                    v.tensor_tensor(l1[:, cs], l1[:, cs], l2[:, cs], ALU.subtract).then_inc(s_rd, 1)
                if last:
                    rows(0, 2, 0)
                for half, cs in enumerate(halves):
                    dve.wait_ge(s_ra, RA * r + 16 + half)
                    stt(xc[:, cs], xc[:, cs], 0.5, l1[:, cs], ALU.mult, ALU.mult).then_inc(s_rd, 1)
                    dve.wait_ge(s_rd, RD * r + 17 + 2 * half)
                    before = ti[:, HALF - 1:HALF] if half else 0.0
                    v.tensor_tensor_scan(ti[:, cs], tr[:, cs], xc[:, cs], before, ALU.mult, ALU.add).then_inc(s_rd, 1)
                    dve.wait_ge(s_rd, RD * r + 18 + 2 * half)
                    y = stt(yt[:, bass.ds(8 + r, 1), cs].rearrange("p o s -> p (o s)"), ti[:, cs], 0.5, tg[:, cs],
                            ALU.mult, ALU.mult)
                y.then_inc(s_unit, 1)

            dve.wait_ge(s_gm, 5)
            v.memset(qb[0][64:66, :].bitcast(F32), 1.0).then_inc(s_on, 1)
            v.memset(qb[1][0:2, :].bitcast(F32), 1.0).then_inc(s_on, 1)
            with dve.Fori(0, TURNS - 1) as a:
                fox(a)
            fox(TURNS - 1)
            dve.wait_ge(s_unit, BEFORE_ML + 1)
            v.memset(wad[:, :, :], 0.0).then_inc(s_rz, 1)
            v.memset(vh2[:, :, P:P + 1].bitcast(F32), 1.0).then_inc(s_mone, 1)
            v.memset(vh2[:, :, P + 1:CV].bitcast(F32), 0.0).then_inc(s_mone, 1)
            v.memset(vl2[:, :, P:CV].bitcast(F32), 0.0).then_inc(s_mone, 1)
            with dve.Fori(0, TURNS - 1) as a:
                mlstm(a)
            mlstm(TURNS - 1, final_unit=True)
            with dve.Fori(0, TURNS - 1) as a:
                rglru(a)
            rglru(TURNS - 1, last=True)

            def save_h(i):
                dve.wait_ge(s_hx, 16 * SB)
                if i % 4 < 3:
                    dve.wait_ge(s_ob, 3 * (i // 4) + i % 4 + 1)
                else:
                    dve.wait_ge(s_om, 12 * (i // 4 + 1))
                v.tensor_tensor(ht[:, i, :], ht[:, i, :], ps[i % 4][:, :], ALU.add).then_inc(s_h, 1)

            rows(0, 3, 1)
            with dve.Fori(2, 5) as n:
                rows(0, 2 * n, 0)
                rows(0, 2 * n + 1, 1)
            rows(0, 10, 0)
            rows(0, 11, 1)
            rows(1, 0, 0)
            for i in range(4):
                save_h(i)
            rows(1, 1, 1)
            ple_column(2, 0)
            ple_column(3, 1)
            with dve.Fori(1, 4) as n:
                for b in range(2):
                    rows(1, 2 * n + b, b, "gate")
                    ple_column(2 * n + (b + 2), b)
            rows(1, 8, 0, "gate")
            rows(1, 9, 1, "gate")
            rows(1, 10, 0, "ple")
            rows(1, 11, 1, "ple")
            v.memset(hr[:, 2:3], 4.0 * EPS).then_inc(s_hr, 1)
            for i in range(4, 8):
                save_h(i)

            def lows(i, b):
                dve.wait_ge(s_qh, i + 1)
                if not (isinstance(i, int) and i < 2):
                    dve.wait_ge(s_gp, 2 * (i - 1))
                v.tensor_tensor(htl[b][:, :, :].rearrange("p k s -> p (k s)"), ps[0][:, :],
                                hth[b][:, :, :].rearrange("p k s -> p (k s)"), ALU.subtract)
                v.tensor_tensor(ptl[b][:, :, :].rearrange("p k s -> p (k s)"), ps[1][:, 0:KP * P],
                                pth[b][:, :, :].rearrange("p k s -> p (k s)"), ALU.subtract).then_inc(s_ql, 1)

            def final(i, b):
                h = ht[:, bass.ds(i, 1), :].rearrange("p o d -> p (o d)")
                dve.wait_ge(s_th, i + 1)
                dve.wait_ge(s_gp, 2 * i + 2)
                v.scalar_tensor_tensor(th[b][:, :], th[b][:, :], 1.0, ps[3][:, :], ALU.add, ALU.mult).then_inc(s_t1, 1)
                dve.wait_ge(s_t1, i + 1)
                v.scalar_tensor_tensor(h, th[b][:, :], 0.5, h, ALU.mult, ALU.add).then_inc(s_fin, 1)

            lows(0, 0)
            lows(1, 1)
            final(0, 0)
            with dve.Fori(1, 4) as n:
                for b in range(2):
                    lows(2 * n + b, b)
                    final(2 * n + (b - 1), 1 - b)
            final(7, 1)


def bc(ap, n):
    return ap.unsqueeze(2).broadcast_to([ap.shape[0], ap.shape[1], n])


_INS = ["x", "p", "norm_g", "w_in", "rg_conv_w", "rg_conv_b", "rg_wa", "rg_ba", "rg_wx", "rg_bx", "rg_lambda",
        "fox_b_f", "fox_q_g", "fox_k_g", "ml_b_i", "ml_b_f", "w_out", "ple_norm_g", "w_ple_gate", "w_ple"]


def kernel(**inputs):
    import numpy as _np
    import concourse.bacc as _bacc
    from concourse.bass_utils import run_bass_kernel_spmd as _run

    nc = _bacc.Bacc("TRN2", target_bir_lowering=False, num_devices=1)
    arrays, args = {}, []
    for name in _INS:
        a = _np.ascontiguousarray(inputs[name])
        arrays[f"in_{name}"] = a
        args.append(nc.dram_tensor(f"in_{name}", a.shape, mybir.dt.from_np(a.dtype), kind="ExternalInput").ap())
    args.append(nc.dram_tensor("out_0", (1, S, D), F32, kind="ExternalOutput").ap())
    hybrid(nc, *args)
    r = _run(nc, [arrays], core_ids=[0])
    return r.results[0]["out_0"]
```
